# Optimizing a Trainium2 kernel written in Bass

```python
import math
import numpy as np
import jax
import jax.numpy as jnp
from jax import lax
import jax, jax.numpy as jnp

D_MODEL = 1024
BATCH = 1
SEQ = 256
DEPTH = 1

HEAD_DIM = 64
Q_BLOCK = 128
EPS = 1e-6
NEG = -1e30
FORCE_SCORE = 1e4

SB_HEADS = 8
SB_W = SB_HEADS * HEAD_DIM
NSA_HEADS = 8
NSA_GROUPS = 2
NSA_HPG = NSA_HEADS // NSA_GROUPS
NSA_W = NSA_HEADS * HEAD_DIM
NSA_KV_W = NSA_GROUPS * HEAD_DIM
CMP_LEN = 32
CMP_STRIDE = 16
SEL_BLOCK = 64
SEL_TOPN = 4
WINDOW = 256
HGRN_HEADS = 4
HGRN_DK = 128
HGRN_DV = 128
HGRN_K_W = HGRN_HEADS * HGRN_DK
HGRN_V_W = HGRN_HEADS * HGRN_DV
HGRN_CHUNK = 64
N_BRANCH = 3
IN_SPLITS = (SB_W, SB_W, SB_W, NSA_W, 6 * NSA_KV_W, 3 * NSA_HEADS, HGRN_K_W, HGRN_K_W, HGRN_V_W, HGRN_V_W, N_BRANCH * D_MODEL)
IN_WIDTH = sum(IN_SPLITS)
PEER_HEADS = 8
PEER_NKEYS = 128
PEER_EXPERTS = PEER_NKEYS * PEER_NKEYS
PEER_TOPK = 16
PEER_QDIM = 128
PEER_TOK_CHUNK = 128


def rms_norm(x, g):
    xf = x.astype(jnp.float32)
    y = xf * lax.rsqrt(jnp.mean(xf * xf, axis=-1, keepdims=True) + EPS)
    return (y * g.astype(jnp.float32)).astype(x.dtype)

def alibi_slopes(n_heads):
    return jnp.exp2(-8.0 * (jnp.arange(n_heads, dtype=jnp.float32) + 1.0) / n_heads)

def stick_breaking_attention(q, k, v):
    B, H, T, dh = q.shape
    scale = dh ** -0.5
    outs = []
    for i in range(T // Q_BLOCK):
        q0 = i * Q_BLOCK
        kl = q0 + Q_BLOCK
        z = jnp.einsum("bhtd,bhsd->bhts", q[:, :, q0:kl], k[:, :, :kl]).astype(jnp.float32) * scale
        before = jnp.arange(kl)[None, :] < (q0 + jnp.arange(Q_BLOCK))[:, None]
        log_1m = jnp.where(before, jax.nn.log_sigmoid(-z), 0.0)
        after = lax.cumsum(log_1m, axis=3, reverse=True) - log_1m
        a = jnp.where(before, jnp.exp(jax.nn.log_sigmoid(z) + after), 0.0)
        outs.append(jnp.einsum("bhts,bhsd->bhtd", a.astype(v.dtype), v[:, :, :kl]))
    return jnp.concatenate(outs, axis=2)

def nsa_attention(q, k_cmp, v_cmp, k_sel, v_sel, k_win, v_win, gates, w_cmp_k, w_cmp_v, cmp_pe):
    B, G, P, T, dh = q.shape
    f32 = jnp.float32
    scale = dh ** -0.5
    slopes = alibi_slopes(G * P).reshape(G, P)
    t_pos = jnp.arange(T)

    n_piece = T // CMP_STRIDE
    per = CMP_LEN // CMP_STRIDE
    n_cmp = n_piece - per + 1

    def compress(x, w):
        pieces = x.reshape(B, G, n_piece, CMP_STRIDE, dh)
        blocks = jnp.concatenate([pieces[:, :, j:j + n_cmp] for j in range(per)], axis=3) + cmp_pe
        return blocks.reshape(B, G, n_cmp, CMP_LEN * dh) @ w

    kc = compress(k_cmp, w_cmp_k)
    vc = compress(v_cmp, w_cmp_v)
    c_start = jnp.arange(n_cmp) * CMP_STRIDE
    dist_c = t_pos[:, None] - (c_start + CMP_LEN - 1)[None, :]
    valid_c = dist_c >= 0
    s_c = jnp.einsum("bgptd,bgcd->bgptc", q, kc).astype(f32) * scale - slopes[:, :, None, None] * dist_c.astype(f32)
    p_c = jnp.where(valid_c, jax.nn.softmax(jnp.where(valid_c, s_c, NEG), axis=-1), 0.0)
    o_c = jnp.einsum("bgptc,bgcd->bgptd", p_c.astype(vc.dtype), vc)

    n_blk = T // SEL_BLOCK
    n_sel = min(SEL_TOPN, n_blk)
    b_start = jnp.arange(n_blk) * SEL_BLOCK
    overlap = ((c_start[:, None] < b_start[None, :] + SEL_BLOCK) & (c_start[:, None] + CMP_LEN > b_start[None, :])).astype(f32)
    imp = jnp.einsum("bgptc,cn->bgtn", p_c, overlap)
    bid = jnp.arange(n_blk)
    forced = (bid[None, :] == (t_pos // SEL_BLOCK)[:, None]) | (bid[None, :] == 0)
    causal_b = b_start[None, :] <= t_pos[:, None]
    imp = jnp.where(forced, FORCE_SCORE, jnp.where(causal_b, imp, NEG))
    _, sel_idx = lax.top_k(imp, n_sel)

    kblk = k_sel.reshape(B, G, n_blk, SEL_BLOCK, dh)
    vblk = v_sel.reshape(B, G, n_blk, SEL_BLOCK, dh)
    nq = T // Q_BLOCK
    q_chunks = jnp.moveaxis(q.reshape(B, G, P, nq, Q_BLOCK, dh), 3, 0)
    idx_chunks = jnp.moveaxis(sel_idx.reshape(B, G, nq, Q_BLOCK, n_sel), 2, 0)
    bi = jnp.arange(B)[:, None, None, None]
    gi = jnp.arange(G)[None, :, None, None]
    n_keys_sel = n_sel * SEL_BLOCK

    def sel_chunk(args):
        qc, ic, c = args
        kg = kblk[bi, gi, ic].reshape(B, G, Q_BLOCK, n_keys_sel, dh)
        vg = vblk[bi, gi, ic].reshape(B, G, Q_BLOCK, n_keys_sel, dh)
        pos = (ic[..., None] * SEL_BLOCK + jnp.arange(SEL_BLOCK)).reshape(B, G, Q_BLOCK, n_keys_sel)
        dist = (c * Q_BLOCK + jnp.arange(Q_BLOCK))[:, None] - pos
        sc = jnp.einsum("bgpqd,bgqsd->bgpqs", qc, kg).astype(f32) * scale - slopes[None, :, :, None, None] * dist[:, :, None].astype(f32)
        pr = jax.nn.softmax(jnp.where(dist[:, :, None] >= 0, sc, NEG), axis=-1)
        return jnp.einsum("bgpqs,bgqsd->bgpqd", pr.astype(vg.dtype), vg)

    o_s = lax.map(sel_chunk, (q_chunks, idx_chunks, jnp.arange(nq)))
    o_s = jnp.moveaxis(o_s, 0, 3).reshape(B, G, P, T, dh)

    nb = T // Q_BLOCK
    nwb = WINDOW // Q_BLOCK
    span = (nwb + 1) * Q_BLOCK

    def band(x):
        xb = jnp.pad(x.reshape(B, G, nb, Q_BLOCK, dh), ((0, 0), (0, 0), (nwb, 0), (0, 0), (0, 0)))
        return jnp.concatenate([xb[:, :, j:j + nb] for j in range(nwb + 1)], axis=3)

    kwb = band(k_win)
    vwb = band(v_win)
    tq = t_pos.reshape(nb, Q_BLOCK)
    sk = jnp.arange(nb)[:, None] * Q_BLOCK - nwb * Q_BLOCK + jnp.arange(span)[None, :]
    dist_w = tq[:, :, None] - sk[:, None, :]
    valid_w = (dist_w >= 0) & (dist_w < WINDOW) & (sk[:, None, :] >= 0)
    s_w = jnp.einsum("bgpnqd,bgnsd->bgpnqs", q.reshape(B, G, P, nb, Q_BLOCK, dh), kwb).astype(f32) * scale - slopes[:, :, None, None, None] * dist_w.astype(f32)
    p_w = jax.nn.softmax(jnp.where(valid_w, s_w, NEG), axis=-1)
    o_w = jnp.einsum("bgpnqs,bgnsd->bgpnqd", p_w.astype(vwb.dtype), vwb).reshape(B, G, P, T, dh)

    g = jax.nn.sigmoid(gates.astype(f32)).reshape(B, T, G, P, 3).transpose(4, 0, 2, 3, 1)
    o = g[0][..., None] * o_c + g[1][..., None] * o_s + g[2][..., None] * o_w
    return o.astype(q.dtype)

def hgrn2_recurrence(q, log_f, k, i):
    B, H, T, dk = q.shape
    dv = i.shape[-1]
    C = HGRN_CHUNK
    nc = T // C

    def to_chunks(x):
        return jnp.moveaxis(x.reshape(B, H, nc, C, x.shape[-1]), 2, 0)

    causal = jnp.tril(jnp.ones((C, C), dtype=bool))

    def step(S, inp):
        qc, gc, kc, ic = inp
        b = jnp.cumsum(gc, axis=2)
        o_inter = jnp.einsum("bhtk,bhkv->bhtv", qc * jnp.exp(b), S)
        rel = b[:, :, :, None, :] - b[:, :, None, :, :]
        decay = jnp.exp(jnp.where(causal[:, :, None], rel, -jnp.inf))
        att = jnp.einsum("bhtk,bhsk,bhtsk->bhts", qc, kc, decay)
        o = o_inter + jnp.einsum("bhts,bhsv->bhtv", att, ic)
        b_last = b[:, :, -1:, :]
        S_new = jnp.exp(b_last[:, :, 0, :, None]) * S + jnp.einsum("bhsk,bhsv->bhkv", kc * jnp.exp(b_last - b), ic)
        return S_new, o

    S0 = jnp.zeros((B, H, dk, dv), dtype=jnp.float32)
    _, o = lax.scan(step, S0, (to_chunks(q), to_chunks(log_f), to_chunks(k), to_chunks(i)))
    return jnp.moveaxis(o, 0, 2).reshape(B, H, T, dv)

def hybrid_mixer(h, w_in, w_cmp_k, w_cmp_v, cmp_pe, hgrn_norm, lower, w_sb, w_nsa, w_hg, w_out):
    B, T, _ = h.shape
    f32 = jnp.float32
    proj = h @ w_in
    offsets = np.cumsum(IN_SPLITS)[:-1].tolist()
    sb_q, sb_k, sb_v, nsa_q, nsa_kv, nsa_g, hg_q, hg_f, hg_i, hg_g, merge_g = jnp.split(proj, offsets, axis=-1)

    def heads(t, n):
        return t.reshape(B, T, n, -1).transpose(0, 2, 1, 3)

    o_sb = stick_breaking_attention(heads(sb_q, SB_HEADS), heads(sb_k, SB_HEADS), heads(sb_v, SB_HEADS))
    o_sb = o_sb.transpose(0, 2, 1, 3).reshape(B, T, SB_W)

    qn = heads(nsa_q, NSA_HEADS).reshape(B, NSA_GROUPS, NSA_HPG, T, HEAD_DIM)
    kv = nsa_kv.reshape(B, T, 6, NSA_GROUPS, HEAD_DIM).transpose(2, 0, 3, 1, 4)
    o_nsa = nsa_attention(qn, kv[0], kv[1], kv[2], kv[3], kv[4], kv[5], nsa_g.reshape(B, T, NSA_HEADS, 3), w_cmp_k, w_cmp_v, cmp_pe)
    o_nsa = o_nsa.reshape(B, NSA_HEADS, T, HEAD_DIM).transpose(0, 2, 1, 3).reshape(B, T, NSA_W)

    lb = lower.reshape(HGRN_HEADS, 1, HGRN_DK)
    f = lb + (1.0 - lb) * jax.nn.sigmoid(heads(hg_f, HGRN_HEADS).astype(f32))
    qh = jax.nn.silu(heads(hg_q, HGRN_HEADS).astype(f32))
    o_hg = hgrn2_recurrence(qh, jnp.log(f), 1.0 - f, heads(hg_i, HGRN_HEADS).astype(f32))
    o_hg = rms_norm(o_hg.transpose(0, 2, 1, 3), hgrn_norm.reshape(HGRN_HEADS, HGRN_DV))
    o_hg = (o_hg * jax.nn.silu(hg_g.astype(f32).reshape(B, T, HGRN_HEADS, HGRN_DV))).reshape(B, T, HGRN_V_W).astype(h.dtype)

    gm = jax.nn.sigmoid(merge_g.astype(f32)).reshape(B, T, N_BRANCH, D_MODEL)
    m = gm[:, :, 0] * (o_sb @ w_sb) + gm[:, :, 1] * (o_nsa @ w_nsa) + gm[:, :, 2] * (o_hg @ w_hg)
    return m.astype(h.dtype) @ w_out

def peer_ffn(x, w_q, sub_keys, u_tab, v_tab):
    B, T, D = x.shape
    f32 = jnp.float32
    Ct = PEER_TOK_CHUNK
    H, K = PEER_HEADS, PEER_TOPK
    xt = x.reshape((B * T) // Ct, Ct, D)

    def chunk(xc):
        qh = (xc @ w_q).reshape(Ct, H, 2, PEER_QDIM // 2)
        s = jnp.einsum("nhad,akd->nhak", qh, sub_keys).astype(f32)
        top_s, top_i = lax.top_k(s, K)
        cand = (top_s[:, :, 0, :, None] + top_s[:, :, 1, None, :]).reshape(Ct, H, K * K)
        cand_idx = (top_i[:, :, 0, :, None] * PEER_NKEYS + top_i[:, :, 1, None, :]).reshape(Ct, H, K * K)
        best_s, pos = lax.top_k(cand, K)
        eidx = jnp.take_along_axis(cand_idx, pos, axis=-1)
        gate = jax.nn.softmax(best_s, axis=-1)
        ug = u_tab[eidx]
        vg = v_tab[eidx]
        hpre = jnp.einsum("nd,nhkd->nhk", xc, ug).astype(f32)
        act = (gate * jax.nn.gelu(hpre, approximate=False)).astype(x.dtype)
        return jnp.einsum("nhk,nhkd->nd", act, vg)

    return lax.map(chunk, xt).reshape(B, T, D)

def first_inputs(seed: int = 0) -> dict:
    key = jax.random.key(seed)
    ks = jax.random.split(key, 20)
    f32 = jnp.float32
    nrm = lambda k, shape, s: jax.random.normal(k, shape, dtype=f32) * s
    L, D = DEPTH, D_MODEL
    return {
        "x": nrm(ks[0], (BATCH, SEQ, D), 1.0),
        "norm_mix": 1.0 + nrm(ks[1], (L, D), 0.02),
        "norm_ffn": 1.0 + nrm(ks[2], (L, D), 0.02),
        "w_in": nrm(ks[3], (L, D, IN_WIDTH), D ** -0.5),
        "nsa_w_cmp_k": nrm(ks[4], (L, CMP_LEN * HEAD_DIM, HEAD_DIM), (CMP_LEN * HEAD_DIM) ** -0.5),
        "nsa_w_cmp_v": nrm(ks[5], (L, CMP_LEN * HEAD_DIM, HEAD_DIM), (CMP_LEN * HEAD_DIM) ** -0.5),
        "nsa_cmp_pe": nrm(ks[6], (L, CMP_LEN, HEAD_DIM), 0.1),
        "hgrn_norm": 1.0 + nrm(ks[7], (L, HGRN_V_W), 0.02),
        "hgrn_lower_bounds": nrm(ks[8], (L, HGRN_K_W), 0.1),
        "w_branch_sb": nrm(ks[9], (L, SB_W, D), SB_W ** -0.5),
        "w_branch_nsa": nrm(ks[10], (L, NSA_W, D), NSA_W ** -0.5),
        "w_branch_hgrn": nrm(ks[11], (L, HGRN_V_W, D), HGRN_V_W ** -0.5),
        "w_out": nrm(ks[12], (L, D, D), 0.5 * D ** -0.5),
        "peer_w_q": nrm(ks[13], (L, D, PEER_HEADS * PEER_QDIM), D ** -0.5),
        "peer_sub_keys": nrm(ks[14], (L, 2, PEER_NKEYS, PEER_QDIM // 2), (PEER_QDIM // 2) ** -0.5),
        "peer_u": nrm(ks[15], (L, PEER_EXPERTS, D), D ** -0.5),
        "peer_v": nrm(ks[16], (L, PEER_EXPERTS, D), (PEER_HEADS * PEER_TOPK) ** -0.5),
        "norm_final": 1.0 + nrm(ks[17], (D,), 0.02),
    }

def first_block(x, norm_mix, norm_ffn, w_in, nsa_w_cmp_k, nsa_w_cmp_v, nsa_cmp_pe, hgrn_norm, hgrn_lower_bounds, w_branch_sb, w_branch_nsa, w_branch_hgrn, w_out, peer_w_q, peer_sub_keys, peer_u, peer_v, norm_final):
    lb_soft = jax.nn.softmax(hgrn_lower_bounds.astype(jnp.float32), axis=0)
    lower = jnp.cumsum(lb_soft, axis=0) - lb_soft[0]
    for l in range(DEPTH):
        h = rms_norm(x, norm_mix[l])
        x = x + hybrid_mixer(h, w_in[l], nsa_w_cmp_k[l], nsa_w_cmp_v[l], nsa_cmp_pe[l], hgrn_norm[l], lower[l], w_branch_sb[l], w_branch_nsa[l], w_branch_hgrn[l], w_out[l])
        h = rms_norm(x, norm_ffn[l])
        x = x + peer_ffn(h, peer_w_q[l], peer_sub_keys[l], peer_u[l], peer_v[l])
    return rms_norm(x, norm_final)


DEPTH_2 = 2

N_A_LAYERS = DEPTH_2 // 2
N_B_LAYERS = DEPTH_2 - N_A_LAYERS
D_FF = 256 * ((8 * D_MODEL // 3 + 255) // 256)
CONV_WIDTH = 3
N_HEADS = D_MODEL // (2 * HEAD_DIM)
LAMBDA_STD = 0.1


def rms_norm_2(x, g):
    xf = x.astype(jnp.float32)
    y = xf * lax.rsqrt(jnp.mean(xf * xf, axis=-1, keepdims=True) + EPS)
    return (y * g.astype(jnp.float32)).astype(x.dtype)

def swiglu(h, w_gate, w_up, w_down):
    return (jax.nn.silu(h @ w_gate) * (h @ w_up)) @ w_down

def short_conv_mixer(h, w_in, w_conv, w_out):
    gate_b, gate_c, u = jnp.split(h @ w_in, 3, axis=-1)
    z = lax.conv_general_dilated(
        gate_c * u, w_conv[:, None, :], window_strides=(1,),
        padding=[(CONV_WIDTH - 1, 0)], dimension_numbers=("NWC", "WIO", "NWC"),
        feature_group_count=D_MODEL)
    return (gate_b * z) @ w_out

def shared_kv(x, g_kv, w_kv):
    b, s, _ = x.shape
    k, v = jnp.split(rms_norm_2(x, g_kv) @ w_kv, 2, axis=-1)
    k = k.reshape(b, s, N_HEADS, 2, HEAD_DIM)
    v = v.reshape(b, s, N_HEADS, 2 * HEAD_DIM)
    return k, v

def diff_attention(h, k, v, w_q, lq1, lk1, lq2, lk2, g_subln, w_o, lambda_init):
    b, s, _ = h.shape
    q = (h @ w_q).reshape(b, s, N_HEADS, 2, HEAD_DIM) * (HEAD_DIM ** -0.5)
    f32 = jnp.float32
    lam = (jnp.exp(jnp.sum(lq1.astype(f32) * lk1.astype(f32)))
           - jnp.exp(jnp.sum(lq2.astype(f32) * lk2.astype(f32))) + lambda_init)
    n_blocks = s // Q_BLOCK
    q_blocks = jnp.moveaxis(q.reshape(b, n_blocks, Q_BLOCK, N_HEADS, 2, HEAD_DIM), 1, 0)
    key_pos = jnp.arange(s)

    def block(args):
        qb, i = args
        scores = jnp.einsum("bqhcd,bkhcd->bhcqk", qb, k).astype(f32)
        q_pos = i * Q_BLOCK + jnp.arange(Q_BLOCK)
        causal = key_pos[None, :] <= q_pos[:, None]
        p = jax.nn.softmax(jnp.where(causal, scores, -jnp.inf), axis=-1)
        a = p[:, :, 0] - lam * p[:, :, 1]
        return jnp.einsum("bhqk,bkhe->bqhe", a.astype(v.dtype), v)

    o = lax.map(block, (q_blocks, jnp.arange(n_blocks)))
    o = jnp.moveaxis(o, 0, 1).reshape(b, s, N_HEADS, 2 * HEAD_DIM)
    o = rms_norm_2(o, g_subln) * (1.0 - lambda_init)
    return o.reshape(b, s, D_MODEL) @ w_o

def second_inputs(seed: int = 0) -> dict:
    key = jax.random.key(seed)
    ks = jax.random.split(key, 20)
    f32 = jnp.float32
    nrm = lambda k, shape, fan_in: jax.random.normal(k, shape, f32) * (fan_in ** -0.5)
    return {
        "x": jax.random.normal(ks[0], (BATCH, SEQ, D_MODEL), f32),
        "g_norm": 1.0 + 0.02 * jax.random.normal(ks[1], (DEPTH_2, 6, D_MODEL), f32),
        "w_ffn_gate": nrm(ks[2], (DEPTH_2, 2, D_MODEL, D_FF), D_MODEL),
        "w_ffn_up": nrm(ks[3], (DEPTH_2, 2, D_MODEL, D_FF), D_MODEL),
        "w_ffn_down": nrm(ks[4], (DEPTH_2, 2, D_FF, D_MODEL), D_FF),
        "w_conv_in": nrm(ks[5], (N_A_LAYERS, D_MODEL, 3 * D_MODEL), D_MODEL),
        "w_conv": nrm(ks[6], (N_A_LAYERS, CONV_WIDTH, D_MODEL), CONV_WIDTH),
        "w_conv_out": nrm(ks[7], (N_A_LAYERS, D_MODEL, D_MODEL), D_MODEL),
        "g_kv": 1.0 + 0.02 * jax.random.normal(ks[8], (D_MODEL,), f32),
        "w_kv": nrm(ks[9], (D_MODEL, 2 * D_MODEL), D_MODEL),
        "w_q": nrm(ks[10], (N_B_LAYERS, D_MODEL, D_MODEL), D_MODEL),
        "lambda_q1": LAMBDA_STD * jax.random.normal(ks[11], (N_B_LAYERS, HEAD_DIM), f32),
        "lambda_k1": LAMBDA_STD * jax.random.normal(ks[12], (N_B_LAYERS, HEAD_DIM), f32),
        "lambda_q2": LAMBDA_STD * jax.random.normal(ks[13], (N_B_LAYERS, HEAD_DIM), f32),
        "lambda_k2": LAMBDA_STD * jax.random.normal(ks[14], (N_B_LAYERS, HEAD_DIM), f32),
        "g_subln": 1.0 + 0.02 * jax.random.normal(ks[15], (N_B_LAYERS, 2 * HEAD_DIM), f32),
        "w_o": nrm(ks[16], (N_B_LAYERS, D_MODEL, D_MODEL), D_MODEL),
    }

def second_block(x, g_norm, w_ffn_gate, w_ffn_up, w_ffn_down, w_conv_in, w_conv, w_conv_out,
              g_kv, w_kv, w_q, lambda_q1, lambda_k1, lambda_q2, lambda_k2, g_subln, w_o):
    k = v = None
    for layer in range(DEPTH_2):
        g = g_norm[layer]
        f = swiglu(rms_norm_2(x, g[0]), w_ffn_gate[layer, 0], w_ffn_up[layer, 0], w_ffn_down[layer, 0])
        x = x + 0.5 * rms_norm_2(f, g[1])
        h = rms_norm_2(x, g[2])
        if layer < N_A_LAYERS:
            m = short_conv_mixer(h, w_conv_in[layer], w_conv[layer], w_conv_out[layer])
        else:
            j = layer - N_A_LAYERS
            lambda_init = 0.8 - 0.6 * math.exp(-0.3 * layer)
            m = diff_attention(h, k, v, w_q[j], lambda_q1[j], lambda_k1[j], lambda_q2[j],
                               lambda_k2[j], g_subln[j], w_o[j], lambda_init)
        x = x + rms_norm_2(m, g[3])
        f = swiglu(rms_norm_2(x, g[4]), w_ffn_gate[layer, 1], w_ffn_up[layer, 1], w_ffn_down[layer, 1])
        x = x + 0.5 * rms_norm_2(f, g[5])
        if layer == N_A_LAYERS - 1:
            k, v = shared_kv(x, g_kv, w_kv)
    return x


def setup_inputs(seed=0):
    out = dict(first_inputs(seed))
    for name, value in second_inputs(seed + 1).items():
        if name != "x":
            out[name + "_2"] = value
    return out


def reference(
    x, norm_mix, norm_ffn, w_in, nsa_w_cmp_k, nsa_w_cmp_v, nsa_cmp_pe, hgrn_norm,
    hgrn_lower_bounds, w_branch_sb, w_branch_nsa, w_branch_hgrn, w_out, peer_w_q, peer_sub_keys,
    peer_u, peer_v, norm_final, g_norm_2, w_ffn_gate_2, w_ffn_up_2, w_ffn_down_2, w_conv_in_2,
    w_conv_2, w_conv_out_2, g_kv_2, w_kv_2, w_q_2, lambda_q1_2, lambda_k1_2, lambda_q2_2,
    lambda_k2_2, g_subln_2, w_o_2,
):
    x = first_block(
        x, norm_mix, norm_ffn, w_in, nsa_w_cmp_k, nsa_w_cmp_v, nsa_cmp_pe, hgrn_norm,
        hgrn_lower_bounds, w_branch_sb, w_branch_nsa, w_branch_hgrn, w_out, peer_w_q,
        peer_sub_keys, peer_u, peer_v, norm_final,
    )
    return second_block(
        x, g_norm_2, w_ffn_gate_2, w_ffn_up_2, w_ffn_down_2, w_conv_in_2, w_conv_2,
        w_conv_out_2, g_kv_2, w_kv_2, w_q_2, lambda_q1_2, lambda_k1_2, lambda_q2_2, lambda_k2_2,
        g_subln_2, w_o_2,
    )


_drawn_inputs = setup_inputs


def setup_inputs(seed=0):
    import zlib

    import numpy as np

    out = dict(_drawn_inputs(seed))
    spreads = {}
    factors = {'norm_mix': 3.025,
     'norm_ffn': 15.169,
     'hgrn_norm': 6.316,
     'g_kv_2': 3.285,
     'g_subln_2': 50.901,
     'nsa_cmp_pe': 5.588}
    for name, (base, spread) in spreads.items():
        noise = np.random.default_rng([zlib.crc32(name.encode()), seed]).standard_normal(out[name].shape)
        drawn = base * np.exp(spread * noise) if base else spread * noise
        out[name] = jnp.asarray(drawn.astype(out[name].dtype))
    for name, factor in factors.items():
        out[name] = (out[name] * factor).astype(out[name].dtype)
    return out
```

```python
from contextlib import ExitStack

import concourse.bass as bass
import concourse.mybir as mybir
import numpy as np

F32, F32R = mybir.dt.float32, mybir.dt.float32r
U32 = mybir.dt.uint32
ALU = mybir.AluOpType
ACT = mybir.ActivationFunctionType
AX = mybir.AxisListType

P = 128
T, D = 256, 1024
TT = T // P
KD = D // P
HD = 64
EPS = 1e-6
NEG = -1e30
FAR = 1e32
SB_W = NSA_W = HG_W = 512
PAIRS = SB_W // P
CMP_LEN, CMP_STRIDE = 32, 16
N_CMP = T // CMP_STRIDE - 1
CPAD = N_CMP + 1
HG_HEADS = 4
LEVELS = 8
F_FF = 2816
FF_STEPS = F_FF // 256
CONV_W = 3
PANEL = 2048
PC = 256
SLOTS = 3
PE_HEADS, PE_K, PE_KEYS = 8, 16, 128
RING, GROUP = 8, 4
LAMBDA_INIT = 0.8 - 0.6 * float(np.exp(-0.3))
DIFF_HEADS = 8

C_SBQ, C_SBK, C_SBV, C_NQ, C_CMP, C_SEL, C_WIN, C_NG = 0, 512, 1024, 1536, 2048, 2304, 2560, 2816
C_HQ, C_HF, C_HI, C_HG, C_MERGE = 2840, 3352, 3864, 4376, 4888
N_GATES = 24


def plan_panels():
    plan = []

    def add(name, count, pieces=1, words=PANEL, banks=(0, 1)):
        for j in range(count):
            b = banks[j % len(banks)] if banks else None
            plan.append((name, pieces, words, b))

    add("sb", 6)
    add("nsa_q", 2, pieces=4)
    add("nsa_kv", 3)
    add("nsa_gate", 1, words=KD * N_GATES, banks=(1,))
    add("hg", 8)
    for _ in range(3):
        for _ in range(2):
            add("merge", 2)
            add("branch", 1, pieces=2, banks=())
    add("w_out", 4)
    add("peer_q", 4)

    def ffn(name):
        for i in range(FF_STEPS):
            add(name, 2)
            if i:
                add(name, 1, banks=())
        add(name, 1, banks=())

    ffn("ffn0")
    add("conv_in", 12, banks=(0, 1, 2))
    add("conv_out", 4, banks=())
    ffn("ffn1")
    add("kv", 8)
    ffn("ffn2")
    add("q", 4)
    add("o", 4, banks=())
    ffn("ffn3")
    return plan


PLAN = plan_panels()
NP = len(PLAN)
FIRST = {}
for _p, _e in enumerate(PLAN):
    FIRST.setdefault(_e[0], _p)
BANK = [e[3] for e in PLAN]
WORDS = [e[2] for e in PLAN]
LANDED = [16 * sum(PLAN[q][1] for q in range(p % SLOTS, p + 1, SLOTS)) for p in range(NP)]
EVAC = [sum(b is not None for b in BANK[:p]) for p in range(NP + 1)]

XPOSE = [("mix", 4), ("hg", 2), ("peer", 4), ("f0", 4), ("conv", 4), ("f1", 4), ("kv", 4), ("f2", 4),
         ("attn", 4), ("diff", 4), ("f3", 4)]
XBASE = {n: sum(b for _, b in XPOSE[:k]) for k, (n, _) in enumerate(XPOSE)}
XEND = {n: XBASE[n] + b for n, b in XPOSE}
GAIN = {n: 8 * k for k, n in enumerate(["mix", "peer", "f0", "conv", "f1", "f2", "attn", "f3", "kv"])}
TAPS = 72
NORMS = [("mix", 2, 1 / D, 1.0), ("hg", 8, 1 / 128, 1.0), ("peer", 2, 1 / D, 1.0), ("final", 2, 1 / D, 1.0),
         ("f0", 2, 1 / D, 1.0), ("p0", 2, 1 / D, 0.5), ("conv", 2, 1 / D, 1.0), ("pc", 2, 1 / D, 1.0),
         ("f1", 2, 1 / D, 1.0), ("p1", 2, 1 / D, 0.5), ("kv", 2, 1 / D, 1.0),
         ("f2", 2, 1 / D, 1.0), ("p2", 2, 1 / D, 0.5), ("attn", 2, 1 / D, 1.0), ("diff", 16, 1 / 128, 1.0 - LAMBDA_INIT),
         ("pa", 2, 1 / D, 1.0), ("f3", 2, 1 / D, 1.0), ("p3", 2, 1 / D, 0.5)]
NIDX = {n: k for k, (n, *_) in enumerate(NORMS)}
SPREAD = ["hg", "peer", "final", "p0", "pc", "p1", "p2", "diff", "pa", "p3"]
X_AT = {n: 2 * (k + 1) for k, n in enumerate(["peer", "final", "p0", "pc", "p1", "p2", "pa", "p3"])}
UNITS = TT * PE_HEADS


SB_TABLES, N_TABLES = 9, 40


def build(nc, io):
    ctx = ExitStack()
    with ctx:
        def sb(name, shape, dt=F32):
            return ctx.enter_context(nc.sbuf_tensor(name, shape, dt))

        def sem(name):
            return ctx.enter_context(nc.semaphore(name))

        raw = [sb(f"raw{s}", [P, PANEL]) for s in range(SLOTS)]
        hi = [sb(f"hi{s}", [P, PANEL], F32R) for s in range(SLOTS)]
        lo = [sb(f"lo{s}", [P, PANEL], F32R) for s in range(SLOTS)]
        x = sb("x", [P, TT, D])
        xn = sb("xn", [P, TT, D])
        xh = sb("xh", [P, KD, T], F32R)
        xl = sb("xl", [P, KD, T], F32R)
        oh = sb("oh", [P, 3, PAIRS, T], F32R)
        ol = sb("ol", [P, 3, PAIRS, T], F32R)
        ah = sb("ah", [P, 2, T], F32R)
        al = sb("al", [P, 2, T], F32R)
        ident = sb("ident", [P, P])
        causal = sb("causal", [P, TT, T])
        cols = sb("cols", [P, 256])
        rowbuf = sb("rowbuf", [P, 3, P])
        gb = sb("gb", [P, D])
        minus_one = sb("minus_one", [P, 1])
        minus_half = sb("minus_half", [P, 16])
        slopes = sb("slopes", [P, 8])
        ss = sb("ss", [P, len(NORMS), 16])
        rstd = sb("rstd", [P, len(NORMS), 16])
        iota16 = sb("iota16", [P, PE_K])
        ARENA = 16400
        arena = sb("arena", [P, ARENA])
        top = [0]

        def carve(*shape, at=None, dt=None):
            n = int(np.prod(shape))
            a = top[0] if at is None else at
            top[0] = a + n
            assert top[0] <= ARENA, (top[0], ARENA)
            v = arena[:, a:a + n]
            if dt is not None:
                v = v.bitcast(dt)
            if len(shape) == 2:
                v = v.rearrange("p (a b) -> p a b", a=shape[0])
            if len(shape) == 3:
                v = v.rearrange("p (a b c) -> p a b c", a=shape[0], b=shape[1])
            return v

        dist = carve(TT, T)
        strict = carve(TT, T)
        level_mask = carve(LEVELS, P)
        zeros = carve(T)
        dist_c = carve(TT, CPAD)
        valid_c = carve(TT, CPAD)
        wcmp_k, wcmp_v = carve(CMP_LEN, HD), carve(CMP_LEN, HD)
        mixer_base = top[0]
        sb_q, sb_k, sb_v = carve(PAIRS, T), carve(PAIRS, T), carve(TT, SB_W)
        q_st, k_st, v_st = carve(T), carve(T), carve(TT, P)
        sb_u = [carve(TT, T) for _ in range(2)]
        sb_p = [carve(TT, T) for _ in range(2)]
        sb_e = [carve(TT, T + 1) for _ in range(2)]
        sb_a = [carve(TT, T) for _ in range(2)]
        sb_pt = [carve(3, P) for _ in range(2)]
        top[0] = mixer_base
        n_q = carve(PAIRS, T)
        n_cmp = carve(2, T)
        n_ksel, n_kwin, n_vsel, n_vwin = carve(T), carve(T), carve(TT, P), carve(TT, P)
        n_gate = carve(TT, N_GATES)
        cmp_blk = carve(2, CMP_LEN, N_CMP)
        kc, vc = carve(CPAD), carve(2, HD)
        nq_st = carve(T)
        n_sc = [carve(TT, T) for _ in range(4)]
        n_pt = [carve(3, P) for _ in range(4)]
        n_scc = carve(2, TT, CPAD)
        n_ptc = carve(2, TT, P)
        n_mx, n_sum, n_coef = carve(4, TT), carve(4, TT), carve(4, TT)
        c_mx, c_sum = carve(2, TT), carve(2, TT)
        nsa_end = top[0]
        top[0] = mixer_base - 2 * CMP_LEN * HD
        hg_q, hg_f = carve(HG_HEADS, T), carve(HG_HEADS, T)
        hg_i, hg_g = carve(TT, HG_W), carve(TT, HG_W)
        hg_k, hg_s, hg_o = carve(HG_HEADS, T), carve(HG_HEADS, T), carve(TT, HG_W)
        q_lev, k_lev = carve(LEVELS, T), carve(LEVELS, T)
        q_x, k_x, a_x = carve(P), carve(P), carve(P)
        hg_t = carve(2, T)
        a_m = [xn[:, t, :].rearrange("p (l t) -> p l t", l=LEVELS) for t in range(TT)]
        top[0] = mixer_base
        gm = [carve(4, T) for _ in range(2)]
        m_t = carve(KD, T)
        m_tmp = [carve(4, T) for _ in range(2)]
        top[0] = 0
        ring = [carve(D) for _ in range(RING)]
        pe_acc = carve(TT, D)
        pe_sc = carve(TT * 2, PE_HEADS, PE_KEYS)
        pe_s = carve(2, PE_KEYS)
        pe_cand = carve(PE_K, PE_K)
        pe_tv, pe_ti, pe_tif = carve(2, PE_K), carve(2, PE_K, dt=U32), carve(2, PE_K)
        pe_best, pe_nb, pe_pos = carve(PE_K), carve(1), carve(PE_K, dt=U32)
        pe_hl, pe_hlf, pe_e = carve(2, PE_K, dt=U32), carve(2, PE_K), carve(2, PE_K)
        pe_idx = carve(UNITS * PE_K, dt=U32)
        pe_exp, pe_sum = carve(UNITS * PE_K), carve(UNITS)
        pe_act = carve(UNITS * PE_K)
        pe_h, pe_gelu = carve(PE_K), carve(PE_K)
        pe_rec, pe_gate = carve(1), carve(PE_K)
        pe_carrier, pool_carrier = carve(1), carve(1)
        pe_hot = [pe_s.rearrange("p a k -> p (a k)").rearrange("p (k i) -> p k i", k=PE_K), pe_cand]
        pe_q = arena[:, 0:PE_HEADS * T].rearrange("p (h t) -> p h t", h=PE_HEADS)
        idx_now = sb("idx_now", [P, RING // GROUP, GROUP], U32)
        top[0] = 0
        ff_s, ff_a = carve(2, T), carve(2, T)
        cv_b, cv_c, cv_z = carve(2, T), carve(2, T), carve(2, T)
        cv_u = carve(2, T + CONV_W - 1)
        df_k, df_v, df_q = carve(DIFF_HEADS, T), carve(TT, D), carve(DIFF_HEADS, T)
        df_qs, df_ks = carve(2, T), carve(2, T)
        df_sc = [carve(TT, T) for _ in range(4)]
        df_pt = [carve(3, P) for _ in range(2)]
        df_o = carve(TT, D)
        df_mx, df_sum, df_r = carve(4, TT), carve(4, TT), carve(4, TT)
        lam_in, lam_dot, lam_exp, lam = carve(4, HD), carve(2), carve(2), carve(1)
        yh = oh[:, :, :, :].rearrange("p b k t -> p (b k) t")[:, 0:KD, :]
        yl = ol[:, :, :, :].rearrange("p b k t -> p (b k) t")[:, 0:KD, :]

        PS = [ctx.enter_context(nc.psum_tensor(f"ps{b}", [P, 512], F32)) for b in range(4)]
        ACC = ctx.enter_context(nc.psum_tensor("acc", [P, 4, 512], F32))

        def bank(b):
            return PS[b][:, :] if b < 4 else ACC[:, b - 4, :]

        x_loaded = sem("x_loaded")
        cols_loaded = sem("cols_loaded")
        wcmp_loaded = sem("wcmp_loaded")
        raw_ready = [sem(f"raw_ready{s}") for s in range(SLOTS)]
        spread_loaded = sem("spread_loaded")
        hi_done, lo_done = sem("hi_done"), sem("lo_done")
        panel_used = sem("panel_used")
        evacuated = sem("evacuated")
        tables = sem("tables")
        cols_turned, cols_ready = sem("cols_turned"), sem("cols_ready")
        sumsq = sem("sumsq")
        rstd_step, rstd_ready = sem("rstd_step"), sem("rstd_ready")
        rows_ready = sem("rows_ready")
        turned, turned_hi, turned_lo = sem("turned"), sem("turned_hi"), sem("turned_lo")
        x_updated = sem("x_updated")
        dve_step = sem("dve_step")
        gain_used = sem("gain_used")
        pe_chain2 = sem("pe_chain2")
        out_stored = sem("out_stored")
        sb_staged, sb_scored, sb_sig, sb_attn = sem("sb_staged"), sem("sb_scored"), sem("sb_sig"), sem("sb_attn")
        sb_scan, sb_turned, sb_pt_ready, sb_out = sem("sb_scan"), sem("sb_turned"), sem("sb_pt_ready"), sem("sb_out")
        o_hi, o_lo = sem("o_hi"), sem("o_lo")
        n_blk, n_kc, n_kc_ready = sem("n_blk"), sem("n_kc"), sem("n_kc_ready")
        n_staged, n_scored, n_biased, n_max = sem("n_staged"), sem("n_scored"), sem("n_biased"), sem("n_max")
        n_exp, n_scaled, n_turned, n_pt_ready, n_out = sem("n_exp"), sem("n_scaled"), sem("n_turned"), sem("n_pt_ready"), sem("n_out")
        n_chain = sem("n_chain")
        c_shift, c_exp, c_scaled = sem("c_shift"), sem("c_exp"), sem("c_scaled")
        h_silu, h_ones, h_lev, h_chain = sem("h_silu"), sem("h_ones"), sem("h_lev"), sem("h_chain")
        h_scored, h_masked, h_cross, h_out, h_o_ready = sem("h_scored"), sem("h_masked"), sem("h_cross"), sem("h_out"), sem("h_o_ready")
        h_zero = sem("h_zero")
        m_zero, m_added, m_mul = sem("m_zero"), sem("m_added"), sem("m_mul")
        m_hi, m_lo = sem("m_hi"), sem("m_lo")

        pe_scored, pe_sc_ready = sem("pe_scored"), sem("pe_sc_ready")
        pe_chain, idx_ready, idx_copied = sem("pe_chain"), sem("idx_ready"), sem("idx_copied")
        rows_landed = [sem(f"rows_landed{k}") for k in range(RING)]
        rows_used = sem("rows_used")
        best_ready, exp_done, gelu_done, act_ready = sem("best_ready"), sem("exp_done"), sem("gelu_done"), sem("act_ready")
        acc_zero = sem("acc_zero")
        ff_hi, ff_lo = sem("ff_hi"), sem("ff_lo")
        cv_pad, cv_chain, cv_y, cv_hi, cv_lo = sem("cv_pad"), sem("cv_chain"), sem("cv_y"), sem("cv_hi"), sem("cv_lo")
        lam_loaded, lam_dots, lam_exped, lam_ready = sem("lam_loaded"), sem("lam_dots"), sem("lam_exped"), sem("lam_ready")
        df_staged, df_scored, df_chain, df_max = sem("df_staged"), sem("df_scored"), sem("df_chain"), sem("df_max")
        df_exp, df_mixed, df_turned, df_pt_ready = sem("df_exp"), sem("df_mixed"), sem("df_turned"), sem("df_pt_ready")
        df_out, df_o_ready = sem("df_out"), sem("df_o_ready")

        def wait(eng, s, value):
            if not isinstance(value, int) or value > 0:
                eng.wait_ge(s, value)

        def along(table, p, m=0, i=0):
            return table[p] + i * (table[p + m] - table[p]) if m else table[p]

        def peeled(eng, n, body):
            body(0)
            with eng.Fori(1, n) as i:
                body(i)

        def w_in_cols(c, n):
            return io["w_in"][0, :, c:c + n].rearrange("(k p) n -> p k n", p=P)

        def rows_1024(w, c, n=PC):
            return w[:, c:c + n].rearrange("(k p) n -> p k n", p=P)

        block = ctx.enter_context(nc.Block())

        @block.sync
        def _(sp):
            sp.dma_start(x[:, :, :], io["x"][0].rearrange("(t p) d -> p t d", p=P)).then_inc(x_loaded, 16)

            def load(p, src, m=0, i=0):
                wait(sp, lo_done, p + m * i - (SLOTS - 1))
                k = src.shape[1]
                sp.dma_start(raw[p % SLOTS][:, 0:k * src.shape[2]].rearrange("p (k n) -> p k n", k=k), src)\
                    .then_inc(raw_ready[p % SLOTS], 16)

            p = 0
            for c in (C_SBQ, C_SBK, C_SBV):
                for j in range(2):
                    load(p, w_in_cols(c + j * PC, PC))
                    p += 1
            for j in range(2):
                wait(sp, lo_done, p - (SLOTS - 1))
                dst = raw[p % SLOTS][:, :].rearrange("p (k q d) -> p k q d", k=KD, q=4)
                for q in range(4):
                    h = 2 * j + q // 2 + 4 * (q % 2)
                    sp.dma_start(dst[:, :, q, :], w_in_cols(C_NQ + h * HD, HD)).then_inc(raw_ready[p % SLOTS], 16)
                p += 1
            for c in (C_CMP, C_SEL, C_WIN):
                load(p, w_in_cols(c, PC))
                p += 1
            load(p, w_in_cols(C_NG, N_GATES))
            p += 1
            for c in (C_HQ, C_HF, C_HI, C_HG):
                for j in range(2):
                    load(p, w_in_cols(c + j * PC, PC))
                    p += 1
            for b, name in enumerate(("w_branch_sb", "w_branch_nsa", "w_branch_hgrn")):
                for half in range(2):
                    for j in range(2):
                        load(p, w_in_cols(C_MERGE + b * D + half * 512 + j * PC, PC))
                        p += 1
                    wait(sp, lo_done, p - (SLOTS - 1))
                    dst = raw[p % SLOTS][:, :].rearrange("p (i n) -> p i n", i=PAIRS)
                    w = io[name][0, :, half * 512:(half + 1) * 512]
                    for a in range(2):
                        src = (w.rearrange("(a i d) n -> a d i n", a=2, d=HD) if b == 1 else
                               w.rearrange("(i a d) n -> a d i n", a=2, d=HD))[a]
                        sp.dma_start(dst[a * HD:(a + 1) * HD], src).then_inc(raw_ready[p % SLOTS], 16)
                    p += 1
            for name in ("w_out", "peer_w_q"):
                for j in range(4):
                    load(p, rows_1024(io[name][0], j * PC))
                    p += 1

            def load_ffn(f):
                l, k = f // 2, f % 2
                gate, up, down = (io[f"w_ffn_{n}_2"][l, k] for n in ("gate", "up", "down"))
                p0 = FIRST[f"ffn{f}"]

                def down_rows(i):
                    return down[bass.ds(i * PC, PC), :].rearrange("(f p) n -> p f n", p=P)

                def column(w, i):
                    return w[:, bass.ds(i * PC, PC)].rearrange("(k p) n -> p k n", p=P)

                load(p0, column(gate, 0))
                load(p0 + 1, column(up, 0))
                with sp.Fori(1, FF_STEPS) as i:
                    load(p0 + 2, column(gate, i), 3, i - 1)
                    load(p0 + 3, column(up, i), 3, i - 1)
                    load(p0 + 4, down_rows(i - 1), 3, i - 1)
                load(p0 + 3 * FF_STEPS - 1, down_rows(FF_STEPS - 1))

            load_ffn(0)
            p0 = FIRST["conv_in"]
            for j in range(4):
                for w in range(3):
                    load(p0 + 3 * j + w, rows_1024(io["w_conv_in_2"][0], w * D + j * PC))
            for j in range(4):
                load(FIRST["conv_out"] + j, rows_1024(io["w_conv_out_2"][0], j * PC))
            load_ffn(1)
            for j in range(8):
                load(FIRST["kv"] + j, rows_1024(io["w_kv_2"], j * PC))
            load_ffn(2)
            for j in range(4):
                load(FIRST["q"] + j, rows_1024(io["w_q_2"][0], j * PC))
            for j in range(4):
                load(FIRST["o"] + j, rows_1024(io["w_o_2"][0], j * PC))
            load_ffn(3)
            sp.wait_ge(x_updated, X_AT["p3"])
            sp.dma_start(io["out"][0].rearrange("(t p) d -> p t d", p=P), x[:, :, :]).then_inc(out_stored, 16)
            sp.wait_ge(out_stored, 16)

        @block.gpsimd
        def _(pool):
            steps = [0]

            def table(ins):
                steps[0] += 1
                ins.then_inc(tables, 1)
                pool.wait_ge(tables, steps[0])

            def select(view, pattern, base, mult, op, fill):
                table(nc.gpsimd.affine_select(out=view, in_=view, pattern=pattern, base=base,
                                              channel_multiplier=mult, compare_op=op, fill=fill))

            g = nc.gpsimd
            table(g.memset(ident[:, :], 0.0))
            select(ident[:, :], [[-1, P]], 0, 1, ALU.not_equal, 1.0)
            table(g.memset(minus_half[:, :], -0.5))
            table(g.memset(minus_one[:, :], -1.0))
            rstd_steps = [0]

            def norm(name):
                k = NIDX[name]
                _, w, scale, factor = NORMS[k]
                s, r = ss[:, k, 0:w], rstd[:, k, 0:w]
                pool.wait_ge(sumsq, 2 * (k + 1))
                g.tensor_scalar(s, s, scale, EPS, ALU.mult, ALU.add).then_inc(rstd_step, 1)
                pool.wait_ge(rstd_step, rstd_steps[0] + 1)
                g.tensor_tensor(r, s, minus_half[:, 0:w], ALU.pow).then_inc(rstd_step, 1)
                pool.wait_ge(rstd_step, rstd_steps[0] + 2)
                g.tensor_scalar(r, r, factor, None, ALU.mult).then_inc(rstd_ready, 1)
                rstd_steps[0] += 2

            norm("mix")
            table(g.memset(strict[:, :, :], 0.0))
            select(strict, [[P, TT], [-1, T]], 0, 1, ALU.is_gt, NEG)
            table(g.memset(zeros, 0.0))
            for a in range(2):
                table(g.memset(sb_e[a][:, :, 0:1], 1.0))
            sb_tables_done = steps[0]
            table(g.iota(dist, [[P, TT], [-1, T]], base=0, channel_multiplier=1, allow_small_or_imprecise_dtypes=True))
            select(dist, [[P, TT], [-1, T]], 0, 1, ALU.is_ge, FAR)
            pat = [[P, TT], [-CMP_STRIDE, CPAD]]
            table(g.iota(dist_c, pat, base=1 - CMP_LEN, channel_multiplier=1, allow_small_or_imprecise_dtypes=True))
            select(dist_c, pat, 1 - CMP_LEN, 1, ALU.is_ge, FAR)
            table(g.memset(valid_c, 1.0))
            select(valid_c, pat, 1 - CMP_LEN, 1, ALU.is_ge, 0.0)
            for h in range(8):
                table(g.memset(slopes[:, h:h + 1], -2.0 ** -(h + 1)))
            table(g.memset(level_mask, 1.0))
            select(level_mask[:, 0, :], [[-1, P]], 0, 1, ALU.is_equal, 0.0)
            for l in range(1, LEVELS - 1):
                w = 2 ** l
                v = level_mask[:, l, :].rearrange("p (b w) -> p b w", w=w)
                select(v, [[-w, P // w], [0, w]], 0, 1, ALU.is_ge, 0.0)
                select(v, [[w, P // w], [0, w]], w - 1, -1, ALU.is_ge, 0.0)
            table(g.memset(causal[:, :, :], 0.0))
            select(causal[:, :, :], [[P, TT], [-1, T]], 0, 1, ALU.is_ge, NEG)
            table(g.iota(iota16[:, :], [[1, PE_K]], base=0, channel_multiplier=0, allow_small_or_imprecise_dtypes=True))
            assert steps[0] == N_TABLES and sb_tables_done == SB_TABLES, (steps[0], sb_tables_done)

            pool.wait_ge(evacuated, EVAC[FIRST["nsa_q"]])

            def stage(i):
                wait(pool, sb_scored, 2 * i)
                g.tensor_copy(q_st, sb_q[:, bass.ds(i, 1), :].rearrange("p a t -> p (a t)")).then_inc(sb_staged, 1)
                g.tensor_copy(k_st, sb_k[:, bass.ds(i, 1), :].rearrange("p a t -> p (a t)")).then_inc(sb_staged, 1)
                wait(pool, sb_out, 2 * i)
                g.tensor_copy(v_st, sb_v[:, :, bass.ds(i * P, P)]).then_inc(sb_staged, 1)

            peeled(pool, PAIRS, stage)
            pool.wait_ge(sb_out, 2 * PAIRS)
            g.memset(vc, 0.0).then_inc(n_kc_ready, 1)
            g.memset(kc, 0.0).then_inc(n_kc_ready, 1)
            pool.wait_ge(evacuated, EVAC[FIRST["hg"]])

            def stage_nsa(i):
                wait(pool, n_scored, 5 * i)
                g.tensor_copy(nq_st, n_q[:, bass.ds(i, 1), :].rearrange("p a t -> p (a t)")).then_inc(n_staged, 1)

            peeled(pool, PAIRS, stage_nsa)
            pool.wait_ge(n_out, 2 * PAIRS)
            pool.wait_ge(o_lo, 2 * PAIRS)
            g.memset(q_lev, 0.0).then_inc(h_zero, 1)
            g.memset(k_lev, 0.0).then_inc(h_zero, 1)
            g.memset(hg_s, 1.0).then_inc(h_zero, 1)
            g.dma_start(gb[:, 0:HG_W], io["hgrn_norm"].partition_broadcast(P).rearrange("p a n -> p (a n)")).then_inc(spread_loaded, 16)
            norm("hg")
            pool.wait_ge(turned, XEND["hg"])
            g.memset(m_t, 0.0).then_inc(m_zero, 1)

            spread = {"hg": io["hgrn_norm"], "peer": io["norm_ffn"], "final": io["norm_final"].unsqueeze(0),
                      "p0": io["g_norm_2"][0, 1:2], "pc": io["g_norm_2"][0, 3:4], "p1": io["g_norm_2"][0, 5:6],
                      "p2": io["g_norm_2"][1, 1:2], "diff": io["g_subln_2"], "pa": io["g_norm_2"][1, 3:4],
                      "p3": io["g_norm_2"][1, 5:6]}

            def load_gain(name):
                pool.wait_ge(gain_used, SPREAD.index(name))
                src = spread[name]
                g.dma_start(gb[:, 0:src.shape[1]], src.partition_broadcast(P).rearrange("p a n -> p (a n)")).then_inc(spread_loaded, 16)

            load_gain("peer")
            norm("peer")
            pool.wait_ge(m_lo, 2)
            g.memset(pe_acc, 0.0).then_inc(acc_zero, 1)
            pool.wait_ge(pe_scored, TT)

            def gather(table_, n, group0):
                for r in range(PE_K // GROUP):
                    q = r % (RING // GROUP)
                    wait(pool, rows_used, GROUP * (group0 + r - 1) if not isinstance(group0, int) or group0 + r > 1 else 0)
                    g.tensor_copy(idx_now[:, q, :], pe_idx[:, bass.ds(n * PE_K + r * GROUP, GROUP)]).then_inc(idx_copied, 1)
                    pool.wait_ge(idx_copied, 2 * (group0 + r) + 1)
                    g.tensor_tensor(pool_carrier, minus_half[:, 0:1], minus_half[:, 0:1], ALU.mult).then_inc(idx_copied, 1)
                    for k in range(GROUP):
                        slot = q * GROUP + k
                        g.indirect_dma_start(out=ring[slot], out_offset=None, in_=table_,
                                             in_offset=bass.IndirectOffsetOnAxis(ap=idx_now[:, q, k:k + 1], axis=0))\
                            .then_inc(rows_landed[slot], 16)

            u_rows, v_rows = io["peer_u"].rearrange("a e d -> (a e) d"), io["peer_v"].rearrange("a e d -> (a e) d")
            pool.wait_ge(idx_ready, 1)
            gather(u_rows, 0, 0)
            with pool.Fori(1, UNITS) as n:
                pool.wait_ge(idx_ready, n + 1)
                gather(u_rows, n, 8 * n - 4)
                gather(v_rows, n - 1, 8 * n)
            gather(v_rows, UNITS - 1, 8 * UNITS - 4)
            load_gain("final")
            norm("final")

            def post(name):
                load_gain(name)
                norm(name)

            norm("f0")
            post("p0")
            g.memset(cv_u, 0.0).then_inc(cv_pad, 1)
            for k, nm in enumerate(("lambda_q1_2", "lambda_k1_2", "lambda_q2_2", "lambda_k2_2")):
                g.dma_start(lam_in[:, k, :], io[nm].partition_broadcast(P).rearrange("p a n -> p (a n)")).then_inc(lam_loaded, 16)
            norm("conv")
            post("pc")
            norm("f1")
            post("p1")
            norm("kv")
            norm("f2")
            post("p2")
            norm("attn")
            load_gain("diff")
            pool.wait_ge(evacuated, EVAC[FIRST["o"]])

            def stage_diff(i):
                wait(pool, df_scored, 4 * i)
                for dst, src in ((df_qs, df_q), (df_ks, df_k)):
                    g.tensor_copy(dst, src[:, bass.ds(2 * i, 2), :]).then_inc(df_staged, 1)

            peeled(pool, DIFF_HEADS // 2, stage_diff)
            norm("diff")
            post("pa")
            norm("f3")
            post("p3")

        @block.scalar
        def _(act):
            def split(p, m=0, i=0):
                s = p % SLOTS
                act.wait_ge(raw_ready[s], along(LANDED, p, m, i))
                wait(act, panel_used, p + m * i - (SLOTS - 1))
                nc.scalar.activation(hi[s][:, 0:WORDS[p]], raw[s][:, 0:WORDS[p]], ACT.Copy).then_inc(hi_done, 1)

            def evac(p, out, func=ACT.Copy, scale=1.0, in_=None, m=0, i=0):
                act.wait_ge(panel_used, p + m * i + 1)
                nc.scalar.activation(out, bank(BANK[p]) if in_ is None else in_, func, scale=scale).then_inc(evacuated, 1)

            for n, (src, r) in enumerate([(io["norm_mix"][0], GAIN["mix"]), (io["norm_ffn"][0], GAIN["peer"]), (io["g_kv_2"], GAIN["kv"])]
                                         + [(io["g_norm_2"][l, j], GAIN[nm]) for l, j, nm in
                                            ((0, 0, "f0"), (0, 2, "conv"), (0, 4, "f1"), (1, 0, "f2"), (1, 2, "attn"), (1, 4, "f3"))]):
                act.dma_start(rowbuf[r:r + 8, 0, :], src.rearrange("(c p) -> c p", p=P)).then_inc(cols_loaded, 16)
            act.dma_start(rowbuf[TAPS:TAPS + 24, 0, :], io["w_conv_2"][0].rearrange("j (c p) -> (j c) p", p=P)).then_inc(cols_loaded, 16)
            for a in range(2):
                act.dma_start(rowbuf[0:CMP_LEN, 1, a * HD:(a + 1) * HD], io["nsa_cmp_pe"][0]).then_inc(cols_loaded, 16)
                act.dma_start(rowbuf[:, 2, a * HD:(a + 1) * HD], io["peer_sub_keys"][0, a]).then_inc(cols_loaded, 16)
            for a in range(2):
                for w, name in ((wcmp_k, "nsa_w_cmp_k"), (wcmp_v, "nsa_w_cmp_v")):
                    act.dma_start(w[a * HD:(a + 1) * HD], io[name][0].rearrange("(l d) j -> d l j", d=HD)).then_inc(wcmp_loaded, 16)

            def sum_squares(name):
                k = NIDX[name]
                nc.scalar.activation(xn[:, 0, :], x[:, 0, :], ACT.Square, accum_out=ss[:, k, 0:1]).then_inc(sumsq, 1)

            def norm_rows(name):
                k = NIDX[name]
                wait(act, turned, XBASE[name])
                sum_squares(name)
                act.wait_ge(rstd_ready, k + 1)
                nc.scalar.activation(xn[:, 1, :], x[:, 1, :], ACT.Copy, scale=rstd[:, k, 1:2]).then_inc(rows_ready, 1)

            def turn(name, out, gain):
                n = XEND[name] - XBASE[name]
                for b in range(n):
                    act.wait_ge(turned, XBASE[name] + b + 1)
                    src = ACC[:, b, :].rearrange("p (k t) -> p k t", k=2)
                    if gain is None:
                        nc.scalar.activation(out[:, 2 * b:2 * b + 2, :], src, ACT.Copy).then_inc(turned_hi, 2)
                        continue
                    for j in range(2):
                        c = GAIN[gain] + 2 * b + j
                        nc.scalar.activation(out[:, 2 * b + j, :], src[:, j, :], ACT.Copy, scale=cols[:, c:c + 1])\
                            .then_inc(turned_hi, 1)

            act.wait_ge(x_loaded, 16)
            norm_rows("mix")
            act.wait_ge(cols_turned, 1)
            nc.scalar.activation(cols[:, :], bank(3)[:, 0:256], ACT.Copy).then_inc(cols_ready, 1)
            split(0)
            split(1)
            act.wait_ge(cols_ready, 1)
            turn("mix", xh, "mix")

            for j in range(2):
                split(j + 2)
                evac(j, sb_q[:, 2 * j:2 * j + 2, :].rearrange("p a t -> p (a t)"), scale=HD ** -0.5)
            for j in range(2):
                split(j + 4)
                evac(2 + j, sb_k[:, 2 * j:2 * j + 2, :].rearrange("p a t -> p (a t)"))
            for j in range(2):
                split(j + 6)
                evac(4 + j, sb_v[:, :, j * PC:(j + 1) * PC], in_=bank(BANK[4 + j]).rearrange("p (t n) -> p t n", t=TT))

            def sb_pair(i):
                for a in range(2):
                    act.wait_ge(sb_scored, 2 * i + a + 1)
                    wait(act, sb_attn, 2 * i + a - 1)
                    z = bank(4 + a).rearrange("p (t s) -> p t s", t=TT)
                    nc.scalar.activation(sb_u[a], z, ACT.Sigmoid, scale=-1.0).then_inc(sb_sig, 1)
                    nc.scalar.activation(sb_p[a], z, ACT.Sigmoid).then_inc(sb_sig, 1)
                for a in range(2):
                    act.wait_ge(sb_turned, 2 * i + a + 1)
                    wait(act, sb_out, 2 * i + a - 1)
                    nc.scalar.activation(sb_pt[a].rearrange("p a b -> p (a b)"), bank(6 + a)[:, 0:3 * P], ACT.Copy).then_inc(sb_pt_ready, 1)
                act.wait_ge(sb_out, 2 * i + 2)
                nc.scalar.activation(oh[:, 0, bass.ds(i, 1), :], bank(3)[:, 0:T].rearrange("p (a t) -> p a t", a=1), ACT.Copy).then_inc(o_hi, 1)

            peeled(act, PAIRS, sb_pair)

            act.wait_ge(o_lo, PAIRS)
            q0 = FIRST["nsa_q"]
            for j in range(2):
                split(q0 + j + 2)
                evac(q0 + j, n_q[:, 2 * j:2 * j + 2, :].rearrange("p a t -> p (a t)"), scale=HD ** -0.5)
            c0 = FIRST["nsa_kv"]
            split(c0 + 2)
            evac(c0, n_cmp.rearrange("p a t -> p (a t)"))
            for j, (k_, v_) in enumerate(((n_ksel, n_vsel), (n_kwin, n_vwin))):
                split(c0 + 3 + j)
                act.wait_ge(panel_used, c0 + 2 + j)
                b = bank(BANK[c0 + 1 + j])
                nc.scalar.activation(k_, b[:, 0:T], ACT.Copy)
                nc.scalar.activation(v_, b[:, T:2 * T].rearrange("p (t n) -> p t n", t=TT), ACT.Copy).then_inc(evacuated, 1)
            g0 = FIRST["nsa_gate"]
            split(g0 + 2)
            evac(g0, n_gate, func=ACT.Sigmoid, in_=bank(BANK[g0])[:, 0:TT * N_GATES].rearrange("p (t n) -> p t n", t=TT))
            act.wait_ge(n_kc, 1)
            act.wait_ge(n_kc_ready, 2)
            nc.scalar.activation(kc[:, 0:N_CMP], bank(2)[:, 0:N_CMP], ACT.Copy)
            nc.scalar.activation(vc[0:N_CMP, 0, :], bank(3)[0:N_CMP, 0:HD], ACT.Copy)
            nc.scalar.activation(vc[0:N_CMP, 1, :], bank(4)[0:N_CMP, 0:HD], ACT.Copy).then_inc(n_kc_ready, 1)

            def nsa_pair(i):
                act.wait_ge(c_shift, i + 1)
                nc.scalar.activation(n_scc, n_scc, ACT.Exp).then_inc(c_exp, 1)
                for u in range(4):
                    act.wait_ge(n_max, 4 * i + u + 1)
                    for t in range(TT):
                        nc.scalar.activation(n_sc[u][:, t, :], n_sc[u][:, t, :], ACT.Exp, bias=n_mx[:, u, t:t + 1],
                                             accum_out=n_sum[:, u, t:t + 1]).then_inc(n_exp, 1)
                for u in range(5):
                    act.wait_ge(n_turned, 5 * i + u + 1)
                    wait(act, n_out, 2 * i)
                    if u < 4:
                        nc.scalar.activation(n_pt[u].rearrange("p a b -> p (a b)"), bank(4 + u)[:, 0:3 * P], ACT.Copy).then_inc(n_pt_ready, 1)
                    else:
                        nc.scalar.activation(n_ptc[0:CPAD].rearrange("p a t s -> p (a t s)"), bank(3)[0:CPAD, :], ACT.Copy).then_inc(n_pt_ready, 1)
                act.wait_ge(n_out, 2 * i + 2)
                nc.scalar.activation(oh[:, 1, bass.ds(i, 1), :], bank(2)[:, 0:T].rearrange("p (a t) -> p a t", a=1), ACT.Copy).then_inc(o_hi, 1)

            peeled(act, PAIRS, nsa_pair)

            act.wait_ge(o_lo, 2 * PAIRS)
            h0 = FIRST["hg"]
            flat = lambda v, j: v[:, 2 * j:2 * j + 2, :].rearrange("p a t -> p (a t)")
            for j in range(2):
                split(h0 + j + 2)
                act.wait_ge(panel_used, h0 + j + 1)
                if j:
                    act.wait_ge(h_silu, 1)
                nc.scalar.activation(flat(hg_q, j), bank(BANK[h0 + j]), ACT.Sigmoid)
                nc.scalar.activation(hg_t.rearrange("p a t -> p (a t)"), bank(BANK[h0 + j]), ACT.Copy).then_inc(evacuated, 1)
            for j in range(2):
                split(h0 + j + 4)
                evac(h0 + 2 + j, flat(hg_f, j), func=ACT.Sigmoid)
            for j in range(2):
                split(h0 + j + 6)
                b = bank(BANK[h0 + 4 + j]).rearrange("p (t n) -> p t n", t=TT)
                evac(h0 + 4 + j, hg_i[:, :, j * PC:(j + 1) * PC], in_=b)
            for j in range(2):
                split(h0 + j + 8)
                act.wait_ge(panel_used, h0 + 6 + j + 1)
                act.wait_ge(h_silu, (2, 4)[j])
                b = bank(BANK[h0 + 6 + j]).rearrange("p (t n) -> p t n", t=TT)
                nc.scalar.activation(hg_g[:, :, j * PC:(j + 1) * PC], b, ACT.Sigmoid)
                nc.scalar.activation(hg_t, b, ACT.Copy).then_inc(evacuated, 1)

            def hg_head(i):
                act.wait_ge(h_scored, i + 1)
                wait(act, h_out, i)
                nc.scalar.activation(a_x, bank(3)[:, 0:P], ACT.Copy).then_inc(h_cross, 1)
                act.wait_ge(h_out, i + 1)
                nc.scalar.activation(hg_o[:, :, bass.ds(i * P, P)], bank(2)[:, 0:2 * P].rearrange("p (t v) -> p t v", t=TT), ACT.Copy).then_inc(h_o_ready, 1)

            peeled(act, HG_HEADS, hg_head)
            turn("hg", oh[:, 2, :, :], None)

            def merge(b):
                for half in range(2):
                    p = FIRST["merge"] + 3 * half
                    for j in range(2):
                        split(p + j + 2, 6, b)
                        wait(act, m_mul, 2 * b + half - 1)
                        evac(p + j, gm[half][:, 2 * j:2 * j + 2, :].rearrange("p a t -> p (a t)"), func=ACT.Sigmoid, m=6, i=b)
                    split(p + 4, 6, b)

            peeled(act, 3, merge)

            act.wait_ge(panel_used, FIRST["w_out"])
            for half in range(2):
                act.wait_ge(m_added, 5 + half)
                nc.scalar.activation(xh[:, 4 * half:4 * half + 4, :], m_t[:, 4 * half:4 * half + 4, :], ACT.Copy).then_inc(m_hi, 1)
            for j in range(4):
                split(FIRST["w_out"] + j + 2)

            act.wait_ge(evacuated, EVAC[FIRST["peer_q"]])
            norm_rows("peer")
            turn("peer", xh, "peer")
            p0 = FIRST["peer_q"]
            for j in range(4):
                split(p0 + j + 2)
                evac(p0 + j, pe_q[:, 2 * j:2 * j + 2, :].rearrange("p h t -> p (h t)"))
            for t in range(TT):
                act.wait_ge(pe_scored, t + 1)
                for a in range(2):
                    nc.scalar.activation(pe_sc[:, 2 * t + a].rearrange("p h k -> p (h k)"),
                                         ACC[:, 2 * a:2 * a + 2, :].rearrange("p b n -> p (b n)"), ACT.Copy).then_inc(pe_sc_ready, 1)

            def best_exp(n):
                act.wait_ge(best_ready, n + 1)
                nc.scalar.activation(pe_exp[:, bass.ds(n * PE_K, PE_K)], pe_best, ACT.Exp, bias=pe_nb,
                                     accum_out=pe_sum[:, bass.ds(n, 1)]).then_inc(exp_done, 1)

            def gelu(n, rows_before):
                act.wait_ge(rows_used, rows_before + PE_K)
                wait(act, act_ready, n)
                nc.scalar.activation(pe_gelu, pe_h, ACT.Gelu).then_inc(gelu_done, 1)

            best_exp(0)
            gelu(0, 0)
            best_exp(1)
            with act.Fori(1, UNITS - 1) as n:
                gelu(n, 2 * PE_K * n - PE_K)
                best_exp(n + 1)
            gelu(UNITS - 1, 2 * PE_K * (UNITS - 1) - PE_K)
            act.wait_ge(x_updated, X_AT["peer"])
            sum_squares("final")

            def ffn(f):
                p0 = FIRST[f"ffn{f}"]
                last = p0 + 3 * FF_STEPS - 1

                def silu(p, m=0, r=0):
                    act.wait_ge(panel_used, p + m * r + 1)
                    act.wait_ge(evacuated, along(EVAC, p, m, r))
                    nc.scalar.activation(ff_s.rearrange("p f t -> p (f t)"), bank(BANK[p]), ACT.Silu).then_inc(evacuated, 1)

                def upper(p, down_done, m=0, r=0):
                    act.wait_ge(evacuated, along(EVAC, p, m, r) + 2)
                    act.wait_ge(panel_used, down_done)
                    nc.scalar.activation(ah[:, :, :], ff_a, ACT.Copy).then_inc(ff_hi, 1)

                split(p0 + 2)
                split(p0 + 3)
                silu(p0)
                upper(p0, p0)

                def step(i, next_up=True):
                    split(p0 + 4, 3, i - 1)
                    split(p0 + 5, 3, i - 1)
                    silu(p0 + 2, 3, i - 1)
                    if next_up:
                        split(p0 + 6, 3, i - 1)
                    upper(p0 + 2, p0 + 5 + 3 * (i - 1), 3, i - 1)

                with act.Fori(1, FF_STEPS - 1) as i:
                    step(i)
                step(FF_STEPS - 1, last + 1 < NP)
                if last + 2 < NP:
                    split(last + 2)

            def post(name, panels):
                k = NIDX[name]
                act.wait_ge(panel_used, panels)
                for t in range(TT):
                    nc.scalar.activation(xn[:, t, :], ACC[:, 2 * t:2 * t + 2, :].rearrange("p b n -> p (b n)"), ACT.Square,
                                         accum_out=ss[:, k, t:t + 1]).then_inc(sumsq, 1)

            def normed(name, x_at):
                act.wait_ge(x_updated, x_at)
                norm_rows(name)
                turn(name, xh, name)

            normed("f0", X_AT["final"])
            ffn(0)
            post("p0", FIRST["conv_in"])
            normed("conv", X_AT["p0"])
            p0 = FIRST["conv_in"]

            def conv(j):
                for w, out in enumerate((cv_b, cv_c, None)):
                    split(p0 + w + 2, 3, j)
                    if out is not None:
                        wait(act, cv_y, j)
                        evac(p0 + w, out.rearrange("p f t -> p (f t)"), m=3, i=j)
                act.wait_ge(cv_y, j + 1)
                nc.scalar.activation(yh[:, bass.ds(2 * j, 2), :], cv_z, ACT.Copy).then_inc(cv_hi, 1)

            peeled(act, 4, conv)
            for j in range(4):
                split(FIRST["conv_out"] + j + 2)
            post("pc", FIRST["ffn1"])
            normed("f1", X_AT["pc"])
            ffn(1)
            post("p1", FIRST["kv"])
            normed("kv", X_AT["p1"])
            for j in range(8):
                p = FIRST["kv"] + j
                split(p + 2)
                if j < 4:
                    evac(p, df_k[:, 2 * j:2 * j + 2, :].rearrange("p h t -> p (h t)"))
                else:
                    c = (j - 4) * PC
                    evac(p, df_v[:, :, c:c + PC], in_=bank(BANK[p]).rearrange("p (t n) -> p t n", t=TT))
            normed("f2", X_AT["p1"])
            ffn(2)
            post("p2", FIRST["q"])
            normed("attn", X_AT["p2"])
            for j in range(4):
                p = FIRST["q"] + j
                split(p + 2)
                evac(p, df_q[:, 2 * j:2 * j + 2, :].rearrange("p h t -> p (h t)"), scale=HD ** -0.5)
            act.wait_ge(lam_dots, 2)
            nc.scalar.activation(lam_exp, lam_dot, ACT.Exp).then_inc(lam_exped, 1)

            def diff_heads(i):
                for u in range(4):
                    act.wait_ge(df_max, 4 * i + u + 1)
                    for t in range(TT):
                        nc.scalar.activation(df_sc[u][:, t, :], df_sc[u][:, t, :], ACT.Exp, bias=df_mx[:, u, t:t + 1],
                                             accum_out=df_sum[:, u, t:t + 1]).then_inc(df_exp, 1)
                for h in range(2):
                    act.wait_ge(df_turned, 2 * i + h + 1)
                    wait(act, df_out, 2 * i + h - 1)
                    nc.scalar.activation(df_pt[h].rearrange("p n t -> p (n t)"), bank(4 + 2 * h)[:, 0:3 * P], ACT.Copy).then_inc(df_pt_ready, 1)
                for h in range(2):
                    act.wait_ge(df_out, 2 * i + h + 1)
                    nc.scalar.activation(df_o[:, :, bass.ds(2 * i * P + h * P, P)], bank(2 + h)[:, 0:TT * P].rearrange("p (t e) -> p t e", t=TT),
                                         ACT.Copy).then_inc(df_o_ready, 1)

            peeled(act, DIFF_HEADS // 2, diff_heads)
            turn("diff", xh, None)
            for j in range(4):
                split(FIRST["o"] + j + 2)
            post("pa", FIRST["ffn3"])
            normed("f3", X_AT["pa"])
            ffn(3)
            post("p3", NP)

        @block.vector
        def _(dve):
            v = nc.vector
            chain = [0]

            def link(ins):
                chain[0] += 1
                ins.then_inc(dve_step, 1)
                dve.wait_ge(dve_step, chain[0])

            def split(p, m=0, i=0):
                s = p % SLOTS
                dve.wait_ge(hi_done, p + m * i + 1)
                v.tensor_tensor(lo[s][:, 0:WORDS[p]], raw[s][:, 0:WORDS[p]], hi[s][:, 0:WORDS[p]].bitcast(F32), ALU.subtract).then_inc(lo_done, 1)

            def sum_squares(name):
                k = NIDX[name]
                v.scalar_tensor_tensor(out=xn[:, 1, :], in0=x[:, 1, :], scalar=1.0, in1=x[:, 1, :], op0=ALU.mult,
                                       op1=ALU.mult, accum_out=ss[:, k, 1:2]).then_inc(sumsq, 1)

            def norm_rows(name):
                k = NIDX[name]
                wait(dve, turned, XBASE[name])
                sum_squares(name)
                dve.wait_ge(rstd_ready, k + 1)
                v.tensor_scalar(xn[:, 0, :], x[:, 0, :], rstd[:, k, 0:1], None, ALU.mult).then_inc(rows_ready, 1)

            def turn(name, out_hi, out_lo, gain):
                n = XEND[name] - XBASE[name]
                for b in range(n):
                    dve.wait_ge(turned_hi, 2 * (XBASE[name] + b + 1))
                    src = ACC[:, b, :].rearrange("p (k t) -> p k t", k=2)
                    for j in range(2):
                        s = 1.0 if gain is None else cols[:, GAIN[gain] + 2 * b + j:GAIN[gain] + 2 * b + j + 1]
                        v.scalar_tensor_tensor(out=out_lo[:, 2 * b + j, :], in0=src[:, j, :], scalar=s,
                                               in1=out_hi[:, 2 * b + j, :].bitcast(F32), op0=ALU.mult, op1=ALU.subtract).then_inc(turned_lo, 1)

            dve.wait_ge(x_loaded, 16)
            norm_rows("mix")
            split(0)
            split(1)
            dve.wait_ge(cols_ready, 1)
            turn("mix", xh, xl, "mix")
            for j in range(6):
                split(j + 2)

            dve.wait_ge(tables, SB_TABLES)

            def sb_pair(i):
                for a in range(2):
                    dve.wait_ge(sb_sig, 4 * i + 2 * a + 1)
                    for t in range(TT):
                        v.tensor_tensor_scan(out=sb_e[a][:, t, 1:T + 1], data0=sb_u[a][:, t, ::-1], data1=zeros, initial=1.0,
                                             op0=ALU.mult, op1=ALU.add).then_inc(sb_scan, 1)
                    dve.wait_ge(sb_scan, 4 * i + 2 * a + 2)
                    dve.wait_ge(sb_sig, 4 * i + 2 * a + 2)
                    wait(dve, sb_turned, 2 * i + a - 1)
                    v.tensor_tensor(sb_a[a], sb_p[a], sb_e[a][:, :, T - 1::-1], ALU.mult).then_inc(sb_attn, 1)
                dve.wait_ge(o_hi, i + 1)
                v.tensor_tensor(ol[:, 0, bass.ds(i, 1), :], bank(3)[:, 0:T].rearrange("p (a t) -> p a t", a=1),
                                oh[:, 0, bass.ds(i, 1), :].bitcast(F32), ALU.subtract).then_inc(o_lo, 1)

            peeled(dve, PAIRS, sb_pair)

            for j in range(3):
                split(FIRST["nsa_kv"] + j)
            dve.wait_ge(evacuated, EVAC[FIRST["nsa_kv"] + 1])
            for w in range(2):
                src = n_cmp[:, w, :].rearrange("p (n l) -> p l n", l=CMP_STRIDE)
                for j in range(2):
                    l0 = j * CMP_STRIDE
                    pe_ = cols[:, 96 + l0:96 + l0 + CMP_STRIDE].unsqueeze(2).to_broadcast([P, CMP_STRIDE, N_CMP])
                    v.tensor_tensor(cmp_blk[:, w, l0:l0 + CMP_STRIDE, :], src[:, :, j:j + N_CMP], pe_, ALU.add).then_inc(n_blk, 1)
            for j in range(3):
                split(FIRST["nsa_kv"] + 3 + j)
            dve.wait_ge(tables, N_TABLES)
            dve.wait_ge(evacuated, EVAC[FIRST["hg"]])

            def nsa_pair(i):
                c = 25 * i
                done = [0]

                def then(ins):
                    done[0] += 1
                    ins.then_inc(n_chain, 1)
                    dve.wait_ge(n_chain, c + done[0])

                wait(dve, n_turned, 5 * i)
                dve.wait_ge(n_scored, 5 * i + 1)
                for a in range(2):
                    s = slopes[:, bass.ds(i + 4 * a, 1)]
                    then(v.scalar_tensor_tensor(out=n_scc[:, a].rearrange("p t c -> p (t c)"), in0=dist_c.rearrange("p t c -> p (t c)"), scalar=s,
                                                in1=bank(a)[:, 0:TT * CPAD], op0=ALU.mult, op1=ALU.add))
                then(v.tensor_reduce(c_mx, n_scc, AX.X, ALU.max))
                v.tensor_tensor(n_scc, n_scc, c_mx.unsqueeze(3).to_broadcast([P, 2, TT, CPAD]), ALU.subtract).then_inc(c_shift, 1)
                for u in range(4):
                    br, a = u // 2, u % 2
                    dve.wait_ge(n_scored, 5 * i + u + 2)
                    then(v.scalar_tensor_tensor(out=n_sc[u].rearrange("p t s -> p (t s)"), in0=dist.rearrange("p t s -> p (t s)"),
                                                scalar=slopes[:, bass.ds(i + 4 * a, 1)], in1=bank(4 + u), op0=ALU.mult, op1=ALU.add))
                    then(v.tensor_reduce(n_mx[:, u, :], n_sc[u], AX.X, ALU.max))
                    v.tensor_scalar(n_mx[:, u, :], n_mx[:, u, :], -1.0, None, ALU.mult).then_inc(n_max, 1)
                dve.wait_ge(c_exp, i + 1)
                then(v.tensor_reduce(c_sum, n_scc, AX.X, ALU.add))
                then(v.reciprocal(c_sum, c_sum))
                for a in range(2):
                    gate = n_gate[:, :, bass.ds(3 * (i + 4 * a), 1)].rearrange("p t o -> p (t o)")
                    then(v.tensor_tensor(c_sum[:, a, :], c_sum[:, a, :], gate, ALU.mult))
                    then(v.tensor_tensor(n_scc[:, a], n_scc[:, a], valid_c, ALU.mult))
                v.tensor_tensor(n_scc, n_scc, c_sum.unsqueeze(3).to_broadcast([P, 2, TT, CPAD]), ALU.mult).then_inc(c_scaled, 1)
                for u in range(4):
                    br, a = u // 2, u % 2
                    dve.wait_ge(n_exp, 8 * i + 2 * u + 2)
                    then(v.reciprocal(n_coef[:, u, :], n_sum[:, u, :]))
                    gate = n_gate[:, :, bass.ds(3 * (i + 4 * a) + 1 + br, 1)].rearrange("p t o -> p (t o)")
                    then(v.tensor_tensor(n_coef[:, u, :], n_coef[:, u, :], gate, ALU.mult))
                    for t in range(TT):
                        v.tensor_scalar(n_sc[u][:, t, :], n_sc[u][:, t, :], n_coef[:, u, t:t + 1], None, ALU.mult).then_inc(n_scaled, 1)
                assert done[0] == 25, done
                dve.wait_ge(o_hi, PAIRS + i + 1)
                v.tensor_tensor(ol[:, 1, bass.ds(i, 1), :], bank(2)[:, 0:T].rearrange("p (a t) -> p a t", a=1),
                                oh[:, 1, bass.ds(i, 1), :].bitcast(F32), ALU.subtract).then_inc(o_lo, 1)

            peeled(dve, PAIRS, nsa_pair)

            h0 = FIRST["hg"]
            flat = lambda w, j: w[:, 2 * j:2 * j + 2, :].rearrange("p a t -> p (a t)")
            for j in range(2):
                split(h0 + j + 2)
                dve.wait_ge(evacuated, EVAC[h0 + j + 1])
                v.tensor_tensor(flat(hg_q, j), flat(hg_q, j), hg_t.rearrange("p a t -> p (a t)"), ALU.mult).then_inc(h_silu, 1)
            for j in range(4):
                split(h0 + j + 4)
            dve.wait_ge(evacuated, EVAC[h0 + 4])
            v.tensor_scalar(hg_k, hg_f, -1.0, 1.0, ALU.mult, ALU.add).then_inc(h_silu, 1)
            dve.wait_ge(spread_loaded, 16)
            for j in range(2):
                split(h0 + j + 8)
                dve.wait_ge(evacuated, EVAC[h0 + 7 + j])
                gv = hg_g[:, :, j * PC:(j + 1) * PC]
                link(v.tensor_tensor(gv, gv, hg_t, ALU.mult))
                v.tensor_tensor(gv, gv, gb[:, j * PC:(j + 1) * PC].unsqueeze(1).to_broadcast([P, TT, PC]), ALU.mult).then_inc(h_silu, 1)
            dve.wait_ge(h_zero, 3)
            dve.wait_ge(h_silu, 5)
            v.tensor_copy(minus_one[:, :], minus_one[:, :]).then_inc(gain_used, 1)

            def hg_head(i):
                c = 14 * i
                done = [0]

                def then(ins, n=1):
                    ins.then_inc(h_chain, 1)
                    done[0] += 1

                def sync():
                    dve.wait_ge(h_chain, c + done[0])

                one = lambda w: w[:, bass.ds(i, 1), :].rearrange("p a t -> p (a t)")
                q, f, k, s = one(hg_q), one(hg_f), one(hg_k), one(hg_s)
                wait(dve, h_scored, i)
                v.tensor_copy(q_lev[:, 0, :], q).then_inc(h_lev, 1)
                v.tensor_copy(k_lev[:, 0, :], k).then_inc(h_lev, 1)
                for l in range(1, LEVELS + 1):
                    h = 2 ** (l - 1)
                    half = lambda w, r: w.rearrange("p (b r h) -> p b r h", r=2, h=h)[:, :, r, :]
                    if l < LEVELS:
                        qo, ko = half(q_lev[:, l, :], 1), half(k_lev[:, l, :], 0)
                    else:
                        qo, ko = q_x.unsqueeze(1), k_x.unsqueeze(1)
                    v.tensor_tensor(qo, half(q, 1), half(f, 1), ALU.mult).then_inc(h_lev, 1)
                    v.tensor_tensor(ko, half(k, 0), half(s, 0), ALU.mult).then_inc(h_lev, 1)
                    if l == LEVELS:
                        break
                    n = T // (2 * h)
                    left = half(f, 0)[:, :, h - 1:h].to_broadcast([P, n, h])
                    right = half(f, 1)[:, :, h - 1:h].to_broadcast([P, n, h])
                    dve.wait_ge(h_lev, 18 * i + 2 * l + 2)
                    then(v.tensor_tensor(half(s, 0), half(s, 0), right, ALU.mult))
                    sync()
                    then(v.tensor_tensor(half(f, 1), half(f, 1), left, ALU.mult))
                    sync()
                for t in range(TT):
                    dve.wait_ge(h_scored, i + 1)
                    wait(dve, h_out, i)
                    v.tensor_tensor(a_m[t], ACC[:, 2 * t:2 * t + 2, :].rearrange("p b (l t) -> p (b l) t", t=P), level_mask, ALU.mult).then_inc(h_masked, 1)

            peeled(dve, HG_HEADS, hg_head)
            k = NIDX["hg"]
            heads = lambda w: w.rearrange("p t (h d) -> p (t h) d", d=P)
            dve.wait_ge(h_o_ready, HG_HEADS)
            dve.wait_ge(h_out, HG_HEADS)
            sq = xn[:, 0, :].rearrange("p (a d) -> p a d", d=P)
            link(v.tensor_tensor(sq, heads(hg_o), heads(hg_o), ALU.mult))
            v.tensor_reduce(ss[:, k, 0:8], sq, AX.X, ALU.add).then_inc(sumsq, 2)
            dve.wait_ge(rstd_ready, k + 1)
            link(v.tensor_tensor(heads(hg_o), heads(hg_o), rstd[:, k, 0:8].unsqueeze(2).to_broadcast([P, 8, P]), ALU.mult))
            v.tensor_tensor(hg_o, hg_o, hg_g, ALU.mult).then_inc(rows_ready, 2)
            turn("hg", oh[:, 2, :, :], ol[:, 2, :, :], None)

            dve.wait_ge(m_zero, 1)

            def merge(b):
                for half in range(2):
                    p = FIRST["merge"] + 3 * half
                    split(p + 2, 6, b)
                    split(p + 3, 6, b)
                    split(p + 4, 6, b)
                    u = 2 * b + half
                    dve.wait_ge(panel_used, p + 6 * b + 3)
                    wait(dve, m_added, u - 1)
                    v.tensor_tensor(m_tmp[half].rearrange("p (b f) t -> p b (f t)", b=2), gm[half].rearrange("p (b f) t -> p b (f t)", b=2),
                                    ACC[:, 2 * half:2 * half + 2, :], ALU.mult).then_inc(m_mul, 1)
                    dve.wait_ge(m_mul, u + 1)
                    v.tensor_tensor(m_t[:, 4 * half:4 * half + 4, :], m_t[:, 4 * half:4 * half + 4, :], m_tmp[half], ALU.add).then_inc(m_added, 1)

            peeled(dve, 3, merge)

            for half in range(2):
                f = slice(4 * half, 4 * half + 4)
                dve.wait_ge(m_hi, half + 1)
                v.tensor_tensor(xl[:, f, :], m_t[:, f, :], xh[:, f, :].bitcast(F32), ALU.subtract).then_inc(m_lo, 1)
            for j in range(4):
                p = FIRST["w_out"] + j
                split(p + 2)
                dve.wait_ge(panel_used, p + 1)
                xc = x[:, :, j * PC:(j + 1) * PC]
                v.tensor_tensor(xc, xc, bank(BANK[p]).rearrange("p (t n) -> p t n", t=TT), ALU.add).then_inc(evacuated, 1)

            dve.wait_ge(evacuated, EVAC[FIRST["peer_q"]])
            norm_rows("peer")
            turn("peer", xh, xl, "peer")
            dve.wait_ge(turned, XEND["peer"])
            dve.wait_ge(spread_loaded, 16 * 2)
            dve.wait_ge(rows_ready, 6)
            link(v.tensor_tensor(xn[:, :, :], xn[:, :, :], gb[:, :].unsqueeze(1).to_broadcast([P, TT, D]), ALU.mult))
            v.tensor_copy(minus_one[:, :], minus_one[:, :]).then_inc(gain_used, 1)
            p0 = FIRST["peer_q"]
            for j in range(4):
                split(p0 + j + 2)

            def best(n, t, h):
                c = 44 * n
                done = [0]

                def then(ins):
                    done[0] += 1
                    ins.then_inc(pe_chain, 1)

                def sync():
                    dve.wait_ge(pe_chain, c + done[0])
                    then(v.tensor_copy(pe_carrier, minus_half[:, 0:1]))

                def top16(src, vals, idx):
                    for a in range(len(src)):
                        then(v.max(vals[a][:, 0:8], src[a]))
                    sync()
                    for a in range(len(src)):
                        then(v.max_index(idx[a][:, 0:8], vals[a][:, 0:8], src[a]))
                    sync()
                    for a in range(len(src)):
                        then(v.match_replace(src[a], vals[a][:, 0:8], src[a], -3e38))
                    sync()
                    for a in range(len(src)):
                        then(v.max(vals[a][:, 8:16], src[a]))
                    sync()
                    for a in range(len(src)):
                        then(v.max_index(idx[a][:, 8:16], vals[a][:, 8:16], src[a]))
                    sync()

                wait(dve, exp_done, n)
                then(v.tensor_copy(pe_s, pe_sc[:, 2 * t:2 * t + 2, bass.ds(h, 1), :].rearrange("p a h k -> p a (h k)")))
                sync()
                top16([pe_s[:, a, :] for a in range(2)], [pe_tv[:, a, :] for a in range(2)], [pe_ti[:, a, :] for a in range(2)])
                then(v.tensor_copy(pe_tif, pe_ti))
                then(v.tensor_tensor(pe_cand, pe_tv[:, 0, :].unsqueeze(2).to_broadcast([P, PE_K, PE_K]),
                                     pe_tv[:, 1, :].unsqueeze(1).to_broadcast([P, PE_K, PE_K]), ALU.add))
                sync()
                top16([pe_cand.rearrange("p i j -> p (i j)")], [pe_best], [pe_pos])
                v.tensor_scalar(pe_nb, pe_best[:, 0:1], -1.0, None, ALU.mult).then_inc(best_ready, 1)
                then(v.tensor_scalar(pe_hl[:, 0, :], pe_pos, 4, None, ALU.logical_shift_right))
                then(v.tensor_scalar(pe_hl[:, 1, :], pe_pos, 15, None, ALU.bitwise_and))
                sync()
                then(v.tensor_copy(pe_hlf, pe_hl))
                sync()
                for a in range(2):
                    then(v.tensor_tensor(pe_hot[a], iota16[:, :].unsqueeze(1).to_broadcast([P, PE_K, PE_K]),
                                         pe_hlf[:, a, :].unsqueeze(2).to_broadcast([P, PE_K, PE_K]), ALU.is_equal))
                sync()
                for a in range(2):
                    then(v.tensor_tensor(pe_hot[a], pe_hot[a], pe_tif[:, a, :].unsqueeze(1).to_broadcast([P, PE_K, PE_K]), ALU.mult))
                sync()
                for a in range(2):
                    then(v.tensor_reduce(pe_e[:, a, :], pe_hot[a], AX.X, ALU.add))
                sync()
                v.scalar_tensor_tensor(out=pe_idx[:, bass.ds(n * PE_K, PE_K)], in0=pe_e[:, 0, :], scalar=float(PE_KEYS), in1=pe_e[:, 1, :],
                                       op0=ALU.mult, op1=ALU.add).then_inc(idx_ready, 1)
                assert done[0] == 44, done

            def dots(n, t, turn_):
                for k in range(PE_K):
                    slot = k % RING
                    dve.wait_ge(rows_landed[slot], 16 * (2 * turn_ + k // RING + 1))
                    v.scalar_tensor_tensor(out=ring[slot], in0=ring[slot], scalar=1.0, in1=xn[:, t, :], op0=ALU.mult, op1=ALU.mult,
                                           accum_out=pe_h[:, k:k + 1]).then_inc(rows_used, 1)

            def weights(n):
                dve.wait_ge(exp_done, n + 1)
                v.reciprocal(pe_rec, pe_sum[:, bass.ds(n, 1)]).then_inc(pe_chain2, 1)
                dve.wait_ge(pe_chain2, 2 * n + 1)
                v.tensor_scalar(pe_gate, pe_exp[:, bass.ds(n * PE_K, PE_K)], pe_rec, None, ALU.mult).then_inc(pe_chain2, 1)
                dve.wait_ge(pe_chain2, 2 * n + 2)
                dve.wait_ge(gelu_done, n + 1)
                v.tensor_tensor(pe_act[:, bass.ds(n * PE_K, PE_K)], pe_gate, pe_gelu, ALU.mult).then_inc(act_ready, 1)

            def sums(n, t, turn_):
                dve.wait_ge(act_ready, n + 1)
                for k in range(PE_K):
                    slot = k % RING
                    dve.wait_ge(rows_landed[slot], 16 * (2 * turn_ + k // RING + 1))
                    dve.wait_ge(rows_used, PE_K * turn_ + k)
                    v.scalar_tensor_tensor(out=pe_acc[:, t, :], in0=ring[slot], scalar=pe_act[:, bass.ds(n * PE_K + k, 1)], in1=pe_acc[:, t, :],
                                           op0=ALU.mult, op1=ALU.add).then_inc(rows_used, 1)

            dve.wait_ge(pe_sc_ready, 2)
            best(0, 0, 0)
            dve.wait_ge(acc_zero, 1)
            dots(0, 0, 0)
            best(1, 0, 1)
            weights(0)
            with dve.Fori(1, PE_HEADS - 1) as n:
                dots(n, 0, 2 * n - 1)
                best(n + 1, 0, n + 1)
                weights(n)
                sums(n - 1, 0, 2 * n)
            dve.wait_ge(pe_sc_ready, 4)
            n = PE_HEADS - 1
            dots(n, 0, 2 * n - 1)
            best(n + 1, 1, 0)
            weights(n)
            sums(n - 1, 0, 2 * n)
            n = PE_HEADS
            dots(n, 1, 2 * n - 1)
            best(n + 1, 1, 1)
            weights(n)
            sums(n - 1, 0, 2 * n)
            with dve.Fori(PE_HEADS + 1, UNITS - 1) as n:
                dots(n, 1, 2 * n - 1)
                best(n + 1, 1, n + 1 - PE_HEADS)
                weights(n)
                sums(n - 1, 1, 2 * n)
            n = UNITS - 1
            dots(n, 1, 2 * n - 1)
            weights(n)
            sums(n - 1, 1, 2 * n)
            sums(n, 1, 2 * n + 1)
            dve.wait_ge(rows_used, 2 * PE_K * UNITS)
            for t in range(TT):
                v.tensor_tensor(x[:, t, :], x[:, t, :], pe_acc[:, t, :], ALU.add).then_inc(x_updated, 1)
            dve.wait_ge(x_updated, X_AT["peer"])
            sum_squares("final")
            dve.wait_ge(rstd_ready, NIDX["final"] + 1)
            dve.wait_ge(spread_loaded, 16 * 3)
            for t in range(TT):
                v.scalar_tensor_tensor(out=x[:, t, :], in0=x[:, t, :], scalar=rstd[:, NIDX["final"], t:t + 1], in1=gb[:, :],
                                       op0=ALU.mult, op1=ALU.mult).then_inc(x_updated, 1)
            dve.wait_ge(x_updated, X_AT["final"])
            v.tensor_copy(minus_one[:, :], minus_one[:, :]).then_inc(gain_used, 1)

            def ffn(f):
                p0 = FIRST[f"ffn{f}"]
                last = p0 + 3 * FF_STEPS - 1

                def product(p, i, m=0, r=0):
                    dve.wait_ge(evacuated, along(EVAC, p, m, r))
                    dve.wait_ge(panel_used, p + m * r + 1)
                    wait(dve, ff_lo, FF_STEPS * f + i)
                    v.tensor_tensor(ff_a.rearrange("p f t -> p (f t)"), ff_s.rearrange("p f t -> p (f t)"), bank(BANK[p]), ALU.mult)\
                        .then_inc(evacuated, 1)

                def rest(i):
                    dve.wait_ge(ff_hi, FF_STEPS * f + i + 1)
                    v.tensor_tensor(al[:, :, :], ff_a, ah[:, :, :].bitcast(F32), ALU.subtract).then_inc(ff_lo, 1)

                split(p0 + 2)
                split(p0 + 3)
                product(p0 + 1, 0)
                rest(0)

                def step(i, next_up=True):
                    split(p0 + 4, 3, i - 1)
                    split(p0 + 5, 3, i - 1)
                    product(p0 + 3, i, 3, i - 1)
                    if next_up:
                        split(p0 + 6, 3, i - 1)
                    rest(i)

                with dve.Fori(1, FF_STEPS - 1) as i:
                    step(i)
                step(FF_STEPS - 1, last + 1 < NP)
                if last + 2 < NP:
                    split(last + 2)

            def post(name):
                k = NIDX[name]
                dve.wait_ge(rstd_ready, k + 1)
                dve.wait_ge(spread_loaded, 16 * (SPREAD.index(name) + 1))
                for t in range(TT):
                    out = ACC[:, 2 * t:2 * t + 2, :].rearrange("p b n -> p (b n)")
                    link(v.scalar_tensor_tensor(out=xn[:, t, :], in0=out, scalar=rstd[:, k, t:t + 1], in1=gb[:, :], op0=ALU.mult, op1=ALU.mult))
                for t in range(TT):
                    v.tensor_tensor(x[:, t, :], x[:, t, :], xn[:, t, :], ALU.add).then_inc(x_updated, 1)
                v.tensor_copy(minus_one[:, :], minus_one[:, :]).then_inc(gain_used, 1)

            def normed(name, x_at):
                dve.wait_ge(x_updated, x_at)
                norm_rows(name)
                turn(name, xh, xl, name)

            normed("f0", X_AT["final"])
            ffn(0)
            post("p0")
            normed("conv", X_AT["p0"])
            p0 = FIRST["conv_in"]
            dve.wait_ge(cv_pad, 1)

            def conv(j):
                c = 5 * j
                done = [0]

                def then(ins, n=1):
                    done[0] += n
                    ins.then_inc(cv_chain, n)
                    dve.wait_ge(cv_chain, c + done[0])

                for w in range(3):
                    split(p0 + w + 2, 3, j)
                dve.wait_ge(evacuated, along(EVAC, p0 + 2, 3, j))
                dve.wait_ge(panel_used, p0 + 3 * j + 3)
                v.tensor_tensor(cv_u[:, :, CONV_W - 1:], cv_c, bank(BANK[p0 + 2]).rearrange("p (f t) -> p f t", f=2), ALU.mult).then_inc(evacuated, 1)
                dve.wait_ge(evacuated, along(EVAC, p0 + 3, 3, j))
                wait(dve, cv_lo, j)
                tap = lambda w, f: cols[:, bass.ds(2 * j + (TAPS + w * KD + f), 1)]
                for f in range(2):
                    v.tensor_scalar(cv_z[:, f, :], cv_u[:, f, 2:2 + T], tap(2, f), None, ALU.mult)
                then(v.tensor_copy(minus_one[:, :], minus_one[:, :]))
                for w in (1, 0):
                    for f in range(2):
                        then(v.scalar_tensor_tensor(out=cv_z[:, f, :], in0=cv_u[:, f, w:w + T], scalar=tap(w, f), in1=cv_z[:, f, :],
                                                    op0=ALU.mult, op1=ALU.add))
                v.tensor_tensor(cv_z, cv_z, cv_b, ALU.mult).then_inc(cv_y, 1)
                dve.wait_ge(cv_hi, j + 1)
                v.tensor_tensor(yl[:, bass.ds(2 * j, 2), :], cv_z, yh[:, bass.ds(2 * j, 2), :].bitcast(F32), ALU.subtract).then_inc(cv_lo, 1)
                assert done[0] == 5

            peeled(dve, 4, conv)
            for j in range(4):
                split(FIRST["conv_out"] + j + 2)
            post("pc")
            normed("f1", X_AT["pc"])
            ffn(1)
            post("p1")
            normed("kv", X_AT["p1"])
            for j in range(8):
                split(FIRST["kv"] + j + 2)
            normed("f2", X_AT["p1"])
            ffn(2)
            post("p2")
            normed("attn", X_AT["p2"])
            for j in range(4):
                split(FIRST["q"] + j + 2)
            dve.wait_ge(lam_loaded, 64)
            for a in range(2):
                v.scalar_tensor_tensor(out=lam_in[:, 2 * a, :], in0=lam_in[:, 2 * a, :], scalar=1.0, in1=lam_in[:, 2 * a + 1, :], op0=ALU.mult,
                                       op1=ALU.mult, accum_out=lam_dot[:, a:a + 1]).then_inc(lam_dots, 1)
            dve.wait_ge(lam_exped, 1)
            link(v.tensor_tensor(lam, lam_exp[:, 1:2], lam_exp[:, 0:1], ALU.subtract))
            link(v.tensor_scalar(lam, lam, -LAMBDA_INIT, None, ALU.add))

            def diff_heads(i):
                c = 14 * i
                done = [0]

                def then(ins):
                    done[0] += 1
                    ins.then_inc(df_chain, 1)
                    dve.wait_ge(df_chain, c + done[0])

                wait(dve, df_turned, 2 * i)
                for u in range(4):
                    dve.wait_ge(df_scored, 4 * i + u + 1)
                    flat = df_sc[u].rearrange("p t s -> p (t s)")
                    then(v.tensor_tensor(flat, bank(4 + u), causal[:, :, :].rearrange("p t s -> p (t s)"), ALU.add))
                    then(v.tensor_reduce(df_mx[:, u, :], df_sc[u], AX.X, ALU.max))
                    v.tensor_scalar(df_mx[:, u, :], df_mx[:, u, :], -1.0, None, ALU.mult).then_inc(df_max, 1)
                for h in range(2):
                    a, b = 2 * h, 2 * h + 1
                    dve.wait_ge(df_exp, 8 * i + 4 * h + 4)
                    then(v.reciprocal(df_r[:, a:b + 1, :], df_sum[:, a:b + 1, :]))
                    then(v.tensor_scalar(df_r[:, b, :], df_r[:, b, :], lam, None, ALU.mult))
                    v.tensor_scalar(df_sc[a][:, 0, :], df_sc[a][:, 0, :], df_r[:, a, 0:1], None, ALU.mult)
                    then(v.tensor_scalar(df_sc[a][:, 1, :], df_sc[a][:, 1, :], df_r[:, a, 1:2], None, ALU.mult))
                    for t in range(TT):
                        v.scalar_tensor_tensor(out=df_sc[a][:, t, :], in0=df_sc[b][:, t, :], scalar=df_r[:, b, t:t + 1], in1=df_sc[a][:, t, :],
                                               op0=ALU.mult, op1=ALU.add).then_inc(df_mixed, 1)
                assert done[0] == 14, done

            peeled(dve, DIFF_HEADS // 2, diff_heads)
            k = NIDX["diff"]
            heads = lambda w: w.rearrange("p t (h e) -> p (t h) e", e=P)
            dve.wait_ge(df_o_ready, DIFF_HEADS)
            link(v.tensor_tensor(xn[:, :, :], df_o, df_o, ALU.mult))
            v.tensor_reduce(ss[:, k, :], heads(xn[:, :, :]), AX.X, ALU.add).then_inc(sumsq, 2)
            dve.wait_ge(rstd_ready, k + 1)
            dve.wait_ge(spread_loaded, 16 * (SPREAD.index("diff") + 1))
            link(v.tensor_tensor(heads(df_o), heads(df_o), rstd[:, k, :].unsqueeze(2).to_broadcast([P, 16, P]), ALU.mult))
            v.tensor_tensor(heads(df_o), heads(df_o), gb[:, 0:P].unsqueeze(1).to_broadcast([P, 16, P]), ALU.mult).then_inc(rows_ready, 2)
            v.tensor_copy(minus_one[:, :], minus_one[:, :]).then_inc(gain_used, 1)
            turn("diff", xh, xl, None)
            for j in range(4):
                split(FIRST["o"] + j + 2)
            post("pa")
            normed("f3", X_AT["pa"])
            ffn(3)
            post("p3")

        @block.tensor
        def _(pe):
            def mm(out, l, r, first, last):
                return nc.tensor.matmul(out, l, r, start=first, stop=last)

            def begin(p, m=0, i=0):
                pe.wait_ge(lo_done, p + m * i + 1)
                if BANK[p] is not None:
                    wait(pe, evacuated, along(EVAC, p, m, i) - 1)

            def exact3(out, lh, ll, rh, rl, first, last):
                mm(out, lh, rh, first, False)
                mm(out, lh, rl, False, False)
                return mm(out, ll, rh, False, last)

            def views(p, kt):
                s = p % SLOTS
                return [w[s][:, :WORDS[p]].rearrange("p (k n) -> p k n", k=kt) for w in (hi, lo)]

            def feature_tile(p, f, out, kt=KD, rh=xh, rl=xl):
                wh, wl = views(p, kt)
                c = slice(f * P, (f + 1) * P)
                for k in range(kt):
                    last = exact3(out, wh[:, k, c], wl[:, k, c], rh[:, k, :], rl[:, k, :], k == 0, k == kt - 1)
                return last

            def token_tile(p, t, out, c=slice(0, PC), lh=xh, ll=xl):
                wh, wl = views(p, KD)
                r = slice(t * P, (t + 1) * P)
                for k in range(KD):
                    last = exact3(out, lh[:, k, r], ll[:, k, r], wh[:, k, c], wl[:, k, c], k == 0, k == KD - 1)
                return last

            def panel_a(p, m=0, i=0):
                begin(p, m, i)
                for f in range(2):
                    last = feature_tile(p, f, bank(BANK[p])[:, f * T:(f + 1) * T])
                last.then_inc(panel_used, 1)

            def panel_b(p, m=0, i=0, n=PC):
                begin(p, m, i)
                for t in range(TT):
                    last = token_tile(p, t, bank(BANK[p])[:, t * n:(t + 1) * n], slice(0, n))
                last.then_inc(panel_used, 1)

            def turn(name, rows):
                pe.wait_ge(rows_ready, 2 * ([n for n, _ in XPOSE].index(name) + 1))
                if XBASE[name]:
                    pe.wait_ge(turned_lo, 2 * XBASE[name])
                for b in range(XEND[name] - XBASE[name]):
                    for j in range(2):
                        for t in range(TT):
                            c = (2 * b + j) * P
                            last = nc.tensor.transpose(ACC[:, b, j * T + t * P:j * T + (t + 1) * P], rows[:, t, c:c + P], ident[:, :])
                    last.then_inc(turned, 1)

            pe.wait_ge(tables, 2)
            pe.wait_ge(cols_loaded, 16 * 14)
            nc.tensor.transpose(bank(3)[:, 0:96], rowbuf[0:96, 0, :], ident[0:96, 0:96])
            nc.tensor.transpose(bank(3)[:, 96:128], rowbuf[0:CMP_LEN, 1, :], ident[0:CMP_LEN, 0:CMP_LEN])
            nc.tensor.transpose(bank(3)[:, 128:256], rowbuf[:, 2, :], ident[:, :]).then_inc(cols_turned, 1)
            turn("mix", xn)
            pe.wait_ge(turned_lo, 2 * XEND["mix"])
            for p in range(4):
                panel_a(p)
            for p in range(4, 6):
                panel_b(p)

            pe.wait_ge(tables, SB_TABLES)

            def sb_pair(i):
                pe.wait_ge(sb_staged, 3 * i + 2)
                for a in range(2):
                    r = slice(a * HD, (a + 1) * HD)
                    wait(pe, sb_sig, 4 * i + 2 * a - 2)
                    for t in range(TT):
                        out = bank(4 + a)[:, t * T:(t + 1) * T]
                        mm(out, q_st[r, t * P:(t + 1) * P], k_st[r, :], True, False)
                        last = mm(out, ident[:, :], strict[:, t, :], False, True)
                    last.then_inc(sb_scored, 1)
                for a in range(2):
                    pe.wait_ge(sb_attn, 2 * i + a + 1)
                    wait(pe, sb_pt_ready, 2 * i + a - 1)
                    for n, (t, s) in enumerate(((0, 0), (1, 0), (1, 1))):
                        last = nc.tensor.transpose(bank(6 + a)[:, n * P:(n + 1) * P], sb_a[a][:, t, s * P:(s + 1) * P], ident[:, :])
                    last.then_inc(sb_turned, 1)
                pe.wait_ge(sb_staged, 3 * i + 3)
                wait(pe, o_lo, i)
                for a in range(2):
                    r = slice(a * HD, (a + 1) * HD)
                    pe.wait_ge(sb_pt_ready, 2 * i + a + 1)
                    mm(bank(3)[r, 0:P], v_st[:, 0, r], sb_pt[a][:, 0, :], True, True)
                    mm(bank(3)[r, P:T], v_st[:, 0, r], sb_pt[a][:, 1, :], True, False)
                    mm(bank(3)[r, P:T], v_st[:, 1, r], sb_pt[a][:, 2, :], False, True).then_inc(sb_out, 1)

            peeled(pe, PAIRS, sb_pair)

            q0, c0, g0 = FIRST["nsa_q"], FIRST["nsa_kv"], FIRST["nsa_gate"]
            for j in range(2):
                panel_a(q0 + j)
            panel_a(c0)
            for j in range(2):
                p = c0 + 1 + j
                begin(p)
                b = bank(BANK[p])
                feature_tile(p, 0, b[:, 0:T])
                for t in range(TT):
                    last = token_tile(p, t, b[:, T + t * P:T + (t + 1) * P], slice(P, 2 * P))
                last.then_inc(panel_used, 1)
            panel_b(g0, n=N_GATES)
            pe.wait_ge(n_blk, 4)
            pe.wait_ge(wcmp_loaded, 64)
            pe.wait_ge(o_lo, PAIRS)
            for g in range(2):
                r = slice(g * HD, (g + 1) * HD)
                for l in range(CMP_LEN):
                    mm(bank(2)[r, 0:N_CMP], wcmp_k[r, l, :], cmp_blk[r, 0, l, :], l == 0, l == CMP_LEN - 1)
                for l in range(CMP_LEN):
                    last = mm(bank(3 + g)[0:N_CMP, 0:HD], cmp_blk[r, 1, l, :], wcmp_v[r, l, :], l == 0, l == CMP_LEN - 1)
            last.then_inc(n_kc, 1)
            pe.wait_ge(n_kc_ready, 3)
            pe.wait_ge(evacuated, EVAC[FIRST["hg"]])

            def nsa_pair(i):
                pe.wait_ge(n_staged, i + 1)
                wait(pe, n_pt_ready, 5 * i)
                for a in range(2):
                    r = slice(a * HD, (a + 1) * HD)
                    for t in range(TT):
                        last = mm(bank(a)[:, t * CPAD:(t + 1) * CPAD], nq_st[r, t * P:(t + 1) * P], kc[r, 0:CPAD], True, True)
                last.then_inc(n_scored, 1)
                for u in range(4):
                    a, key = u % 2, (n_ksel, n_kwin)[u // 2]
                    r = slice(a * HD, (a + 1) * HD)
                    for t in range(TT):
                        last = mm(bank(4 + u)[:, t * T:(t + 1) * T], nq_st[r, t * P:(t + 1) * P], key[r, :], True, True)
                    last.then_inc(n_scored, 1)
                for u in range(4):
                    pe.wait_ge(n_scaled, 8 * i + 2 * u + 2)
                    for n, (t, s) in enumerate(((0, 0), (1, 0), (1, 1))):
                        last = nc.tensor.transpose(bank(4 + u)[:, n * P:(n + 1) * P], n_sc[u][:, t, s * P:(s + 1) * P], ident[:, :])
                    last.then_inc(n_turned, 1)
                pe.wait_ge(c_scaled, i + 1)
                for a in range(2):
                    for t in range(TT):
                        c = (a * TT + t) * P
                        last = nc.tensor.transpose(bank(3)[0:CPAD, c:c + P], n_scc[:, a, t, :], ident[:, :])
                last.then_inc(n_turned, 1)
                pe.wait_ge(n_pt_ready, 5 * i + 5)
                wait(pe, o_lo, PAIRS + i)
                for a in range(2):
                    r = slice(a * HD, (a + 1) * HD)
                    for t in range(TT):
                        out = bank(2)[r, t * P:(t + 1) * P]
                        mm(out, vc[0:CPAD, a, :], n_ptc[0:CPAD, a, t, :], True, False)
                        for br, val in enumerate((n_vsel, n_vwin)):
                            pt = n_pt[2 * br + a]
                            for s in range(t + 1):
                                last = mm(out, val[:, s, r], pt[:, t + s, :], False, br == 1 and s == t)
                    last.then_inc(n_out, 1)

            peeled(pe, PAIRS, nsa_pair)

            h0 = FIRST["hg"]
            for j in range(4):
                panel_a(h0 + j)
            for j in range(4, 8):
                panel_b(h0 + j)

            def hg_head(i):
                pe.wait_ge(h_lev, 18 * i + 18)
                wait(pe, h_masked, 2 * i)
                wait(pe, h_cross, i)
                if isinstance(i, int):
                    pe.wait_ge(evacuated, EVAC[FIRST["merge"]])
                    pe.wait_ge(o_lo, 2 * PAIRS)
                for t in range(TT):
                    for l in range(LEVELS):
                        c = slice(t * P, (t + 1) * P)
                        mm(ACC[:, 2 * t + l // 4, (l % 4) * P:(l % 4 + 1) * P], k_lev[:, l, c], q_lev[:, l, c], True, True)
                mm(bank(3)[:, 0:P], k_x, q_x, True, True).then_inc(h_scored, 1)
                wait(pe, h_o_ready, i)
                for t in range(TT):
                    pe.wait_ge(h_masked, 2 * i + t + 1)
                    out = bank(2)[:, t * P:(t + 1) * P]
                    for l in range(LEVELS):
                        last = mm(out, a_m[t][:, l, :], hg_i[:, t, bass.ds(i * P, P)], l == 0, l == LEVELS - 1 and t == 0)
                pe.wait_ge(h_cross, i + 1)
                mm(out, a_x, hg_i[:, 0, bass.ds(i * P, P)], False, True).then_inc(h_out, 1)

            peeled(pe, HG_HEADS, hg_head)
            turn("hg", hg_o)

            pe.wait_ge(turned_lo, 2 * XEND["hg"])

            def merge(b):
                for half in range(2):
                    p = FIRST["merge"] + 3 * half
                    for j in range(2):
                        panel_a(p + j, 6, b)
                    begin(p + 2, 6, b)
                    wait(pe, m_mul, 2 * b + half - 1)
                    rh = oh[:, bass.ds(b, 1)].rearrange("p a k t -> p (a k) t")
                    rl = ol[:, bass.ds(b, 1)].rearrange("p a k t -> p (a k) t")
                    for f in range(4):
                        last = feature_tile(p + 2, f, ACC[:, 2 * half + f // 2, (f % 2) * T:(f % 2 + 1) * T], PAIRS, rh, rl)
                    last.then_inc(panel_used, 1)

            peeled(pe, 3, merge)

            pe.wait_ge(m_lo, 2)
            for j in range(4):
                panel_b(FIRST["w_out"] + j)

            def normed(name, rows=xn):
                turn(name, rows)
                pe.wait_ge(turned_lo, 2 * XEND[name])

            normed("peer")
            for j in range(4):
                panel_a(FIRST["peer_q"] + j)
            pe.wait_ge(evacuated, EVAC[FIRST["ffn0"]])
            for t in range(TT):
                if t:
                    pe.wait_ge(pe_sc_ready, 2 * t)
                for h in range(PE_HEADS):
                    for a in range(2):
                        r = slice(a * HD, (a + 1) * HD)
                        last = mm(ACC[:, 2 * a + h // 4, (h % 4) * P:(h % 4 + 1) * P], pe_q[r, h, t * P:(t + 1) * P], cols[r, P:2 * P], True, True)
                last.then_inc(pe_scored, 1)

            def ffn(f):
                p0 = FIRST[f"ffn{f}"]

                def down(p, i, m=0, r=0, first=False, final=False):
                    begin(p, m, r)
                    pe.wait_ge(ff_lo, FF_STEPS * f + i + 1)
                    wh, wl = views(p, 2)
                    for t in range(TT):
                        for half in range(2):
                            for k in range(2):
                                c, w = slice(t * P, (t + 1) * P), slice(half * 512, (half + 1) * 512)
                                last = exact3(ACC[:, 2 * t + half, :], ah[:, k, c], al[:, k, c], wh[:, k, w], wl[:, k, w],
                                              first and k == 0, final and k == 1)
                    last.then_inc(panel_used, 1)

                panel_a(p0)
                panel_a(p0 + 1)
                panel_a(p0 + 2)
                panel_a(p0 + 3)
                down(p0 + 4, 0, first=True)
                with pe.Fori(2, FF_STEPS) as i:
                    panel_a(p0 + 2, 3, i - 1)
                    panel_a(p0 + 3, 3, i - 1)
                    down(p0 + 4, i - 1, 3, i - 1)
                down(p0 + 3 * FF_STEPS - 1, FF_STEPS - 1, final=True)

            def project(name, lh, ll):
                for j in range(4):
                    p = FIRST[name] + j
                    begin(p)
                    for t in range(TT):
                        last = token_tile(p, t, ACC[:, 2 * t + j // 2, (j % 2) * PC:(j % 2 + 1) * PC], lh=lh, ll=ll)
                    last.then_inc(panel_used, 1)

            normed("f0")
            ffn(0)
            normed("conv")

            def conv(j):
                for w in range(3):
                    panel_a(FIRST["conv_in"] + w, 3, j)

            peeled(pe, 4, conv)
            pe.wait_ge(cv_lo, 4)
            project("conv_out", yh, yl)
            normed("f1")
            ffn(1)
            normed("kv")
            for j in range(4):
                panel_a(FIRST["kv"] + j)
            for j in range(4, 8):
                panel_b(FIRST["kv"] + j)
            normed("f2")
            ffn(2)
            normed("attn")
            for j in range(4):
                panel_a(FIRST["q"] + j)

            def diff_heads(i):
                pe.wait_ge(df_staged, 2 * i + 2)
                for u in range(4):
                    h, r = u // 2, slice(u % 2 * HD, (u % 2 + 1) * HD)
                    wait(pe, df_pt_ready, 2 * i)
                    for t in range(TT):
                        last = mm(bank(4 + u)[:, t * T:(t + 1) * T], df_qs[r, h, t * P:(t + 1) * P], df_ks[r, h, :], True, True)
                    last.then_inc(df_scored, 1)
                for h in range(2):
                    pe.wait_ge(df_mixed, 4 * i + 2 * h + 2)
                    for n, (t, s) in enumerate(((0, 0), (1, 0), (1, 1))):
                        last = nc.tensor.transpose(bank(4 + 2 * h)[:, n * P:(n + 1) * P], df_sc[2 * h][:, t, s * P:(s + 1) * P], ident[:, :])
                    last.then_inc(df_turned, 1)
                for h in range(2):
                    pe.wait_ge(df_pt_ready, 2 * i + h + 1)
                    wait(pe, df_o_ready, 2 * i + h - 1)
                    val = lambda s: df_v[:, s, bass.ds(2 * i * P + h * P, P)]
                    mm(bank(2 + h)[:, 0:P], df_pt[h][:, 0, :], val(0), True, True)
                    mm(bank(2 + h)[:, P:2 * P], df_pt[h][:, 1, :], val(0), True, False)
                    mm(bank(2 + h)[:, P:2 * P], df_pt[h][:, 2, :], val(1), False, True).then_inc(df_out, 1)

            peeled(pe, DIFF_HEADS // 2, diff_heads)
            normed("diff", df_o)
            project("o", xh, xl)
            normed("f3")
            ffn(3)


def kernel(**inputs):
    import concourse.bacc as bacc
    from concourse.bass_utils import run_bass_kernel_spmd

    nc = bacc.Bacc("TRN2", target_bir_lowering=False, num_devices=1)
    arrays, io = {}, {}
    for name, a in inputs.items():
        a = np.ascontiguousarray(a)
        arrays[f"in_{name}"] = a
        io[name] = nc.dram_tensor(f"in_{name}", a.shape, mybir.dt.from_np(a.dtype), kind="ExternalInput").ap()
    io["out"] = nc.dram_tensor("out_0", (1, T, D), F32, kind="ExternalOutput").ap()
    build(nc, io)
    r = run_bass_kernel_spmd(nc, [arrays], core_ids=[0])
    return r.results[0]["out_0"]
```

```python
from contextlib import ExitStack

import concourse.bass as bass
import concourse.mybir as mybir
import numpy as np

F32, F32R = mybir.dt.float32, mybir.dt.float32r
U32 = mybir.dt.uint32
ALU = mybir.AluOpType
ACT = mybir.ActivationFunctionType
AX = mybir.AxisListType

P = 128
T, D = 256, 1024
TT = T // P
KD = D // P
HD = 64
EPS = 1e-6
NEG = -1e30
FAR = 1e32
SB_W = NSA_W = HG_W = 512
PAIRS = SB_W // P
CMP_LEN, CMP_STRIDE = 32, 16
N_CMP = T // CMP_STRIDE - 1
CPAD = N_CMP + 1
HG_HEADS = 4
LEVELS = 8
F_FF = 2816
FF_STEPS = F_FF // 256
CONV_W = 3
PANEL = 2048
PC = 256
SLOTS = 3
PE_HEADS, PE_K, PE_KEYS = 8, 16, 128
RING, GROUP = 8, 4
DIAGS = 8
LAMBDA_INIT = 0.8 - 0.6 * float(np.exp(-0.3))
DIFF_HEADS = 8

C_SBQ, C_SBK, C_SBV, C_NQ, C_CMP, C_SEL, C_WIN, C_NG = 0, 512, 1024, 1536, 2048, 2304, 2560, 2816
C_HQ, C_HF, C_HI, C_HG, C_MERGE = 2840, 3352, 3864, 4376, 4888
N_GATES = 24


def plan_panels():
    plan = []

    def add(name, count, pieces=1, words=PANEL, banks=(0, 1)):
        for j in range(count):
            b = banks[j % len(banks)] if banks else None
            plan.append((name, pieces, words, b))

    add("sb", 6)
    add("nsa_q", 2, pieces=4)
    add("nsa_kv", 3)
    add("nsa_gate", 1, words=KD * N_GATES, banks=(1,))
    add("hg", 8)
    for _ in range(3):
        for _ in range(2):
            add("merge", 2)
            add("branch", 1, pieces=2, banks=())
    add("w_out", 4)
    add("peer_q", 4)

    def ffn(name):
        for i in range(FF_STEPS):
            add(name, 2)
            if i:
                add(name, 1, banks=())
        add(name, 1, banks=())

    ffn("ffn0")
    add("conv_in", 12, banks=(0, 1, 2))
    add("conv_out", 4, banks=())
    ffn("ffn1")
    add("kv", 8)
    ffn("ffn2")
    add("q", 4)
    add("o", 4, banks=())
    ffn("ffn3")
    return plan


PLAN = plan_panels()
NP = len(PLAN)
FIRST = {}
for _p, _e in enumerate(PLAN):
    FIRST.setdefault(_e[0], _p)
BANK = [e[3] for e in PLAN]
WORDS = [e[2] for e in PLAN]
LANDED = [16 * sum(PLAN[q][1] for q in range(p % SLOTS, p + 1, SLOTS)) for p in range(NP)]
EVAC = [sum(b is not None for b in BANK[:p]) for p in range(NP + 1)]

XPOSE = [("mix", 4), ("hg", 2), ("peer", 4), ("f0", 4), ("conv", 4), ("f1", 4), ("kv", 4), ("attn", 4), ("diff", 4), ("f3", 4)]
XBASE = {n: sum(b for _, b in XPOSE[:k]) for k, (n, _) in enumerate(XPOSE)}
XEND = {n: XBASE[n] + b for n, b in XPOSE}
XIDX = {n: k for k, (n, _) in enumerate(XPOSE)}
_splits = [(n, 2 * b) for n, b in XPOSE]
_splits.insert(XIDX["kv"] + 1, ("f2", KD))
SBASE = {n: sum(b for _, b in _splits[:k]) for k, (n, _) in enumerate(_splits)}
SEND = {n: SBASE[n] + b for n, b in _splits}
GAIN = {n: 8 * k for k, n in enumerate(["mix", "peer", "f0", "conv", "f1", "f2", "attn", "f3", "kv"])}
TAPS = 72
NORMS = [("mix", 2, 1 / D, 1.0), ("hg", 8, 1 / 128, 1.0), ("peer", 2, 1 / D, 1.0), ("final", 2, 1 / D, 1.0),
         ("f0", 2, 1 / D, 1.0), ("p0", 2, 1 / D, 0.5), ("conv", 2, 1 / D, 1.0), ("pc", 2, 1 / D, 1.0),
         ("f1", 2, 1 / D, 1.0), ("p1", 2, 1 / D, 0.5), ("kv", 2, 1 / D, 1.0),
         ("p2", 2, 1 / D, 0.5), ("attn", 2, 1 / D, 1.0), ("diff", 16, 1 / 128, 1.0 - LAMBDA_INIT),
         ("pa", 2, 1 / D, 1.0), ("f3", 2, 1 / D, 1.0), ("p3", 2, 1 / D, 0.5)]
NIDX = {n: k for k, (n, *_) in enumerate(NORMS)}
SPREAD = ["hg", "peer", "final", "p0", "pc", "p1", "p2", "diff", "pa", "p3"]
X_AT = {n: 2 * (k + 1) for k, n in enumerate(["peer", "final", "p0", "pc", "p1", "p2", "pa", "p3"])}
POSTS = [("p0", "conv"), ("pc", "f1"), ("p1", "kv"), ("p2", "attn"), ("pa", "f3"), ("p3", None)]
UNITS = TT * PE_HEADS


SB_TABLES, N_TABLES = 8, 37


def build(nc, io):
    ctx = ExitStack()
    with ctx:
        def sb(name, shape, dt=F32):
            return ctx.enter_context(nc.sbuf_tensor(name, shape, dt))

        def sem(name):
            return ctx.enter_context(nc.semaphore(name))

        raw = [sb(f"raw{s}", [P, PANEL]) for s in range(SLOTS)]
        hi = [sb(f"hi{s}", [P, PANEL], F32R) for s in range(SLOTS)]
        lo = [sb(f"lo{s}", [P, PANEL], F32R) for s in range(SLOTS)]
        x = sb("x", [P, TT, D])
        xn = sb("xn", [P, TT, D])
        xh = sb("xh", [P, KD, T], F32R)
        xl = sb("xl", [P, KD, T], F32R)
        oh = sb("oh", [P, 3, PAIRS, T], F32R)
        ol = sb("ol", [P, 3, PAIRS, T], F32R)
        ah = sb("ah", [P, 2, T], F32R)
        al = sb("al", [P, 2, T], F32R)
        ident = sb("ident", [P, P])
        cols = sb("cols", [P, 256])
        rowbuf = sb("rowbuf", [P, 3, P])
        gb = sb("gb", [P, D])
        minus_half = sb("minus_half", [P, 16])
        slopes = sb("slopes", [P, 8])
        ss = sb("ss", [P, len(NORMS), 16])
        rstd = sb("rstd", [P, len(NORMS), 16])
        iota16 = sb("iota16", [P, PE_K])
        ARENA = 16944
        arena = sb("arena", [P, ARENA])
        top = [0]

        def carve(*shape, at=None, dt=None):
            n = int(np.prod(shape))
            a = top[0] if at is None else at
            top[0] = a + n
            assert top[0] <= ARENA, (top[0], ARENA)
            v = arena[:, a:a + n]
            if dt is not None:
                v = v.bitcast(dt)
            if len(shape) == 2:
                v = v.rearrange("p (a b) -> p a b", a=shape[0])
            if len(shape) == 3:
                v = v.rearrange("p (a b c) -> p a b c", a=shape[0], b=shape[1])
            return v

        dist = carve(TT, T)
        strict = carve(TT, T)
        level_mask = carve(LEVELS, P)
        zeros = carve(T)
        dist_c = carve(TT, CPAD)
        valid_c = carve(TT, CPAD)
        wcmp_k, wcmp_v = carve(CMP_LEN, HD), carve(CMP_LEN, HD)
        mixer_base = top[0]
        sb_q, sb_k, sb_v = carve(PAIRS, T), carve(PAIRS, T), carve(TT, SB_W)
        q_st, k_st, v_st = carve(T), carve(T), carve(TT, P)
        sb_u = [carve(TT, T) for _ in range(2)]
        sb_p = [carve(TT, T) for _ in range(2)]
        sb_e = [carve(TT, T + 1) for _ in range(2)]
        sb_a = [carve(TT, T) for _ in range(2)]
        sb_pt = [carve(3, P) for _ in range(2)]
        top[0] = mixer_base
        n_q = carve(PAIRS, T)
        n_cmp = carve(2, T)
        n_ksel, n_kwin, n_vsel, n_vwin = carve(T), carve(T), carve(TT, P), carve(TT, P)
        n_gate = carve(TT, N_GATES)
        cmp_blk = carve(2, CMP_LEN, N_CMP)
        kc, vc = carve(CPAD), carve(2, HD)
        nq_st = carve(T)
        n_sc = [carve(TT, T) for _ in range(4)]
        n_pt = [carve(3, P) for _ in range(4)]
        n_scc = carve(2, TT, CPAD)
        n_ptc = carve(2, TT, P)
        n_mx, n_sum, n_coef = carve(4, TT), carve(4, TT), carve(4, TT)
        c_mx, c_sum = carve(2, TT), carve(2, TT)
        nsa_end = top[0]
        top[0] = mixer_base - 2 * CMP_LEN * HD
        hg_q, hg_f = carve(HG_HEADS, T), carve(HG_HEADS, T)
        hg_i, hg_g = carve(TT, HG_W), carve(TT, HG_W)
        hg_k, hg_s, hg_o = carve(HG_HEADS, T), carve(HG_HEADS, T), carve(TT, HG_W)
        q_lev, k_lev = carve(LEVELS, T), carve(LEVELS, T)
        q_x, k_x, a_x = carve(P), carve(P), carve(P)
        hg_t = carve(2, T)
        a_m = [xn[:, t, :].rearrange("p (l t) -> p l t", l=LEVELS) for t in range(TT)]
        top[0] = mixer_base
        gm = [carve(4, T) for _ in range(2)]
        m_t = carve(KD, T)
        m_tmp = [carve(4, T) for _ in range(2)]
        top[0] = 0
        spare = [raw[(FIRST["ffn0"] + j) % SLOTS] for j in (1, 2)]
        diag = spare[1][:, 0:DIAGS * P].rearrange("p (k t) -> p k t", k=DIAGS)
        v_ring = [spare[1][:, D:2 * D], spare[0][:, 0:D], spare[0][:, D:2 * D]]
        v_ring += [carve(D) for _ in range(RING - len(v_ring))]
        u_ring = [carve(D) for _ in range(RING)]
        pe_sc = carve(2, PE_HEADS, PE_KEYS)
        pe_s = carve(2, PE_KEYS)
        pe_cand = carve(PE_K, PE_K)
        pe_tv, pe_ti, pe_tif = carve(2, PE_K), carve(2, PE_K, dt=U32), carve(2, PE_K)
        pe_best, pe_nb, pe_pos = carve(PE_K), carve(1), carve(PE_K, dt=U32)
        pe_hl, pe_hlf, pe_e = carve(2, PE_K, dt=U32), carve(2, PE_K), carve(2, PE_K)
        pe_idx = carve(UNITS * PE_K, dt=U32)
        pe_exp, pe_sum = carve(UNITS * PE_K), carve(UNITS)
        pe_act = carve(PE_K)
        pe_h, pe_gelu = carve(PE_K), carve(PE_K)
        pe_rec, pe_gate = carve(1), carve(PE_K)
        pe_carrier, pool_carrier = carve(1), carve(1)
        pe_hot = [pe_s.rearrange("p a k -> p (a k)").rearrange("p (k i) -> p k i", k=PE_K), pe_cand]
        pe_q = arena[:, 0:PE_HEADS * T].rearrange("p (h t) -> p h t", h=PE_HEADS)
        idx_now = sb("idx_now", [P, 2, PE_K], U32)
        top[0] = 0
        ff_s, ff_a = carve(2, T), carve(2, T)
        causal = carve(TT, T)
        cv_b, cv_c, cv_z = carve(2, T), carve(2, T), carve(2, T)
        cv_u = carve(2, T + CONV_W - 1)
        df_k, df_v, df_q = carve(DIFF_HEADS, T), carve(TT, D), carve(DIFF_HEADS, T)
        df_qs, df_ks = carve(2, T), carve(2, T)
        df_sc = [carve(TT, T) for _ in range(4)]
        df_pt = [carve(3, P) for _ in range(2)]
        df_o = carve(TT, D)
        df_mx, df_sum, df_r = carve(4, TT), carve(4, TT), carve(4, TT)
        sq_dump = carve(D)
        lam_in, lam_dot, lam_exp, lam = carve(4, HD), carve(2), carve(2), carve(1)
        yh = oh[:, :, :, :].rearrange("p b k t -> p (b k) t")[:, 0:KD, :]
        yl = ol[:, :, :, :].rearrange("p b k t -> p (b k) t")[:, 0:KD, :]

        PS = ctx.enter_context(nc.psum_tensor("ps", [P, 4, 512], F32))
        ACC = ctx.enter_context(nc.psum_tensor("acc", [P, 4, 512], F32))

        def bank(b):
            return PS[:, b, :] if b < 4 else ACC[:, b - 4, :]

        x_loaded = sem("x_loaded")
        cols_loaded = sem("cols_loaded")
        wcmp_loaded = sem("wcmp_loaded")
        raw_ready = [sem(f"raw_ready{s}") for s in range(SLOTS)]
        spread_loaded = sem("spread_loaded")
        hi_done, lo_done = sem("hi_done"), sem("lo_done")
        panel_used = sem("panel_used")
        evacuated = sem("evacuated")
        tables = sem("tables")
        cols_turned, cols_ready = sem("cols_turned"), sem("cols_ready")
        sumsq = [sem(f"sumsq{t}") for t in range(TT)]
        rstd_ready = [sem(f"rstd_ready{t}") for t in range(TT)]
        rows_ready = [sem(f"rows_ready{t}") for t in range(TT)]
        rstd_step = sem("rstd_step")
        branch_half = sem("branch_half")
        turned, turned_hi, turned_lo = sem("turned"), sem("turned_hi"), sem("turned_lo")
        x_updated = sem("x_updated")
        dve_step = sem("dve_step")
        gain_used = sem("gain_used")
        pe_chain2 = sem("pe_chain2")
        out_stored = sem("out_stored")
        sb_staged, sb_scored, sb_sig, sb_attn = sem("sb_staged"), sem("sb_scored"), sem("sb_sig"), sem("sb_attn")
        sb_scan, sb_turned, sb_pt_ready, sb_out = sem("sb_scan"), sem("sb_turned"), sem("sb_pt_ready"), sem("sb_out")
        o_hi, o_lo = sem("o_hi"), sem("o_lo")
        n_blk, n_kc, n_kc_ready = sem("n_blk"), sem("n_kc"), sem("n_kc_ready")
        n_staged, n_scored, n_biased, n_max = sem("n_staged"), sem("n_scored"), sem("n_biased"), sem("n_max")
        n_exp, n_scaled, n_turned, n_pt_ready, n_out = sem("n_exp"), sem("n_scaled"), sem("n_turned"), sem("n_pt_ready"), sem("n_out")
        n_chain = sem("n_chain")
        c_scored, c_shift, c_exp, c_scaled = sem("c_scored"), sem("c_shift"), sem("c_exp"), sem("c_scaled")
        h_silu, h_ones, h_lev, h_chain = sem("h_silu"), sem("h_ones"), sem("h_lev"), sem("h_chain")
        h_scored, h_masked, h_cross, h_out, h_o_ready = sem("h_scored"), sem("h_masked"), sem("h_cross"), sem("h_out"), sem("h_o_ready")
        h_zero = sem("h_zero")
        m_zero, m_added, m_mul = sem("m_zero"), sem("m_added"), sem("m_mul")
        m_hi, m_lo = sem("m_hi"), sem("m_lo")

        pe_scored, pe_sc_ready = sem("pe_scored"), sem("pe_sc_ready")
        pe_chain, idx_ready, idx_copied = sem("pe_chain"), sem("idx_ready"), sem("idx_copied")
        u_landed = [sem(f"u_landed{k}") for k in range(RING)]
        v_landed = [sem(f"v_landed{k}") for k in range(RING)]
        u_used, v_used, diag_ready = sem("u_used"), sem("v_used"), sem("diag_ready")
        best_ready, exp_done, gelu_done, act_ready = sem("best_ready"), sem("exp_done"), sem("gelu_done"), sem("act_ready")
        ff_hi, ff_lo = sem("ff_hi"), sem("ff_lo")
        cv_pad, cv_chain, cv_y, cv_hi, cv_lo = sem("cv_pad"), sem("cv_chain"), sem("cv_y"), sem("cv_hi"), sem("cv_lo")
        lam_loaded, lam_dots, lam_exped, lam_ready = sem("lam_loaded"), sem("lam_dots"), sem("lam_exped"), sem("lam_ready")
        df_staged, df_scored, df_chain, df_max = sem("df_staged"), sem("df_scored"), sem("df_chain"), sem("df_max")
        df_exp, df_mixed, df_turned, df_pt_ready = sem("df_exp"), sem("df_mixed"), sem("df_turned"), sem("df_pt_ready")
        df_out, df_o_ready = sem("df_out"), sem("df_o_ready")

        def wait(eng, s, value):
            if not isinstance(value, int) or value > 0:
                eng.wait_ge(s, value)

        def along(table, p, m=0, i=0):
            return table[p] + i * (table[p + m] - table[p]) if m else table[p]

        def peeled(eng, n, body):
            body(0)
            with eng.Fori(1, n) as i:
                body(i)

        def skewed(eng, n, body):
            body(0, True)
            with eng.Fori(1, n - 1) as i:
                body(i, True)
            body(n - 1, False)

        def w_in_cols(c, n):
            return io["w_in"][0, :, c:c + n].rearrange("(k p) n -> p k n", p=P)

        def rows_1024(w, c, n=PC):
            return w[:, c:c + n].rearrange("(k p) n -> p k n", p=P)

        block = ctx.enter_context(nc.Block())

        @block.sync
        def _(sp):
            sp.dma_start(x[:, :, :], io["x"][0].rearrange("(t p) d -> p t d", p=P)).then_inc(x_loaded, 16)

            def load(p, src, m=0, i=0):
                wait(sp, lo_done, p + m * i - (SLOTS - 1))
                k = src.shape[1]
                sp.dma_start(raw[p % SLOTS][:, 0:k * src.shape[2]].rearrange("p (k n) -> p k n", k=k), src)\
                    .then_inc(raw_ready[p % SLOTS], 16)

            p = 0
            for c in (C_SBQ, C_SBK, C_SBV):
                for j in range(2):
                    load(p, w_in_cols(c + j * PC, PC))
                    p += 1
            for j in range(2):
                wait(sp, lo_done, p - (SLOTS - 1))
                dst = raw[p % SLOTS][:, :].rearrange("p (k q d) -> p k q d", k=KD, q=4)
                for q in range(4):
                    h = 2 * j + q // 2 + 4 * (q % 2)
                    sp.dma_start(dst[:, :, q, :], w_in_cols(C_NQ + h * HD, HD)).then_inc(raw_ready[p % SLOTS], 16)
                p += 1
            for c in (C_CMP, C_SEL, C_WIN):
                load(p, w_in_cols(c, PC))
                p += 1
            load(p, w_in_cols(C_NG, N_GATES))
            p += 1
            for c in (C_HQ, C_HF, C_HI, C_HG):
                for j in range(2):
                    load(p, w_in_cols(c + j * PC, PC))
                    p += 1
            for b, name in enumerate(("w_branch_sb", "w_branch_nsa", "w_branch_hgrn")):
                for half in range(2):
                    for j in range(2):
                        load(p, w_in_cols(C_MERGE + b * D + half * 512 + j * PC, PC))
                        p += 1
                    wait(sp, lo_done, p - (SLOTS - 1))
                    dst = raw[p % SLOTS][:, :].rearrange("p (i n) -> p i n", i=PAIRS)
                    w = io[name][0, :, half * 512:(half + 1) * 512]
                    for a in range(2):
                        src = (w.rearrange("(a i d) n -> a d i n", a=2, d=HD) if b == 1 else
                               w.rearrange("(i a d) n -> a d i n", a=2, d=HD))[a]
                        sp.dma_start(dst[a * HD:(a + 1) * HD], src).then_inc(raw_ready[p % SLOTS], 16)
                    p += 1
            for name in ("w_out", "peer_w_q"):
                for j in range(4):
                    load(p, rows_1024(io[name][0], j * PC))
                    p += 1

            def load_ffn(f):
                l, k = f // 2, f % 2
                gate, up, down = (io[f"w_ffn_{n}_2"][l, k] for n in ("gate", "up", "down"))
                p0 = FIRST[f"ffn{f}"]

                def down_rows(i):
                    return down[bass.ds(i * PC, PC), :].rearrange("(f p) n -> p f n", p=P)

                def column(w, i):
                    return w[:, bass.ds(i * PC, PC)].rearrange("(k p) n -> p k n", p=P)

                load(p0, column(gate, 0))
                if f == 0:
                    sp.wait_ge(v_used, UNITS * PE_K)
                load(p0 + 1, column(up, 0))
                with sp.Fori(1, FF_STEPS) as i:
                    load(p0 + 2, column(gate, i), 3, i - 1)
                    load(p0 + 3, column(up, i), 3, i - 1)
                    load(p0 + 4, down_rows(i - 1), 3, i - 1)
                load(p0 + 3 * FF_STEPS - 1, down_rows(FF_STEPS - 1))

            load_ffn(0)
            p0 = FIRST["conv_in"]
            for j in range(4):
                for w in range(3):
                    load(p0 + 3 * j + w, rows_1024(io["w_conv_in_2"][0], w * D + j * PC))
            for j in range(4):
                load(FIRST["conv_out"] + j, rows_1024(io["w_conv_out_2"][0], j * PC))
            load_ffn(1)
            for j in range(8):
                load(FIRST["kv"] + j, rows_1024(io["w_kv_2"], j * PC))
            load_ffn(2)
            for j in range(4):
                load(FIRST["q"] + j, rows_1024(io["w_q_2"][0], j * PC))
            for j in range(4):
                load(FIRST["o"] + j, rows_1024(io["w_o_2"][0], j * PC))
            load_ffn(3)
            for t in range(TT):
                sp.wait_ge(x_updated, X_AT["p3"] - TT + t + 1)
                sp.dma_start(io["out"][0, t * P:(t + 1) * P, :], x[:, t, :]).then_inc(out_stored, 16)
            sp.wait_ge(out_stored, 16 * TT)

        @block.gpsimd
        def _(pool):
            steps = [0]

            def table(ins):
                steps[0] += 1
                ins.then_inc(tables, 1)
                pool.wait_ge(tables, steps[0])

            def select(view, pattern, base, mult, op, fill):
                table(nc.gpsimd.affine_select(out=view, in_=view, pattern=pattern, base=base,
                                              channel_multiplier=mult, compare_op=op, fill=fill))

            g = nc.gpsimd
            table(g.memset(ident[:, :], 0.0))
            select(ident[:, :], [[-1, P]], 0, 1, ALU.not_equal, 1.0)
            table(g.memset(minus_half[:, :], -0.5))
            rstd_steps = [0]

            def norm_tile(name, t):
                k = NIDX[name]
                _, w, scale, factor = NORMS[k]
                c = slice(t * w // TT, (t + 1) * w // TT)
                m, rs = ss[:, k, c], rstd[:, k, c]
                pool.wait_ge(sumsq[t], k + 1)
                g.tensor_scalar(m, m, scale / factor ** 2, EPS / factor ** 2, ALU.mult, ALU.add).then_inc(rstd_step, 1)
                rstd_steps[0] += 1
                pool.wait_ge(rstd_step, rstd_steps[0])
                g.tensor_tensor(rs, m, minus_half[:, c], ALU.pow).then_inc(rstd_ready[t], 1)

            def norm(name):
                for t in range(TT):
                    norm_tile(name, t)

            norm("mix")
            table(g.memset(strict[:, :, :], 0.0))
            select(strict, [[P, TT], [-1, T]], 0, 1, ALU.is_gt, NEG)
            table(g.memset(zeros, 0.0))
            for a in range(2):
                table(g.memset(sb_e[a][:, :, 0:1], 1.0))
            sb_tables_done = steps[0]
            table(g.iota(dist, [[P, TT], [-1, T]], base=0, channel_multiplier=1, allow_small_or_imprecise_dtypes=True))
            select(dist, [[P, TT], [-1, T]], 0, 1, ALU.is_ge, FAR)
            pat = [[P, TT], [-CMP_STRIDE, CPAD]]
            table(g.iota(dist_c, pat, base=1 - CMP_LEN, channel_multiplier=1, allow_small_or_imprecise_dtypes=True))
            select(dist_c, pat, 1 - CMP_LEN, 1, ALU.is_ge, FAR)
            table(g.memset(valid_c, 1.0))
            select(valid_c, pat, 1 - CMP_LEN, 1, ALU.is_ge, 0.0)
            for h in range(8):
                table(g.memset(slopes[:, h:h + 1], -2.0 ** -(h + 1)))
            table(g.memset(level_mask, 1.0))
            select(level_mask[:, 0, :], [[-1, P]], 0, 1, ALU.is_equal, 0.0)
            for l in range(1, LEVELS - 1):
                w = 2 ** l
                v = level_mask[:, l, :].rearrange("p (b w) -> p b w", w=w)
                select(v, [[-w, P // w], [0, w]], 0, 1, ALU.is_ge, 0.0)
                select(v, [[w, P // w], [0, w]], w - 1, -1, ALU.is_ge, 0.0)
            table(g.iota(iota16[:, :], [[1, PE_K]], base=0, channel_multiplier=0, allow_small_or_imprecise_dtypes=True))
            assert steps[0] == N_TABLES and sb_tables_done == SB_TABLES, (steps[0], sb_tables_done)

            pool.wait_ge(evacuated, EVAC[FIRST["nsa_q"]])

            def stage(i):
                wait(pool, sb_scored, 2 * i)
                g.tensor_copy(q_st, sb_q[:, bass.ds(i, 1), :].rearrange("p a t -> p (a t)")).then_inc(sb_staged, 1)
                g.tensor_copy(k_st, sb_k[:, bass.ds(i, 1), :].rearrange("p a t -> p (a t)")).then_inc(sb_staged, 1)
                wait(pool, sb_out, 2 * i)
                g.tensor_copy(v_st, sb_v[:, :, bass.ds(i * P, P)]).then_inc(sb_staged, 1)

            peeled(pool, PAIRS, stage)
            pool.wait_ge(sb_out, 2 * PAIRS)
            g.memset(vc, 0.0).then_inc(n_kc_ready, 1)
            g.memset(kc, 0.0).then_inc(n_kc_ready, 1)
            pool.wait_ge(evacuated, EVAC[FIRST["hg"]])

            def stage_nsa(i):
                wait(pool, c_scored, 2 * i)
                g.tensor_copy(nq_st, n_q[:, bass.ds(i, 1), :].rearrange("p a t -> p (a t)")).then_inc(n_staged, 1)

            peeled(pool, PAIRS, stage_nsa)
            pool.wait_ge(n_out, 2 * PAIRS)
            pool.wait_ge(o_lo, 2 * PAIRS)
            g.memset(q_lev, 0.0).then_inc(h_zero, 1)
            g.memset(k_lev, 0.0).then_inc(h_zero, 1)
            g.memset(hg_s, 1.0).then_inc(h_zero, 1)
            g.dma_start(gb[:, 0:HG_W], io["hgrn_norm"].partition_broadcast(P).rearrange("p a n -> p (a n)")).then_inc(spread_loaded, 16)
            norm("hg")
            pool.wait_ge(turned, XEND["hg"])
            g.memset(m_t, 0.0).then_inc(m_zero, 1)

            spread = {"hg": io["hgrn_norm"], "peer": io["norm_ffn"], "final": io["norm_final"].unsqueeze(0),
                      "p0": io["g_norm_2"][0, 1:2], "pc": io["g_norm_2"][0, 3:4], "p1": io["g_norm_2"][0, 5:6],
                      "p2": io["g_norm_2"][1, 1:2], "diff": io["g_subln_2"], "pa": io["g_norm_2"][1, 3:4],
                      "p3": io["g_norm_2"][1, 5:6]}

            gain_free = {"peer": (h_silu, 5), "final": (gain_used, TT), "p0": (x_updated, X_AT["final"]),
                         "pa": (rows_ready[1], XIDX["diff"] + 1)}
            for k, (name, _) in enumerate(POSTS):
                if k:
                    gain_free[("diff" if name == "pa" else name)] = (gain_used, TT * (k + 1))
            gain_free["p3"] = (gain_used, TT * 6)

            def load_gain(name):
                pool.wait_ge(*gain_free[name])
                src = spread[name]
                g.dma_start(gb[:, 0:src.shape[1]], src.partition_broadcast(P).rearrange("p a n -> p (a n)")).then_inc(spread_loaded, 16)

            load_gain("peer")
            norm("peer")
            pool.wait_ge(pe_scored, PE_HEADS // 2 + 1)
            tables_, rings, landed, used = ([io[w].rearrange("a e d -> (a e) d") for w in ("peer_u", "peer_v")], (u_ring, v_ring),
                                            (u_landed, v_landed), (u_used, v_used))

            def gather(w, n, r, count):
                wait(pool, used[w], PE_K * n + GROUP * (r + 1) - RING)
                own = slice(r * GROUP, (r + 1) * GROUP)
                g.tensor_copy(idx_now[:, w, own], pe_idx[:, bass.ds(n * PE_K + r * GROUP, GROUP)]).then_inc(idx_copied, 1)
                pool.wait_ge(idx_copied, 2 * count + 1)
                g.tensor_tensor(pool_carrier, minus_half[:, 0:1], minus_half[:, 0:1], ALU.mult).then_inc(idx_copied, 1)
                for k in range(r * GROUP, (r + 1) * GROUP):
                    slot = k % RING
                    g.indirect_dma_start(out=rings[w][slot], out_offset=None, in_=tables_[w],
                                         in_offset=bass.IndirectOffsetOnAxis(ap=idx_now[:, w, k:k + 1], axis=0))\
                        .then_inc(landed[w][slot], 16)

            groups = PE_K // GROUP

            def gather_unit(n):
                pool.wait_ge(idx_ready, n + 1)
                for r in range(groups):
                    gather(0, n, r, 2 * groups * n - groups + 2 * r)
                    gather(1, n - 1, r, 2 * groups * n - groups + 2 * r + 1)

            pool.wait_ge(idx_ready, 1)
            for r in range(groups):
                gather(0, 0, r, r)
            gather_unit(1)
            with pool.Fori(2, UNITS) as n:
                gather_unit(n)
            for r in range(groups):
                gather(1, UNITS - 1, r, 2 * groups * UNITS - groups + r)
            load_gain("final")
            for t in range(TT):
                norm_tile("final", t)
                norm_tile("f0", t)

            def post(name):
                load_gain(name)
                norm(name)

            g.memset(cv_u, 0.0).then_inc(cv_pad, 1)
            table(g.memset(causal, 0.0))
            select(causal, [[P, TT], [-1, T]], 0, 1, ALU.is_ge, NEG)
            for k, nm in enumerate(("lambda_q1_2", "lambda_k1_2", "lambda_q2_2", "lambda_k2_2")):
                g.dma_start(lam_in[:, k, :], io[nm].partition_broadcast(P).rearrange("p a n -> p (a n)")).then_inc(lam_loaded, 16)
            post("p0")
            norm("conv")
            post("pc")
            norm("f1")
            post("p1")
            norm("kv")
            post("p2")
            norm("attn")
            load_gain("diff")
            pool.wait_ge(evacuated, EVAC[FIRST["o"]])

            def stage_diff(i):
                for b in range(2):
                    h = 2 * i + b
                    wait(pool, df_scored, 2 * h - 2)
                    for dst, src in ((df_qs, df_q), (df_ks, df_k)):
                        g.tensor_copy(dst[:, b, :], src[:, bass.ds(h, 1), :].rearrange("p a t -> p (a t)")).then_inc(df_staged, 1)

            stage_diff(0)
            with pool.Fori(1, DIFF_HEADS // 2) as i:
                stage_diff(i)
            norm("diff")
            post("pa")
            norm("f3")
            post("p3")

        @block.scalar
        def _(act):
            def split(p, m=0, i=0):
                s = p % SLOTS
                act.wait_ge(raw_ready[s], along(LANDED, p, m, i))
                wait(act, panel_used, p + m * i - (SLOTS - 1))
                nc.scalar.activation(hi[s][:, 0:WORDS[p]], raw[s][:, 0:WORDS[p]], ACT.Copy).then_inc(hi_done, 1)

            def evac(p, out, func=ACT.Copy, scale=1.0, in_=None, m=0, i=0):
                act.wait_ge(panel_used, p + m * i + 1)
                nc.scalar.activation(out, bank(BANK[p]) if in_ is None else in_, func, scale=scale).then_inc(evacuated, 1)

            for n, (src, r) in enumerate([(io["norm_mix"][0], GAIN["mix"]), (io["norm_ffn"][0], GAIN["peer"]), (io["g_kv_2"], GAIN["kv"])]
                                         + [(io["g_norm_2"][l, j], GAIN[nm]) for l, j, nm in
                                            ((0, 0, "f0"), (0, 2, "conv"), (0, 4, "f1"), (1, 0, "f2"), (1, 2, "attn"), (1, 4, "f3"))]):
                act.dma_start(rowbuf[r:r + 8, 0, :], src.rearrange("(c p) -> c p", p=P)).then_inc(cols_loaded, 16)
            act.dma_start(rowbuf[TAPS:TAPS + 24, 0, :], io["w_conv_2"][0].rearrange("j (c p) -> (j c) p", p=P)).then_inc(cols_loaded, 16)
            for a in range(2):
                act.dma_start(rowbuf[0:CMP_LEN, 1, a * HD:(a + 1) * HD], io["nsa_cmp_pe"][0]).then_inc(cols_loaded, 16)
                act.dma_start(rowbuf[:, 2, a * HD:(a + 1) * HD], io["peer_sub_keys"][0, a]).then_inc(cols_loaded, 16)
            for a in range(2):
                for w, name in ((wcmp_k, "nsa_w_cmp_k"), (wcmp_v, "nsa_w_cmp_v")):
                    act.dma_start(w[a * HD:(a + 1) * HD], io[name][0].rearrange("(l d) j -> d l j", d=HD)).then_inc(wcmp_loaded, 16)

            def norm_rows(name):
                k = NIDX[name]
                wait(act, turned, XBASE[name])
                nc.scalar.activation(xn[:, 0, :], x[:, 0, :], ACT.Square, accum_out=ss[:, k, 0:1]).then_inc(sumsq[0], 1)
                act.wait_ge(rstd_ready[1], k + 1)
                nc.scalar.activation(xn[:, 1, :], x[:, 1, :], ACT.Copy, scale=rstd[:, k, 1:2]).then_inc(rows_ready[1], 1)

            def turn(name, out, gain):
                for b in range((SEND[name] - SBASE[name]) // 2):
                    if name in XBASE:
                        act.wait_ge(turned, XBASE[name] + b + 1)
                    src = ACC[:, b, :].rearrange("p (k t) -> p k t", k=2)
                    if gain is None:
                        nc.scalar.activation(out[:, 2 * b:2 * b + 2, :], src, ACT.Copy).then_inc(turned_hi, 2)
                        continue
                    for j in range(2):
                        c = GAIN[gain] + 2 * b + j
                        nc.scalar.activation(out[:, 2 * b + j, :], src[:, j, :], ACT.Copy, scale=cols[:, c:c + 1])\
                            .then_inc(turned_hi, 1)

            act.wait_ge(x_loaded, 16)
            norm_rows("mix")
            act.wait_ge(cols_turned, 1)
            nc.scalar.activation(cols[:, :], bank(3)[:, 0:256], ACT.Copy).then_inc(cols_ready, 1)
            split(0)
            split(1)
            act.wait_ge(cols_ready, 1)
            turn("mix", xh, "mix")

            for j in range(2):
                split(j + 2)
                evac(j, sb_q[:, 2 * j:2 * j + 2, :].rearrange("p a t -> p (a t)"), scale=HD ** -0.5)
            for j in range(2):
                split(j + 4)
                evac(2 + j, sb_k[:, 2 * j:2 * j + 2, :].rearrange("p a t -> p (a t)"))
            for j in range(2):
                split(j + 6)
                evac(4 + j, sb_v[:, :, j * PC:(j + 1) * PC], in_=bank(BANK[4 + j]).rearrange("p (t n) -> p t n", t=TT))

            def sb_pair(i):
                for a in range(2):
                    act.wait_ge(sb_scored, 2 * i + a + 1)
                    wait(act, sb_attn, 2 * i + a - 1)
                    z = bank(4 + a).rearrange("p (t s) -> p t s", t=TT)
                    nc.scalar.activation(sb_u[a], z, ACT.Sigmoid, scale=-1.0).then_inc(sb_sig, 1)
                    nc.scalar.activation(sb_p[a], z, ACT.Sigmoid).then_inc(sb_sig, 1)
                for a in range(2):
                    act.wait_ge(sb_turned, 2 * i + a + 1)
                    wait(act, sb_out, 2 * i + a - 1)
                    nc.scalar.activation(sb_pt[a].rearrange("p a b -> p (a b)"), bank(6 + a)[:, 0:3 * P], ACT.Copy).then_inc(sb_pt_ready, 1)
                act.wait_ge(sb_out, 2 * i + 2)
                nc.scalar.activation(oh[:, 0, bass.ds(i, 1), :], bank(3)[:, 0:T].rearrange("p (a t) -> p a t", a=1), ACT.Copy).then_inc(o_hi, 1)

            peeled(act, PAIRS, sb_pair)

            act.wait_ge(o_lo, PAIRS)
            q0 = FIRST["nsa_q"]
            for j in range(2):
                split(q0 + j + 2)
                evac(q0 + j, n_q[:, 2 * j:2 * j + 2, :].rearrange("p a t -> p (a t)"), scale=HD ** -0.5)
            c0 = FIRST["nsa_kv"]
            split(c0 + 2)
            evac(c0, n_cmp.rearrange("p a t -> p (a t)"))
            for j, (k_, v_) in enumerate(((n_ksel, n_vsel), (n_kwin, n_vwin))):
                split(c0 + 3 + j)
                act.wait_ge(panel_used, c0 + 2 + j)
                b = bank(BANK[c0 + 1 + j])
                nc.scalar.activation(k_, b[:, 0:T], ACT.Copy)
                nc.scalar.activation(v_, b[:, T:2 * T].rearrange("p (t n) -> p t n", t=TT), ACT.Copy).then_inc(evacuated, 1)
            g0 = FIRST["nsa_gate"]
            split(g0 + 2)
            evac(g0, n_gate, func=ACT.Sigmoid, in_=bank(BANK[g0])[:, 0:TT * N_GATES].rearrange("p (t n) -> p t n", t=TT))
            act.wait_ge(n_kc, 1)
            act.wait_ge(n_kc_ready, 2)
            nc.scalar.activation(kc[:, 0:N_CMP], bank(2)[:, 0:N_CMP], ACT.Copy)
            nc.scalar.activation(vc[0:N_CMP, 0, :], bank(3)[0:N_CMP, 0:HD], ACT.Copy)
            nc.scalar.activation(vc[0:N_CMP, 1, :], bank(4)[0:N_CMP, 0:HD], ACT.Copy).then_inc(n_kc_ready, 1)

            def nsa_exp(h, a):
                for br in range(2):
                    u = 2 * br + a
                    act.wait_ge(n_max, 2 * h + br + 1)
                    for t in range(TT):
                        nc.scalar.activation(n_sc[u][:, t, :], n_sc[u][:, t, :], ACT.Exp, bias=n_mx[:, u, t:t + 1],
                                             accum_out=n_sum[:, u, t:t + 1]).then_inc(n_exp, 1)
                act.wait_ge(c_shift, h + 1)
                nc.scalar.activation(n_scc[:, a], n_scc[:, a], ACT.Exp).then_inc(c_exp, 1)

            def nsa_turned(h, a):
                wait(act, n_out, h - 1)
                for br in range(2):
                    act.wait_ge(n_turned, 3 * h + br + 1)
                    nc.scalar.activation(n_pt[2 * br + a].rearrange("p a b -> p (a b)"), bank(br)[:, 0:3 * P], ACT.Copy).then_inc(n_pt_ready, 1)
                act.wait_ge(n_turned, 3 * h + 3)
                nc.scalar.activation(n_ptc[0:CPAD, a].rearrange("p t s -> p (t s)"), bank(3)[0:CPAD, 0:TT * P], ACT.Copy).then_inc(n_pt_ready, 1)

            def nsa_out(i):
                act.wait_ge(n_out, 2 * i + 2)
                nc.scalar.activation(oh[:, 1, bass.ds(i, 1), :], bank(2)[:, 0:T].rearrange("p (a t) -> p a t", a=1), ACT.Copy).then_inc(o_hi, 1)

            def nsa_pair(i, more):
                if not isinstance(i, int) or i > 0:
                    nsa_out(i - 1)
                for a in range(2):
                    nsa_turned(2 * i + a, a)
                if more:
                    for a in range(2):
                        nsa_exp(2 * i + 2 + a, a)

            for a in range(2):
                nsa_exp(a, a)
            skewed(act, PAIRS, nsa_pair)
            nsa_out(PAIRS - 1)

            act.wait_ge(o_lo, 2 * PAIRS)
            h0 = FIRST["hg"]
            flat = lambda v, j: v[:, 2 * j:2 * j + 2, :].rearrange("p a t -> p (a t)")
            for j in range(2):
                split(h0 + j + 2)
                act.wait_ge(panel_used, h0 + j + 1)
                if j:
                    act.wait_ge(h_silu, 1)
                nc.scalar.activation(flat(hg_q, j), bank(BANK[h0 + j]), ACT.Sigmoid)
                nc.scalar.activation(hg_t.rearrange("p a t -> p (a t)"), bank(BANK[h0 + j]), ACT.Copy).then_inc(evacuated, 1)
            for j in range(2):
                split(h0 + j + 4)
                evac(h0 + 2 + j, flat(hg_f, j), func=ACT.Sigmoid)
            for j in range(2):
                split(h0 + j + 6)
                b = bank(BANK[h0 + 4 + j]).rearrange("p (t n) -> p t n", t=TT)
                evac(h0 + 4 + j, hg_i[:, :, j * PC:(j + 1) * PC], in_=b)
            for j in range(2):
                split(h0 + j + 8)
                act.wait_ge(panel_used, h0 + 6 + j + 1)
                act.wait_ge(h_silu, (2, 4)[j])
                b = bank(BANK[h0 + 6 + j]).rearrange("p (t n) -> p t n", t=TT)
                nc.scalar.activation(hg_g[:, :, j * PC:(j + 1) * PC], b, ACT.Sigmoid)
                nc.scalar.activation(hg_t, b, ACT.Copy).then_inc(evacuated, 1)

            def hg_head(i):
                act.wait_ge(h_scored, i + 1)
                wait(act, h_out, i)
                nc.scalar.activation(a_x, bank(3)[:, 0:P], ACT.Copy).then_inc(h_cross, 1)
                act.wait_ge(h_out, i + 1)
                nc.scalar.activation(hg_o[:, :, bass.ds(i * P, P)], bank(2)[:, 0:2 * P].rearrange("p (t v) -> p t v", t=TT), ACT.Copy).then_inc(h_o_ready, 1)

            peeled(act, HG_HEADS, hg_head)
            turn("hg", oh[:, 2, :, :], None)

            def merge(b):
                for half in range(2):
                    p = FIRST["merge"] + 3 * half
                    for j in range(2):
                        split(p + j + 2, 6, b)
                        wait(act, m_mul, 2 * b + half - 1)
                        evac(p + j, gm[half][:, 2 * j:2 * j + 2, :].rearrange("p a t -> p (a t)"), func=ACT.Sigmoid, m=6, i=b)
                    split(p + 4, 6, b)

            peeled(act, 3, merge)

            act.wait_ge(panel_used, FIRST["w_out"])
            for half in range(2):
                act.wait_ge(m_added, 5 + half)
                nc.scalar.activation(xh[:, 4 * half:4 * half + 4, :], m_t[:, 4 * half:4 * half + 4, :], ACT.Copy).then_inc(m_hi, 1)
            for j in range(4):
                split(FIRST["w_out"] + j + 2)

            act.wait_ge(evacuated, EVAC[FIRST["peer_q"]])
            norm_rows("peer")
            turn("peer", xh, "peer")
            p0 = FIRST["peer_q"]
            for j in range(4):
                if j < 3:
                    split(p0 + j + 2)
                evac(p0 + j, pe_q[:, 2 * j:2 * j + 2, :].rearrange("p h t -> p (h t)"))
                act.wait_ge(pe_scored, j + 1)
                own = slice(j % 2 * 2 * P, (j % 2 + 1) * 2 * P)
                for a in range(2):
                    nc.scalar.activation(pe_sc[:, a, 2 * j:2 * j + 2, :].rearrange("p h k -> p (h k)"), ACC[:, 2 * a + j // 2, own],
                                         ACT.Copy).then_inc(pe_sc_ready, 1)
            def best_exp(n):
                act.wait_ge(best_ready, n + 1)
                nc.scalar.activation(pe_exp[:, bass.ds(n * PE_K, PE_K)], pe_best, ACT.Exp, bias=pe_nb,
                                     accum_out=pe_sum[:, bass.ds(n, 1)]).then_inc(exp_done, 1)

            def weights(n):
                act.wait_ge(u_used, PE_K * (n + 1))
                wait(act, act_ready, n)
                nc.scalar.activation(pe_gelu, pe_h, ACT.Gelu).then_inc(gelu_done, 1)
                act.wait_ge(act_ready, n + 1)
                for k in range(PE_K):
                    wait(act, v_used, PE_K * n + k + 1 - DIAGS)
                    nc.scalar.activation(diag[:, k % DIAGS, :], ident[:, :], ACT.Copy, scale=pe_act[:, k:k + 1]).then_inc(diag_ready, 1)

            best_exp(0)
            best_exp(1)
            weights(0)
            with act.Fori(1, UNITS - 1) as n:
                best_exp(n + 1)
                weights(n)
            weights(UNITS - 1)

            def ffn(f):
                p0 = FIRST[f"ffn{f}"]
                last = p0 + 3 * FF_STEPS - 1

                def silu(p, m=0, r=0):
                    act.wait_ge(panel_used, p + m * r + 1)
                    act.wait_ge(evacuated, along(EVAC, p, m, r))
                    nc.scalar.activation(ff_s.rearrange("p f t -> p (f t)"), bank(BANK[p]), ACT.Silu).then_inc(evacuated, 1)

                def upper(p, down_done, m=0, r=0):
                    act.wait_ge(evacuated, along(EVAC, p, m, r) + 2)
                    act.wait_ge(panel_used, down_done)
                    nc.scalar.activation(ah[:, :, :], ff_a, ACT.Copy).then_inc(ff_hi, 1)

                split(p0 + 2)
                split(p0 + 3)
                silu(p0)
                upper(p0, p0)

                def step(i, next_up=True):
                    split(p0 + 4, 3, i - 1)
                    split(p0 + 5, 3, i - 1)
                    silu(p0 + 2, 3, i - 1)
                    if next_up:
                        split(p0 + 6, 3, i - 1)
                    upper(p0 + 2, p0 + 5 + 3 * (i - 1), 3, i - 1)

                with act.Fori(1, FF_STEPS - 1) as i:
                    step(i)
                step(FF_STEPS - 1, last + 1 < NP)
                if last + 2 < NP:
                    split(last + 2)

            def post(name, panels):
                k, after = NIDX[name], dict(POSTS)[name]
                for t in range(TT):
                    act.wait_ge(*((branch_half, [n for n, _ in POSTS].index(name) + 1) if t == 0 else (panel_used, panels)))
                    act.wait_ge(sumsq[1 - t], k + t)
                    nc.scalar.activation(sq_dump, ACC[:, 2 * t:2 * t + 2, :].rearrange("p b n -> p (b n)"), ACT.Square,
                                         accum_out=ss[:, k, t:t + 1]).then_inc(sumsq[t], 1)
                if after is None:
                    return
                k = NIDX[after]
                act.wait_ge(x_updated, X_AT[name] - 1)
                act.wait_ge(sumsq[1], k)
                nc.scalar.activation(sq_dump, x[:, 0, :], ACT.Square, accum_out=ss[:, k, 0:1]).then_inc(sumsq[0], 1)
                act.wait_ge(rstd_ready[0], k + 1)
                nc.scalar.activation(xn[:, 0, :], x[:, 0, :], ACT.Copy, scale=rstd[:, k, 0:1]).then_inc(rows_ready[0], 1)
                turn(after, xh, after)

            split(FIRST["ffn0"] + 1)
            turn("f0", xh, "f0")
            ffn(0)
            post("p0", FIRST["conv_in"])
            p0 = FIRST["conv_in"]

            def conv(j):
                for w, out in enumerate((cv_b, cv_c, None)):
                    split(p0 + w + 2, 3, j)
                    if out is not None:
                        wait(act, cv_y, j)
                        evac(p0 + w, out.rearrange("p f t -> p (f t)"), m=3, i=j)
                act.wait_ge(cv_y, j + 1)
                nc.scalar.activation(yh[:, bass.ds(2 * j, 2), :], cv_z, ACT.Copy).then_inc(cv_hi, 1)

            peeled(act, 4, conv)
            for j in range(4):
                split(FIRST["conv_out"] + j + 2)
            post("pc", FIRST["ffn1"])
            ffn(1)
            post("p1", FIRST["kv"])
            for j in range(8):
                p = FIRST["kv"] + j
                split(p + 2)
                if j < 4:
                    evac(p, df_k[:, 2 * j:2 * j + 2, :].rearrange("p h t -> p (h t)"))
                else:
                    c = (j - 4) * PC
                    evac(p, df_v[:, :, c:c + PC], in_=bank(BANK[p]).rearrange("p (t n) -> p t n", t=TT))
            act.wait_ge(panel_used, FIRST["ffn2"])
            turn("f2", xh, "f2")
            ffn(2)
            post("p2", FIRST["q"])
            for j in range(4):
                p = FIRST["q"] + j
                split(p + 2)
                evac(p, df_q[:, 2 * j:2 * j + 2, :].rearrange("p h t -> p (h t)"), scale=HD ** -0.5)
            act.wait_ge(lam_dots, 2)
            nc.scalar.activation(lam_exp, lam_dot, ACT.Exp).then_inc(lam_exped, 1)

            def diff_exp(h, b):
                for c in range(2):
                    u = 2 * b + c
                    act.wait_ge(df_max, 2 * h + c + 1)
                    for t in range(TT):
                        nc.scalar.activation(df_sc[u][:, t, :], df_sc[u][:, t, :], ACT.Exp, bias=df_mx[:, u, t:t + 1],
                                             accum_out=df_sum[:, u, t:t + 1]).then_inc(df_exp, 1)

            def diff_turned(h, b):
                act.wait_ge(df_turned, h + 1)
                wait(act, df_out, h - 1)
                nc.scalar.activation(df_pt[b].rearrange("p n t -> p (n t)"), bank(b)[:, 0:3 * P], ACT.Copy).then_inc(df_pt_ready, 1)

            def diff_out(h, b):
                act.wait_ge(df_out, h + 1)
                nc.scalar.activation(df_o[:, :, bass.ds(h * P, P)], bank(2 + b)[:, 0:TT * P].rearrange("p (t e) -> p t e", t=TT),
                                     ACT.Copy).then_inc(df_o_ready, 1)

            def diff_pair(i, more):
                for b in range(2):
                    diff_turned(2 * i + b, b)
                if more:
                    for b in range(2):
                        diff_exp(2 * i + 2 + b, b)
                for b in range(2):
                    diff_out(2 * i + b, b)

            for b in range(2):
                diff_exp(b, b)
            skewed(act, DIFF_HEADS // 2, diff_pair)
            turn("diff", xh, None)
            for j in range(4):
                split(FIRST["o"] + j + 2)
            post("pa", FIRST["ffn3"])
            ffn(3)
            post("p3", NP)

        @block.vector
        def _(dve):
            v = nc.vector
            chain = [0]

            def link(ins):
                chain[0] += 1
                ins.then_inc(dve_step, 1)
                dve.wait_ge(dve_step, chain[0])

            def split(p, m=0, i=0):
                s = p % SLOTS
                dve.wait_ge(hi_done, p + m * i + 1)
                v.tensor_tensor(lo[s][:, 0:WORDS[p]], raw[s][:, 0:WORDS[p]], hi[s][:, 0:WORDS[p]].bitcast(F32), ALU.subtract).then_inc(lo_done, 1)

            def square(rows, dump, out):
                return v.scalar_tensor_tensor(out=dump, in0=rows, scalar=1.0, in1=rows, op0=ALU.mult, op1=ALU.mult, accum_out=out)

            def norm_rows(name):
                k = NIDX[name]
                wait(dve, turned, XBASE[name])
                square(x[:, 1, :], xn[:, 1, :], ss[:, k, 1:2]).then_inc(sumsq[1], 1)
                dve.wait_ge(rstd_ready[0], k + 1)
                v.tensor_scalar(xn[:, 0, :], x[:, 0, :], rstd[:, k, 0:1], None, ALU.mult).then_inc(rows_ready[0], 1)

            def turn(name, out_hi, out_lo, gain):
                for b in range((SEND[name] - SBASE[name]) // 2):
                    dve.wait_ge(turned_hi, SBASE[name] + 2 * b + 2)
                    src = ACC[:, b, :].rearrange("p (k t) -> p k t", k=2)
                    for j in range(2):
                        s = 1.0 if gain is None else cols[:, GAIN[gain] + 2 * b + j:GAIN[gain] + 2 * b + j + 1]
                        v.scalar_tensor_tensor(out=out_lo[:, 2 * b + j, :], in0=src[:, j, :], scalar=s,
                                               in1=out_hi[:, 2 * b + j, :].bitcast(F32), op0=ALU.mult, op1=ALU.subtract).then_inc(turned_lo, 1)

            dve.wait_ge(x_loaded, 16)
            norm_rows("mix")
            split(0)
            split(1)
            dve.wait_ge(cols_ready, 1)
            turn("mix", xh, xl, "mix")
            for j in range(6):
                split(j + 2)

            dve.wait_ge(tables, SB_TABLES)

            def sb_pair(i):
                for a in range(2):
                    dve.wait_ge(sb_sig, 4 * i + 2 * a + 1)
                    for t in range(TT):
                        v.tensor_tensor_scan(out=sb_e[a][:, t, 1:T + 1], data0=sb_u[a][:, t, ::-1], data1=zeros, initial=1.0,
                                             op0=ALU.mult, op1=ALU.add).then_inc(sb_scan, 1)
                    dve.wait_ge(sb_scan, 4 * i + 2 * a + 2)
                    dve.wait_ge(sb_sig, 4 * i + 2 * a + 2)
                    wait(dve, sb_turned, 2 * i + a - 1)
                    v.tensor_tensor(sb_a[a], sb_p[a], sb_e[a][:, :, T - 1::-1], ALU.mult).then_inc(sb_attn, 1)
                dve.wait_ge(o_hi, i + 1)
                v.tensor_tensor(ol[:, 0, bass.ds(i, 1), :], bank(3)[:, 0:T].rearrange("p (a t) -> p a t", a=1),
                                oh[:, 0, bass.ds(i, 1), :].bitcast(F32), ALU.subtract).then_inc(o_lo, 1)

            peeled(dve, PAIRS, sb_pair)

            for j in range(3):
                split(FIRST["nsa_kv"] + j)
            dve.wait_ge(evacuated, EVAC[FIRST["nsa_kv"] + 1])
            for w in range(2):
                src = n_cmp[:, w, :].rearrange("p (n l) -> p l n", l=CMP_STRIDE)
                for j in range(2):
                    l0 = j * CMP_STRIDE
                    pe_ = cols[:, 96 + l0:96 + l0 + CMP_STRIDE].unsqueeze(2).to_broadcast([P, CMP_STRIDE, N_CMP])
                    v.tensor_tensor(cmp_blk[:, w, l0:l0 + CMP_STRIDE, :], src[:, :, j:j + N_CMP], pe_, ALU.add).then_inc(n_blk, 1)
            for j in range(3):
                split(FIRST["nsa_kv"] + 3 + j)
            dve.wait_ge(tables, N_TABLES)
            dve.wait_ge(evacuated, EVAC[FIRST["hg"]])

            SCORE_LINKS, SCALE_LINKS = 6, 8

            def nsa_links(before):
                done = [before]

                def then(ins):
                    done[0] = done[0] + 1
                    ins.then_inc(n_chain, 1)
                    dve.wait_ge(n_chain, done[0])
                return then

            def nsa_scores(h, i, a, before):
                then = nsa_links(before)
                wait(dve, n_turned, 3 * h - 3)
                slope = slopes[:, bass.ds(i + 4 * a, 1)]
                for br in range(2):
                    u = 2 * br + a
                    dve.wait_ge(n_scored, 2 * h + br + 1)
                    then(v.scalar_tensor_tensor(out=n_sc[u].rearrange("p t s -> p (t s)"), in0=dist.rearrange("p t s -> p (t s)"),
                                                scalar=slope, in1=bank(4 + 2 * a + br), op0=ALU.mult, op1=ALU.add))
                    then(v.tensor_reduce(n_mx[:, u, :], n_sc[u], AX.X, ALU.max))
                    v.tensor_scalar(n_mx[:, u, :], n_mx[:, u, :], -1.0, None, ALU.mult).then_inc(n_max, 1)
                dve.wait_ge(c_scored, h + 1)
                then(v.scalar_tensor_tensor(out=n_scc[:, a].rearrange("p t c -> p (t c)"), in0=dist_c.rearrange("p t c -> p (t c)"), scalar=slope,
                                            in1=bank(3)[:, T:T + TT * CPAD], op0=ALU.mult, op1=ALU.add))
                then(v.tensor_reduce(c_mx[:, a, :], n_scc[:, a], AX.X, ALU.max))
                v.tensor_tensor(n_scc[:, a], n_scc[:, a], c_mx[:, a, :].unsqueeze(2).to_broadcast([P, TT, CPAD]), ALU.subtract).then_inc(c_shift, 1)

            def nsa_scale(h, i, a, before):
                then = nsa_links(before)
                gate = lambda br: n_gate[:, :, bass.ds(3 * (i + 4 * a) + br, 1)].rearrange("p t o -> p (t o)")
                dve.wait_ge(c_exp, h + 1)
                then(v.tensor_reduce(c_sum[:, a, :], n_scc[:, a], AX.X, ALU.add))
                then(v.reciprocal(c_sum[:, a, :], c_sum[:, a, :]))
                then(v.tensor_tensor(c_sum[:, a, :], c_sum[:, a, :], gate(0), ALU.mult))
                then(v.tensor_tensor(n_scc[:, a], n_scc[:, a], valid_c, ALU.mult))
                v.tensor_tensor(n_scc[:, a], n_scc[:, a], c_sum[:, a, :].unsqueeze(2).to_broadcast([P, TT, CPAD]), ALU.mult).then_inc(c_scaled, 1)
                for br in range(2):
                    u = 2 * br + a
                    dve.wait_ge(n_exp, 4 * h + 2 * br + 2)
                    then(v.reciprocal(n_coef[:, u, :], n_sum[:, u, :]))
                    then(v.tensor_tensor(n_coef[:, u, :], n_coef[:, u, :], gate(1 + br), ALU.mult))
                    for t in range(TT):
                        v.tensor_scalar(n_sc[u][:, t, :], n_sc[u][:, t, :], n_coef[:, u, t:t + 1], None, ALU.mult).then_inc(n_scaled, 1)

            def nsa_out(i):
                dve.wait_ge(o_hi, PAIRS + i + 1)
                v.tensor_tensor(ol[:, 1, bass.ds(i, 1), :], bank(2)[:, 0:T].rearrange("p (a t) -> p a t", a=1),
                                oh[:, 1, bass.ds(i, 1), :].bitcast(F32), ALU.subtract).then_inc(o_lo, 1)

            def nsa_pair(i, more):
                c = 2 * SCORE_LINKS + 2 * (SCORE_LINKS + SCALE_LINKS) * i
                for a in range(2):
                    nsa_scale(2 * i + a, i, a, c + a * SCALE_LINKS)
                if not isinstance(i, int) or i > 0:
                    nsa_out(i - 1)
                c = c + 2 * SCALE_LINKS
                if more:
                    for a in range(2):
                        nsa_scores(2 * i + 2 + a, i + 1, a, c + a * SCORE_LINKS)

            for a in range(2):
                nsa_scores(a, 0, a, a * SCORE_LINKS)
            skewed(dve, PAIRS, nsa_pair)
            nsa_out(PAIRS - 1)

            h0 = FIRST["hg"]
            flat = lambda w, j: w[:, 2 * j:2 * j + 2, :].rearrange("p a t -> p (a t)")
            for j in range(2):
                split(h0 + j + 2)
                dve.wait_ge(evacuated, EVAC[h0 + j + 1])
                v.tensor_tensor(flat(hg_q, j), flat(hg_q, j), hg_t.rearrange("p a t -> p (a t)"), ALU.mult).then_inc(h_silu, 1)
            for j in range(4):
                split(h0 + j + 4)
            dve.wait_ge(evacuated, EVAC[h0 + 4])
            v.tensor_scalar(hg_k, hg_f, -1.0, 1.0, ALU.mult, ALU.add).then_inc(h_silu, 1)
            dve.wait_ge(spread_loaded, 16)
            for j in range(2):
                split(h0 + j + 8)
                dve.wait_ge(evacuated, EVAC[h0 + 7 + j])
                gv = hg_g[:, :, j * PC:(j + 1) * PC]
                link(v.tensor_tensor(gv, gv, hg_t, ALU.mult))
                v.tensor_tensor(gv, gv, gb[:, j * PC:(j + 1) * PC].unsqueeze(1).to_broadcast([P, TT, PC]), ALU.mult).then_inc(h_silu, 1)
            dve.wait_ge(h_zero, 3)
            dve.wait_ge(h_silu, 5)

            def hg_head(i):
                c = 14 * i
                done = [0]

                def then(ins, n=1):
                    ins.then_inc(h_chain, 1)
                    done[0] += 1

                def sync():
                    dve.wait_ge(h_chain, c + done[0])

                one = lambda w: w[:, bass.ds(i, 1), :].rearrange("p a t -> p (a t)")
                q, f, k, s = one(hg_q), one(hg_f), one(hg_k), one(hg_s)
                wait(dve, h_scored, i)
                v.tensor_copy(q_lev[:, 0, :], q).then_inc(h_lev, 1)
                v.tensor_copy(k_lev[:, 0, :], k).then_inc(h_lev, 1)
                for l in range(1, LEVELS + 1):
                    h = 2 ** (l - 1)
                    half = lambda w, r: w.rearrange("p (b r h) -> p b r h", r=2, h=h)[:, :, r, :]
                    if l < LEVELS:
                        qo, ko = half(q_lev[:, l, :], 1), half(k_lev[:, l, :], 0)
                    else:
                        qo, ko = q_x.unsqueeze(1), k_x.unsqueeze(1)
                    v.tensor_tensor(qo, half(q, 1), half(f, 1), ALU.mult).then_inc(h_lev, 1)
                    v.tensor_tensor(ko, half(k, 0), half(s, 0), ALU.mult).then_inc(h_lev, 1)
                    if l == LEVELS:
                        break
                    n = T // (2 * h)
                    left = half(f, 0)[:, :, h - 1:h].to_broadcast([P, n, h])
                    right = half(f, 1)[:, :, h - 1:h].to_broadcast([P, n, h])
                    dve.wait_ge(h_lev, 18 * i + 2 * l + 2)
                    then(v.tensor_tensor(half(s, 0), half(s, 0), right, ALU.mult))
                    sync()
                    then(v.tensor_tensor(half(f, 1), half(f, 1), left, ALU.mult))
                    sync()
                for t in range(TT):
                    dve.wait_ge(h_scored, i + 1)
                    wait(dve, h_out, i)
                    v.tensor_tensor(a_m[t], ACC[:, 2 * t:2 * t + 2, :].rearrange("p b (l t) -> p (b l) t", t=P), level_mask, ALU.mult).then_inc(h_masked, 1)

            peeled(dve, HG_HEADS, hg_head)
            k = NIDX["hg"]
            heads = lambda w: w.rearrange("p t (h d) -> p (t h) d", d=P)
            dve.wait_ge(h_o_ready, HG_HEADS)
            dve.wait_ge(h_out, HG_HEADS)
            sq = xn[:, 0, :].rearrange("p (a d) -> p a d", d=P)
            link(v.tensor_tensor(sq, heads(hg_o), heads(hg_o), ALU.mult))
            for t in range(TT):
                own = slice(t * HG_HEADS, (t + 1) * HG_HEADS)
                v.tensor_reduce(ss[:, k, own], sq[:, own, :], AX.X, ALU.add).then_inc(sumsq[t], 1)
            for t in range(TT):
                own = slice(t * HG_HEADS, (t + 1) * HG_HEADS)
                dve.wait_ge(rstd_ready[t], k + 1)
                link(v.tensor_tensor(heads(hg_o)[:, own], heads(hg_o)[:, own], rstd[:, k, own].unsqueeze(2).to_broadcast([P, HG_HEADS, P]), ALU.mult))
                v.tensor_tensor(hg_o[:, t, :], hg_o[:, t, :], hg_g[:, t, :], ALU.mult).then_inc(rows_ready[t], 1)
            turn("hg", oh[:, 2, :, :], ol[:, 2, :, :], None)

            dve.wait_ge(m_zero, 1)

            def merge(b):
                for half in range(2):
                    p = FIRST["merge"] + 3 * half
                    split(p + 2, 6, b)
                    split(p + 3, 6, b)
                    split(p + 4, 6, b)
                    u = 2 * b + half
                    dve.wait_ge(panel_used, p + 6 * b + 3)
                    wait(dve, m_added, u - 1)
                    v.tensor_tensor(m_tmp[half].rearrange("p (b f) t -> p b (f t)", b=2), gm[half].rearrange("p (b f) t -> p b (f t)", b=2),
                                    ACC[:, 2 * half:2 * half + 2, :], ALU.mult).then_inc(m_mul, 1)
                    dve.wait_ge(m_mul, u + 1)
                    v.tensor_tensor(m_t[:, 4 * half:4 * half + 4, :], m_t[:, 4 * half:4 * half + 4, :], m_tmp[half], ALU.add).then_inc(m_added, 1)

            peeled(dve, 3, merge)

            for half in range(2):
                f = slice(4 * half, 4 * half + 4)
                dve.wait_ge(m_hi, half + 1)
                v.tensor_tensor(xl[:, f, :], m_t[:, f, :], xh[:, f, :].bitcast(F32), ALU.subtract).then_inc(m_lo, 1)
            for j in range(4):
                p = FIRST["w_out"] + j
                split(p + 2)
                dve.wait_ge(panel_used, p + 1)
                xc = x[:, :, j * PC:(j + 1) * PC]
                v.tensor_tensor(xc, xc, bank(BANK[p]).rearrange("p (t n) -> p t n", t=TT), ALU.add).then_inc(evacuated, 1)

            dve.wait_ge(evacuated, EVAC[FIRST["peer_q"]])
            norm_rows("peer")
            turn("peer", xh, xl, "peer")
            dve.wait_ge(turned, XEND["peer"])
            dve.wait_ge(spread_loaded, 16 * 2)
            for t in range(TT):
                dve.wait_ge(rows_ready[t], XIDX["peer"] + 1)
                v.tensor_tensor(xn[:, t, :], xn[:, t, :], gb[:, :], ALU.mult).then_inc(gain_used, 1)
            dve.wait_ge(gain_used, TT)
            p0 = FIRST["peer_q"]
            for j in range(3):
                split(p0 + j + 2)

            def best(n, t, h):
                c = 44 * n
                done = [0]

                def then(ins):
                    done[0] += 1
                    ins.then_inc(pe_chain, 1)

                def sync():
                    dve.wait_ge(pe_chain, c + done[0])
                    then(v.tensor_copy(pe_carrier, minus_half[:, 0:1]))

                def top16(src, vals, idx):
                    for a in range(len(src)):
                        then(v.max(vals[a][:, 0:8], src[a]))
                    sync()
                    for a in range(len(src)):
                        then(v.max_index(idx[a][:, 0:8], vals[a][:, 0:8], src[a]))
                    sync()
                    for a in range(len(src)):
                        then(v.match_replace(src[a], vals[a][:, 0:8], src[a], -3e38))
                    sync()
                    for a in range(len(src)):
                        then(v.max(vals[a][:, 8:16], src[a]))
                    sync()
                    for a in range(len(src)):
                        then(v.max_index(idx[a][:, 8:16], vals[a][:, 8:16], src[a]))
                    sync()

                wait(dve, exp_done, n)
                scores = PS[:, :, :].rearrange("p (a g) (h k) -> p a (g h) k", a=2, h=PE_HEADS // 2) if t else pe_sc
                then(v.tensor_copy(pe_s, scores[:, :, bass.ds(h, 1), :].rearrange("p a h k -> p a (h k)")))
                sync()
                top16([pe_s[:, a, :] for a in range(2)], [pe_tv[:, a, :] for a in range(2)], [pe_ti[:, a, :] for a in range(2)])
                then(v.tensor_copy(pe_tif, pe_ti))
                then(v.tensor_tensor(pe_cand, pe_tv[:, 0, :].unsqueeze(2).to_broadcast([P, PE_K, PE_K]),
                                     pe_tv[:, 1, :].unsqueeze(1).to_broadcast([P, PE_K, PE_K]), ALU.add))
                sync()
                top16([pe_cand.rearrange("p i j -> p (i j)")], [pe_best], [pe_pos])
                v.tensor_scalar(pe_nb, pe_best[:, 0:1], -1.0, None, ALU.mult).then_inc(best_ready, 1)
                then(v.tensor_scalar(pe_hl[:, 0, :], pe_pos, 4, None, ALU.logical_shift_right))
                then(v.tensor_scalar(pe_hl[:, 1, :], pe_pos, 15, None, ALU.bitwise_and))
                sync()
                then(v.tensor_copy(pe_hlf, pe_hl))
                sync()
                for a in range(2):
                    then(v.tensor_tensor(pe_hot[a], iota16[:, :].unsqueeze(1).to_broadcast([P, PE_K, PE_K]),
                                         pe_hlf[:, a, :].unsqueeze(2).to_broadcast([P, PE_K, PE_K]), ALU.is_equal))
                sync()
                for a in range(2):
                    then(v.tensor_tensor(pe_hot[a], pe_hot[a], pe_tif[:, a, :].unsqueeze(1).to_broadcast([P, PE_K, PE_K]), ALU.mult))
                sync()
                for a in range(2):
                    then(v.tensor_reduce(pe_e[:, a, :], pe_hot[a], AX.X, ALU.add))
                sync()
                v.scalar_tensor_tensor(out=pe_idx[:, bass.ds(n * PE_K, PE_K)], in0=pe_e[:, 0, :], scalar=float(PE_KEYS), in1=pe_e[:, 1, :],
                                       op0=ALU.mult, op1=ALU.add).then_inc(idx_ready, 1)
                assert done[0] == 44, done

            def dots(n, t):
                wait(dve, gelu_done, n)
                for k in range(PE_K):
                    slot = k % RING
                    dve.wait_ge(u_landed[slot], 16 * (PE_K // RING * n + k // RING + 1))
                    v.scalar_tensor_tensor(out=u_ring[slot], in0=u_ring[slot], scalar=1.0, in1=xn[:, t, :], op0=ALU.mult, op1=ALU.mult,
                                           accum_out=pe_h[:, k:k + 1]).then_inc(u_used, 1)

            def weights(n):
                dve.wait_ge(exp_done, n + 1)
                v.reciprocal(pe_rec, pe_sum[:, bass.ds(n, 1)]).then_inc(pe_chain2, 1)
                dve.wait_ge(pe_chain2, 2 * n + 1)
                v.tensor_scalar(pe_gate, pe_exp[:, bass.ds(n * PE_K, PE_K)], pe_rec, None, ALU.mult).then_inc(pe_chain2, 1)
                dve.wait_ge(pe_chain2, 2 * n + 2)
                wait(dve, diag_ready, PE_K * n)
                dve.wait_ge(gelu_done, n + 1)
                v.tensor_tensor(pe_act, pe_gate, pe_gelu, ALU.mult).then_inc(act_ready, 1)

            dve.wait_ge(pe_sc_ready, 2)
            best(0, 0, 0)
            best(1, 0, 1)
            dve.wait_ge(pe_sc_ready, PE_HEADS)
            dots(0, 0)
            weights(0)
            with dve.Fori(1, PE_HEADS - 1) as n:
                best(n + 1, 0, n + 1)
                dots(n, 0)
                weights(n)
            dve.wait_ge(pe_scored, PE_HEADS // 2 + 1)
            n = PE_HEADS - 1
            best(n + 1, 1, 0)
            dots(n, 0)
            weights(n)
            with dve.Fori(PE_HEADS, UNITS - 1) as n:
                best(n + 1, 1, n + 1 - PE_HEADS)
                dots(n, 1)
                weights(n)
            dots(UNITS - 1, 1)
            weights(UNITS - 1)
            dve.wait_ge(spread_loaded, 16 * 3)
            for t in range(TT):
                dve.wait_ge(v_used, PE_K * PE_HEADS * (t + 1))
                v.tensor_tensor(x[:, t, :], x[:, t, :], ACC[:, 2 * t:2 * t + 2, :].rearrange("p b n -> p (b n)"), ALU.add).then_inc(x_updated, 1)
                dve.wait_ge(x_updated, 2 * t + 1)
                k = NIDX["final"]
                square(x[:, t, :], xn[:, t, :], ss[:, k, t:t + 1]).then_inc(sumsq[t], 1)
                dve.wait_ge(rstd_ready[t], k + 1)
                v.scalar_tensor_tensor(out=x[:, t, :], in0=x[:, t, :], scalar=rstd[:, k, t:t + 1], in1=gb[:, :],
                                       op0=ALU.mult, op1=ALU.mult).then_inc(x_updated, 1)
                dve.wait_ge(x_updated, 2 * t + 2)
                k = NIDX["f0"]
                square(x[:, t, :], xn[:, t, :], ss[:, k, t:t + 1]).then_inc(sumsq[t], 1)
                dve.wait_ge(rstd_ready[t], k + 1)
                v.tensor_scalar(xn[:, t, :], x[:, t, :], rstd[:, k, t:t + 1], None, ALU.mult).then_inc(rows_ready[t], 1)
            turn("f0", xh, xl, "f0")
            split(FIRST["ffn0"] + 1)

            def ffn(f):
                p0 = FIRST[f"ffn{f}"]
                last = p0 + 3 * FF_STEPS - 1

                def product(p, i, m=0, r=0):
                    dve.wait_ge(evacuated, along(EVAC, p, m, r))
                    dve.wait_ge(panel_used, p + m * r + 1)
                    wait(dve, ff_lo, FF_STEPS * f + i)
                    v.tensor_tensor(ff_a.rearrange("p f t -> p (f t)"), ff_s.rearrange("p f t -> p (f t)"), bank(BANK[p]), ALU.mult)\
                        .then_inc(evacuated, 1)

                def rest(i):
                    dve.wait_ge(ff_hi, FF_STEPS * f + i + 1)
                    v.tensor_tensor(al[:, :, :], ff_a, ah[:, :, :].bitcast(F32), ALU.subtract).then_inc(ff_lo, 1)

                split(p0 + 2)
                split(p0 + 3)
                product(p0 + 1, 0)
                rest(0)

                def step(i, next_up=True):
                    split(p0 + 4, 3, i - 1)
                    split(p0 + 5, 3, i - 1)
                    product(p0 + 3, i, 3, i - 1)
                    if next_up:
                        split(p0 + 6, 3, i - 1)
                    rest(i)

                with dve.Fori(1, FF_STEPS - 1) as i:
                    step(i)
                step(FF_STEPS - 1, last + 1 < NP)
                if last + 2 < NP:
                    split(last + 2)

            def post(name):
                k, after = NIDX[name], dict(POSTS)[name]
                u = TT * (1 + [n for n, _ in POSTS].index(name))
                dve.wait_ge(spread_loaded, 16 * (SPREAD.index(name) + 1))
                dve.wait_ge(turned, XBASE[after] if after else XEND["f3"])
                for t in range(TT):
                    dve.wait_ge(sumsq[t], k + 1)
                    v.tensor_tensor(xn[:, t, :], ACC[:, 2 * t:2 * t + 2, :].rearrange("p b n -> p (b n)"), gb[:, :], ALU.mult).then_inc(gain_used, 1)
                    dve.wait_ge(gain_used, u + t + 1)
                    dve.wait_ge(rstd_ready[t], k + 1)
                    v.scalar_tensor_tensor(out=x[:, t, :], in0=xn[:, t, :], scalar=rstd[:, k, t:t + 1], in1=x[:, t, :],
                                           op0=ALU.mult, op1=ALU.add).then_inc(x_updated, 1)
                if after is None:
                    return
                k = NIDX[after]
                dve.wait_ge(x_updated, X_AT[name])
                square(x[:, 1, :], xn[:, 1, :], ss[:, k, 1:2]).then_inc(sumsq[1], 1)
                dve.wait_ge(rstd_ready[1], k + 1)
                v.tensor_scalar(xn[:, 1, :], x[:, 1, :], rstd[:, k, 1:2], None, ALU.mult).then_inc(rows_ready[1], 1)
                turn(after, xh, xl, after)

            ffn(0)
            post("p0")
            p0 = FIRST["conv_in"]
            dve.wait_ge(cv_pad, 1)

            def conv(j):
                c = 5 * j
                done = [0]

                def then(ins, n=1):
                    done[0] += n
                    ins.then_inc(cv_chain, n)
                    dve.wait_ge(cv_chain, c + done[0])

                for w in range(3):
                    split(p0 + w + 2, 3, j)
                dve.wait_ge(evacuated, along(EVAC, p0 + 2, 3, j))
                dve.wait_ge(panel_used, p0 + 3 * j + 3)
                v.tensor_tensor(cv_u[:, :, CONV_W - 1:], cv_c, bank(BANK[p0 + 2]).rearrange("p (f t) -> p f t", f=2), ALU.mult).then_inc(evacuated, 1)
                dve.wait_ge(evacuated, along(EVAC, p0 + 3, 3, j))
                wait(dve, cv_lo, j)
                tap = lambda w, f: cols[:, bass.ds(2 * j + (TAPS + w * KD + f), 1)]
                v.tensor_scalar(cv_z[:, 0, :], cv_u[:, 0, 2:2 + T], tap(2, 0), None, ALU.mult)
                then(v.tensor_scalar(cv_z[:, 1, :], cv_u[:, 1, 2:2 + T], tap(2, 1), None, ALU.mult))
                for w in (1, 0):
                    for f in range(2):
                        then(v.scalar_tensor_tensor(out=cv_z[:, f, :], in0=cv_u[:, f, w:w + T], scalar=tap(w, f), in1=cv_z[:, f, :],
                                                    op0=ALU.mult, op1=ALU.add))
                v.tensor_tensor(cv_z, cv_z, cv_b, ALU.mult).then_inc(cv_y, 1)
                dve.wait_ge(cv_hi, j + 1)
                v.tensor_tensor(yl[:, bass.ds(2 * j, 2), :], cv_z, yh[:, bass.ds(2 * j, 2), :].bitcast(F32), ALU.subtract).then_inc(cv_lo, 1)
                assert done[0] == 5

            peeled(dve, 4, conv)
            for j in range(4):
                split(FIRST["conv_out"] + j + 2)
            post("pc")
            ffn(1)
            post("p1")
            for j in range(8):
                split(FIRST["kv"] + j + 2)
            turn("f2", xh, xl, "f2")
            ffn(2)
            post("p2")
            for j in range(4):
                split(FIRST["q"] + j + 2)
            dve.wait_ge(lam_loaded, 64)
            for a in range(2):
                v.scalar_tensor_tensor(out=lam_in[:, 2 * a, :], in0=lam_in[:, 2 * a, :], scalar=1.0, in1=lam_in[:, 2 * a + 1, :], op0=ALU.mult,
                                       op1=ALU.mult, accum_out=lam_dot[:, a:a + 1]).then_inc(lam_dots, 1)
            dve.wait_ge(lam_exped, 1)
            link(v.tensor_tensor(lam, lam_exp[:, 1:2], lam_exp[:, 0:1], ALU.subtract))
            link(v.tensor_scalar(lam, lam, -LAMBDA_INIT, None, ALU.add))

            DIFF_SCORE_LINKS, DIFF_MIX_LINKS = 4, 3

            def diff_links(before):
                done = [before]

                def then(ins):
                    done[0] = done[0] + 1
                    ins.then_inc(df_chain, 1)
                    dve.wait_ge(df_chain, done[0])
                return then

            def diff_scores(h, b, before):
                then = diff_links(before)
                wait(dve, df_turned, h - 1)
                for c in range(2):
                    u = 2 * b + c
                    dve.wait_ge(df_scored, 2 * h + c + 1)
                    then(v.tensor_tensor(df_sc[u].rearrange("p t s -> p (t s)"), bank(4 + u), causal.rearrange("p t s -> p (t s)"), ALU.add))
                    then(v.tensor_reduce(df_mx[:, u, :], df_sc[u], AX.X, ALU.max))
                    v.tensor_scalar(df_mx[:, u, :], df_mx[:, u, :], -1.0, None, ALU.mult).then_inc(df_max, 1)

            def diff_mix(h, b, before):
                then = diff_links(before)
                p, q = 2 * b, 2 * b + 1
                dve.wait_ge(df_exp, 4 * h + 4)
                then(v.reciprocal(df_r[:, p:q + 1, :], df_sum[:, p:q + 1, :]))
                then(v.tensor_scalar(df_r[:, q, :], df_r[:, q, :], lam, None, ALU.mult))
                v.tensor_scalar(df_sc[p][:, 0, :], df_sc[p][:, 0, :], df_r[:, p, 0:1], None, ALU.mult)
                then(v.tensor_scalar(df_sc[p][:, 1, :], df_sc[p][:, 1, :], df_r[:, p, 1:2], None, ALU.mult))
                for t in range(TT):
                    v.scalar_tensor_tensor(out=df_sc[p][:, t, :], in0=df_sc[q][:, t, :], scalar=df_r[:, q, t:t + 1], in1=df_sc[p][:, t, :],
                                           op0=ALU.mult, op1=ALU.add).then_inc(df_mixed, 1)

            def diff_pair(i, more):
                c = 2 * DIFF_SCORE_LINKS + 2 * (DIFF_SCORE_LINKS + DIFF_MIX_LINKS) * i
                for b in range(2):
                    diff_mix(2 * i + b, b, c + b * DIFF_MIX_LINKS)
                c = c + 2 * DIFF_MIX_LINKS
                if more:
                    for b in range(2):
                        diff_scores(2 * i + 2 + b, b, c + b * DIFF_SCORE_LINKS)

            dve.wait_ge(tables, N_TABLES + 2)
            for b in range(2):
                diff_scores(b, b, b * DIFF_SCORE_LINKS)
            skewed(dve, DIFF_HEADS // 2, diff_pair)
            k = NIDX["diff"]
            heads = lambda w: w.rearrange("p t (h e) -> p (t h) e", e=P)
            dve.wait_ge(df_o_ready, DIFF_HEADS)
            link(v.tensor_tensor(xn[:, :, :], df_o, df_o, ALU.mult))
            for t in range(TT):
                own = slice(t * DIFF_HEADS, (t + 1) * DIFF_HEADS)
                v.tensor_reduce(ss[:, k, own], heads(xn[:, :, :])[:, own], AX.X, ALU.add).then_inc(sumsq[t], 1)
            dve.wait_ge(spread_loaded, 16 * (SPREAD.index("diff") + 1))
            for t in range(TT):
                own = slice(t * DIFF_HEADS, (t + 1) * DIFF_HEADS)
                o = heads(df_o)[:, own]
                dve.wait_ge(rstd_ready[t], k + 1)
                link(v.tensor_tensor(o, o, rstd[:, k, own].unsqueeze(2).to_broadcast([P, DIFF_HEADS, P]), ALU.mult))
                v.tensor_tensor(o, o, gb[:, 0:P].unsqueeze(1).to_broadcast([P, DIFF_HEADS, P]), ALU.mult).then_inc(rows_ready[t], 1)
            turn("diff", xh, xl, None)
            for j in range(4):
                split(FIRST["o"] + j + 2)
            post("pa")
            ffn(3)
            post("p3")

        @block.tensor
        def _(pe):
            def mm(out, l, r, first, last):
                return nc.tensor.matmul(out, l, r, start=first, stop=last)

            def begin(p, m=0, i=0):
                pe.wait_ge(lo_done, p + m * i + 1)
                if BANK[p] is not None:
                    wait(pe, evacuated, along(EVAC, p, m, i) - 1)

            def exact3(out, lh, ll, rh, rl, first, last):
                mm(out, lh, rh, first, False)
                mm(out, lh, rl, False, False)
                return mm(out, ll, rh, False, last)

            def views(p, kt):
                s = p % SLOTS
                return [w[s][:, :WORDS[p]].rearrange("p (k n) -> p k n", k=kt) for w in (hi, lo)]

            def feature_tile(p, f, out, kt=KD, rh=xh, rl=xl, stream=None):
                wh, wl = views(p, kt)
                c = slice(f * P, (f + 1) * P)
                for k in range(kt):
                    if stream:
                        pe.wait_ge(turned_lo, SBASE[stream] + k + 1)
                    last = exact3(out, wh[:, k, c], wl[:, k, c], rh[:, k, :], rl[:, k, :], k == 0, k == kt - 1)
                return last

            def token_tile(p, t, out, c=slice(0, PC), lh=xh, ll=xl):
                wh, wl = views(p, KD)
                r = slice(t * P, (t + 1) * P)
                for k in range(KD):
                    last = exact3(out, lh[:, k, r], ll[:, k, r], wh[:, k, c], wl[:, k, c], k == 0, k == KD - 1)
                return last

            def panel_a(p, m=0, i=0, stream=None):
                begin(p, m, i)
                for f in range(2):
                    last = feature_tile(p, f, bank(BANK[p])[:, f * T:(f + 1) * T], stream=None if f else stream)
                last.then_inc(panel_used, 1)

            def panel_b(p, m=0, i=0, n=PC):
                begin(p, m, i)
                for t in range(TT):
                    last = token_tile(p, t, bank(BANK[p])[:, t * n:(t + 1) * n], slice(0, n))
                last.then_inc(panel_used, 1)

            def turn(name, rows):
                if SBASE[name]:
                    pe.wait_ge(turned_lo, SBASE[name])
                for t in range(TT):
                    pe.wait_ge(rows_ready[t], XIDX[name] + 1)
                    for b in range(XEND[name] - XBASE[name]):
                        for j in range(2):
                            c = (2 * b + j) * P
                            last = nc.tensor.transpose(ACC[:, b, j * T + t * P:j * T + (t + 1) * P], rows[:, t, c:c + P], ident[:, :])
                        if t == TT - 1:
                            last.then_inc(turned, 1)

            pe.wait_ge(tables, 2)
            pe.wait_ge(cols_loaded, 16 * 14)
            nc.tensor.transpose(bank(3)[:, 0:96], rowbuf[0:96, 0, :], ident[0:96, 0:96])
            nc.tensor.transpose(bank(3)[:, 96:128], rowbuf[0:CMP_LEN, 1, :], ident[0:CMP_LEN, 0:CMP_LEN])
            nc.tensor.transpose(bank(3)[:, 128:256], rowbuf[:, 2, :], ident[:, :]).then_inc(cols_turned, 1)
            turn("mix", xn)
            for p in range(4):
                panel_a(p, stream=None if p else "mix")
            for p in range(4, 6):
                panel_b(p)

            pe.wait_ge(tables, SB_TABLES)

            def sb_pair(i):
                pe.wait_ge(sb_staged, 3 * i + 2)
                for a in range(2):
                    r = slice(a * HD, (a + 1) * HD)
                    wait(pe, sb_sig, 4 * i + 2 * a - 2)
                    for t in range(TT):
                        out = bank(4 + a)[:, t * T:(t + 1) * T]
                        mm(out, q_st[r, t * P:(t + 1) * P], k_st[r, :], True, False)
                        last = mm(out, ident[:, :], strict[:, t, :], False, True)
                    last.then_inc(sb_scored, 1)
                for a in range(2):
                    pe.wait_ge(sb_attn, 2 * i + a + 1)
                    wait(pe, sb_pt_ready, 2 * i + a - 1)
                    for n, (t, s) in enumerate(((0, 0), (1, 0), (1, 1))):
                        last = nc.tensor.transpose(bank(6 + a)[:, n * P:(n + 1) * P], sb_a[a][:, t, s * P:(s + 1) * P], ident[:, :])
                    last.then_inc(sb_turned, 1)
                pe.wait_ge(sb_staged, 3 * i + 3)
                wait(pe, o_lo, i)
                for a in range(2):
                    r = slice(a * HD, (a + 1) * HD)
                    pe.wait_ge(sb_pt_ready, 2 * i + a + 1)
                    mm(bank(3)[r, 0:P], v_st[:, 0, r], sb_pt[a][:, 0, :], True, True)
                    mm(bank(3)[r, P:T], v_st[:, 0, r], sb_pt[a][:, 1, :], True, False)
                    mm(bank(3)[r, P:T], v_st[:, 1, r], sb_pt[a][:, 2, :], False, True).then_inc(sb_out, 1)

            peeled(pe, PAIRS, sb_pair)

            q0, c0, g0 = FIRST["nsa_q"], FIRST["nsa_kv"], FIRST["nsa_gate"]
            for j in range(2):
                panel_a(q0 + j)
            panel_a(c0)
            for j in range(2):
                p = c0 + 1 + j
                begin(p)
                b = bank(BANK[p])
                feature_tile(p, 0, b[:, 0:T])
                for t in range(TT):
                    last = token_tile(p, t, b[:, T + t * P:T + (t + 1) * P], slice(P, 2 * P))
                last.then_inc(panel_used, 1)
            panel_b(g0, n=N_GATES)
            pe.wait_ge(n_blk, 4)
            pe.wait_ge(wcmp_loaded, 64)
            pe.wait_ge(o_lo, PAIRS)
            for g in range(2):
                r = slice(g * HD, (g + 1) * HD)
                for l in range(CMP_LEN):
                    mm(bank(2)[r, 0:N_CMP], wcmp_k[r, l, :], cmp_blk[r, 0, l, :], l == 0, l == CMP_LEN - 1)
                for l in range(CMP_LEN):
                    last = mm(bank(3 + g)[0:N_CMP, 0:HD], cmp_blk[r, 1, l, :], wcmp_v[r, l, :], l == 0, l == CMP_LEN - 1)
            last.then_inc(n_kc, 1)
            pe.wait_ge(n_kc_ready, 3)
            pe.wait_ge(evacuated, EVAC[FIRST["hg"]])

            def nsa_scores(h, i, a):
                pe.wait_ge(n_staged, i + 1)
                r = slice(a * HD, (a + 1) * HD)
                for br, key in enumerate((n_ksel, n_kwin)):
                    wait(pe, n_max, 2 * h - 3 + br)
                    for t in range(TT):
                        last = mm(bank(4 + 2 * a + br)[:, t * T:(t + 1) * T], nq_st[r, t * P:(t + 1) * P], key[r, :], True, True)
                    last.then_inc(n_scored, 1)

            def nsa_cmp_scores(h, i, a):
                r = slice(a * HD, (a + 1) * HD)
                wait(pe, c_shift, h)
                wait(pe, n_pt_ready, 6 * i)
                for t in range(TT):
                    c = T + t * CPAD
                    last = mm(bank(3)[:, c:c + CPAD], nq_st[r, t * P:(t + 1) * P], kc[r, 0:CPAD], True, True)
                last.then_inc(c_scored, 1)

            def nsa_turn(h, a):
                wait(pe, n_pt_ready, 3 * h)
                for br in range(2):
                    pe.wait_ge(n_scaled, 4 * h + 2 * br + 2)
                    for n, (t, s) in enumerate(((0, 0), (1, 0), (1, 1))):
                        last = nc.tensor.transpose(bank(br)[:, n * P:(n + 1) * P], n_sc[2 * br + a][:, t, s * P:(s + 1) * P], ident[:, :])
                    last.then_inc(n_turned, 1)
                pe.wait_ge(c_scaled, h + 1)
                for t in range(TT):
                    last = nc.tensor.transpose(bank(3)[0:CPAD, t * P:(t + 1) * P], n_scc[:, a, t, :], ident[:, :])
                last.then_inc(n_turned, 1)

            def nsa_sum(h, i, a):
                pe.wait_ge(n_pt_ready, 3 * h + 3)
                if a == 0:
                    wait(pe, o_lo, PAIRS + i)
                r = slice(a * HD, (a + 1) * HD)
                for t in range(TT):
                    out = bank(2)[r, t * P:(t + 1) * P]
                    mm(out, vc[0:CPAD, a, :], n_ptc[0:CPAD, a, t, :], True, False)
                    for br, val in enumerate((n_vsel, n_vwin)):
                        pt = n_pt[2 * br + a]
                        for s in range(t + 1):
                            last = mm(out, val[:, s, r], pt[:, t + s, :], False, br == 1 and s == t)
                last.then_inc(n_out, 1)

            def nsa_pair(i, more):
                if more:
                    for a in range(2):
                        nsa_scores(2 * i + 2 + a, i + 1, a)
                for a in range(2):
                    nsa_turn(2 * i + a, a)
                if more:
                    nsa_cmp_scores(2 * i + 2, i + 1, 0)
                for a in range(2):
                    nsa_sum(2 * i + a, i, a)
                if more:
                    nsa_cmp_scores(2 * i + 3, i + 1, 1)

            for a in range(2):
                nsa_scores(a, 0, a)
                nsa_cmp_scores(a, 0, a)
            skewed(pe, PAIRS, nsa_pair)

            h0 = FIRST["hg"]
            for j in range(4):
                panel_a(h0 + j)
            for j in range(4, 8):
                panel_b(h0 + j)

            def hg_head(i):
                if isinstance(i, int):
                    pe.wait_ge(evacuated, EVAC[FIRST["merge"]])
                    pe.wait_ge(o_lo, 2 * PAIRS)
                for l in range(LEVELS):
                    pe.wait_ge(h_lev, 18 * i + 2 * l + 2)
                    for t in range(TT):
                        c = slice(t * P, (t + 1) * P)
                        mm(ACC[:, 2 * t + l // 4, (l % 4) * P:(l % 4 + 1) * P], k_lev[:, l, c], q_lev[:, l, c], True, True)
                pe.wait_ge(h_lev, 18 * i + 18)
                wait(pe, h_cross, i)
                mm(bank(3)[:, 0:P], k_x, q_x, True, True).then_inc(h_scored, 1)
                wait(pe, h_o_ready, i)
                for t in range(TT):
                    pe.wait_ge(h_masked, 2 * i + t + 1)
                    out = bank(2)[:, t * P:(t + 1) * P]
                    for l in range(LEVELS):
                        last = mm(out, a_m[t][:, l, :], hg_i[:, t, bass.ds(i * P, P)], l == 0, l == LEVELS - 1 and t == 0)
                pe.wait_ge(h_cross, i + 1)
                mm(out, a_x, hg_i[:, 0, bass.ds(i * P, P)], False, True).then_inc(h_out, 1)

            peeled(pe, HG_HEADS, hg_head)
            turn("hg", hg_o)

            pe.wait_ge(turned_lo, SEND["hg"])

            def merge(b):
                for half in range(2):
                    p = FIRST["merge"] + 3 * half
                    for j in range(2):
                        panel_a(p + j, 6, b)
                    begin(p + 2, 6, b)
                    wait(pe, m_mul, 2 * b + half - 1)
                    rh = oh[:, bass.ds(b, 1)].rearrange("p a k t -> p (a k) t")
                    rl = ol[:, bass.ds(b, 1)].rearrange("p a k t -> p (a k) t")
                    for f in range(4):
                        last = feature_tile(p + 2, f, ACC[:, 2 * half + f // 2, (f % 2) * T:(f % 2 + 1) * T], PAIRS, rh, rl)
                    last.then_inc(panel_used, 1)

            peeled(pe, 3, merge)

            pe.wait_ge(m_lo, 2)
            for j in range(4):
                panel_b(FIRST["w_out"] + j)

            turn("peer", xn)
            def peer_scores(out, t, heads):
                for h in heads:
                    for a in range(2):
                        r = slice(a * HD, (a + 1) * HD)
                        last = mm(out[:, 2 * a + h // 4, (h % 4) * P:(h % 4 + 1) * P], pe_q[r, h, t * P:(t + 1) * P], cols[r, P:2 * P], True, True)
                last.then_inc(pe_scored, 1)

            def first_scores(j):
                pe.wait_ge(evacuated, EVAC[FIRST["peer_q"]] + j + 1)
                wait(pe, pe_sc_ready, 2 * j)
                peer_scores(ACC, 0, (2 * j, 2 * j + 1))

            for j in range(4):
                panel_a(FIRST["peer_q"] + j, stream=None if j else "peer")
                if j:
                    first_scores(j - 1)
            first_scores(3)
            peer_scores(PS, 1, range(PE_HEADS))
            pe.wait_ge(pe_sc_ready, PE_HEADS)
            for t in range(TT):
                def expert_sums(n, first=False, final=False):
                    for k in range(PE_K):
                        slot = k % RING
                        pe.wait_ge(diag_ready, PE_K * n + k + 1)
                        pe.wait_ge(v_landed[slot], 16 * (PE_K // RING * n + k // RING + 1))
                        for half in range(2):
                            last = mm(ACC[:, 2 * t + half, :], diag[:, k % DIAGS, :], v_ring[slot][:, half * 512:(half + 1) * 512],
                                      first and k == 0, final and k == PE_K - 1)
                        last.then_inc(v_used, 1)

                n0 = t * PE_HEADS
                expert_sums(n0, first=True)
                with pe.Fori(n0 + 1, n0 + PE_HEADS - 1) as n:
                    expert_sums(n)
                expert_sums(n0 + PE_HEADS - 1, final=True)

            def ffn(f):
                p0 = FIRST[f"ffn{f}"]

                def down(p, i, m=0, r=0, first=False, final=False):
                    begin(p, m, r)
                    pe.wait_ge(ff_lo, FF_STEPS * f + i + 1)
                    wh, wl = views(p, 2)
                    for t in range(TT):
                        for half in range(2):
                            for k in range(2):
                                c, w = slice(t * P, (t + 1) * P), slice(half * 512, (half + 1) * 512)
                                last = exact3(ACC[:, 2 * t + half, :], ah[:, k, c], al[:, k, c], wh[:, k, w], wl[:, k, w],
                                              first and k == 0, final and k == 1)
                        if final and t == 0:
                            last.then_inc(branch_half, 1)
                    last.then_inc(panel_used, 1)

                panel_a(p0, stream=f"f{f}")
                panel_a(p0 + 1)
                panel_a(p0 + 2)
                panel_a(p0 + 3)
                down(p0 + 4, 0, first=True)
                with pe.Fori(2, FF_STEPS) as i:
                    panel_a(p0 + 2, 3, i - 1)
                    panel_a(p0 + 3, 3, i - 1)
                    down(p0 + 4, i - 1, 3, i - 1)
                down(p0 + 3 * FF_STEPS - 1, FF_STEPS - 1, final=True)

            def project(name, lh, ll):
                for j in range(4):
                    p = FIRST[name] + j
                    begin(p)
                    for t in range(TT):
                        last = token_tile(p, t, ACC[:, 2 * t + j // 2, (j % 2) * PC:(j % 2 + 1) * PC], lh=lh, ll=ll)
                        if j == 3 and t == 0:
                            last.then_inc(branch_half, 1)
                    last.then_inc(panel_used, 1)

            def turn_after(post):
                k = [n for n, _ in POSTS].index(post)
                pe.wait_ge(gain_used, TT * (k + 2))
                turn(POSTS[k][1], xn)

            for t in range(TT):
                pe.wait_ge(rows_ready[t], XIDX["f0"] + 1)
            turn("f0", xn)
            ffn(0)
            turn_after("p0")

            def conv(j):
                for w in range(3):
                    panel_a(FIRST["conv_in"] + w, 3, j, stream="conv" if w == 0 and isinstance(j, int) else None)

            peeled(pe, 4, conv)
            pe.wait_ge(cv_lo, 4)
            project("conv_out", yh, yl)
            turn_after("pc")
            ffn(1)
            turn_after("p1")
            for j in range(4):
                panel_a(FIRST["kv"] + j, stream=None if j else "kv")
            for j in range(4, 8):
                panel_b(FIRST["kv"] + j)
            ffn(2)
            turn_after("p2")
            for j in range(4):
                panel_a(FIRST["q"] + j, stream=None if j else "attn")

            def diff_scores(h, b):
                pe.wait_ge(df_staged, 2 * h + 2)
                for c in range(2):
                    u, r = 2 * b + c, slice(c * HD, (c + 1) * HD)
                    wait(pe, df_max, 2 * h - 3 + c)
                    for t in range(TT):
                        last = mm(bank(4 + u)[:, t * T:(t + 1) * T], df_qs[r, b, t * P:(t + 1) * P], df_ks[r, b, :], True, True)
                    last.then_inc(df_scored, 1)

            def diff_turn(h, b):
                pe.wait_ge(df_mixed, 2 * h + 2)
                wait(pe, df_pt_ready, h - 1)
                for n, (t, s) in enumerate(((0, 0), (1, 0), (1, 1))):
                    last = nc.tensor.transpose(bank(b)[:, n * P:(n + 1) * P], df_sc[2 * b][:, t, s * P:(s + 1) * P], ident[:, :])
                last.then_inc(df_turned, 1)

            def diff_values(h, b):
                pe.wait_ge(df_pt_ready, h + 1)
                wait(pe, df_o_ready, h - 1)
                out = bank(2 + b)
                val = lambda s: df_v[:, s, bass.ds(h * P, P)]
                mm(out[:, 0:P], df_pt[b][:, 0, :], val(0), True, True)
                mm(out[:, P:2 * P], df_pt[b][:, 1, :], val(0), True, False)
                mm(out[:, P:2 * P], df_pt[b][:, 2, :], val(1), False, True).then_inc(df_out, 1)

            def diff_pair(i, more):
                if more:
                    for b in range(2):
                        diff_scores(2 * i + 2 + b, b)
                for b in range(2):
                    diff_turn(2 * i + b, b)
                for b in range(2):
                    diff_values(2 * i + b, b)

            for b in range(2):
                diff_scores(b, b)
            skewed(pe, DIFF_HEADS // 2, diff_pair)
            turn("diff", df_o)
            pe.wait_ge(turned_lo, SEND["diff"])
            project("o", xh, xl)
            turn_after("pa")
            ffn(3)


def kernel(**inputs):
    import concourse.bacc as bacc
    from concourse.bass_utils import run_bass_kernel_spmd

    nc = bacc.Bacc("TRN2", target_bir_lowering=False, num_devices=1)
    arrays, io = {}, {}
    for name, a in inputs.items():
        a = np.ascontiguousarray(a)
        arrays[f"in_{name}"] = a
        io[name] = nc.dram_tensor(f"in_{name}", a.shape, mybir.dt.from_np(a.dtype), kind="ExternalInput").ap()
    io["out"] = nc.dram_tensor("out_0", (1, T, D), F32, kind="ExternalOutput").ap()
    build(nc, io)
    r = run_bass_kernel_spmd(nc, [arrays], core_ids=[0])
    return r.results[0]["out_0"]
```

```python
from contextlib import ExitStack

import concourse.bass as bass
import concourse.mybir as mybir
import numpy as np

F32, F32R = mybir.dt.float32, mybir.dt.float32r
U32 = mybir.dt.uint32
ALU = mybir.AluOpType
ACT = mybir.ActivationFunctionType
AX = mybir.AxisListType

P = 128
T, D = 256, 1024
TT = T // P
KD = D // P
HD = 64
EPS = 1e-6
NEG = -1e30
FAR = 1e32
SB_W = HG_W = 512
PAIRS = SB_W // P
BLOCKS = ((0, 0), (1, 0), (1, 1))
BW = len(BLOCKS) * P
KEYS = (slice(0, P), slice(P, BW))
CMP_LEN, CMP_STRIDE = 32, 16
N_CMP = T // CMP_STRIDE - 1
CPAD = N_CMP + 1
HG_HEADS = 4
LEVELS = 8
F_FF = 2816
FF_STEPS = F_FF // 256
CONV_W = 3
PANEL = 2048
PC = 256
SLOTS = 3
PE_HEADS, PE_K, PE_KEYS = 8, 16, 128
RING, GROUP = 8, 4
DIAGS = 8
LAMBDA_INIT = 0.8 - 0.6 * float(np.exp(-0.3))
DIFF_HEADS = 8

C_SBQ, C_SBK, C_SBV, C_NQ, C_CMP, C_SEL, C_WIN, C_NG = 0, 512, 1024, 1536, 2048, 2304, 2560, 2816
C_HQ, C_HF, C_HI, C_HG, C_MERGE = 2840, 3352, 3864, 4376, 4888
N_GATES = 24


def plan_panels():
    plan = []

    def add(name, count, pieces=1, words=PANEL, banks=(0, 1)):
        for j in range(count):
            b = banks[j % len(banks)] if banks else None
            plan.append((name, pieces, words, b))

    add("sb", 6)
    add("nsa_q", 2, pieces=4)
    add("nsa_kv", 3)
    add("nsa_gate", 1, words=KD * N_GATES, banks=(1,))
    add("hg", 8)
    for _ in range(3):
        for _ in range(2):
            add("merge", 2)
            add("branch", 1, pieces=2, banks=())
    add("w_out", 4)
    add("peer_q", 4)

    def ffn(name):
        for i in range(FF_STEPS):
            add(name, 2)
            if i:
                add(name, 1, banks=())
        add(name, 1, banks=())

    ffn("ffn0")
    add("conv_in", 12, banks=(0, 1, 2))
    add("conv_out", 4, banks=())
    ffn("ffn1")
    add("kv", 8)
    ffn("ffn2")
    add("q", 4)
    add("o", 4, banks=())
    ffn("ffn3")
    return plan


PLAN = plan_panels()
NP = len(PLAN)
FIRST = {}
for _p, _e in enumerate(PLAN):
    FIRST.setdefault(_e[0], _p)
BANK = [e[3] for e in PLAN]
WORDS = [e[2] for e in PLAN]
LANDED = [16 * sum(PLAN[q][1] for q in range(p % SLOTS, p + 1, SLOTS)) for p in range(NP)]
EVAC = [sum(b is not None for b in BANK[:p]) for p in range(NP + 1)]

XPOSE = [("mix", 4), ("hg", 2), ("peer", 4), ("f0", 4), ("conv", 4), ("f1", 4), ("kv", 4), ("attn", 4), ("diff", 4), ("f3", 4)]
XBASE = {n: sum(b for _, b in XPOSE[:k]) for k, (n, _) in enumerate(XPOSE)}
XEND = {n: XBASE[n] + b for n, b in XPOSE}
XIDX = {n: k for k, (n, _) in enumerate(XPOSE)}
_splits = [(n, 2 * b) for n, b in XPOSE]
_splits.insert(XIDX["kv"] + 1, ("f2", KD))
SBASE = {n: sum(b for _, b in _splits[:k]) for k, (n, _) in enumerate(_splits)}
SEND = {n: SBASE[n] + b for n, b in _splits}
GAIN = {n: KD * j for n, j in (("f0", 0), ("conv", 2), ("f1", 4), ("f2", 6), ("attn", 8), ("f3", 10))}
CMP_AT = KD * 12
GAIN.update(mix=P, peer=P + KD, kv=P + 2 * KD)
TAPS = P + 3 * KD
GAIN["diff"] = TAPS + CONV_W * KD
KEYS_AT = GAIN["diff"] + 1
assert CMP_AT + CMP_LEN == P
NORMS = [("mix", 2, 1 / D, 1.0), ("hg", 8, 1 / 128, 1.0), ("peer", 2, 1 / D, 1.0), ("final", 2, 1 / D, 1.0),
         ("f0", 2, 1 / D, 1.0), ("p0", 2, 1 / D, 0.5), ("conv", 2, 1 / D, 1.0), ("pc", 2, 1 / D, 1.0),
         ("f1", 2, 1 / D, 1.0), ("p1", 2, 1 / D, 0.5), ("kv", 2, 1 / D, 1.0),
         ("p2", 2, 1 / D, 0.5), ("attn", 2, 1 / D, 1.0), ("diff", 16, 1 / 128, 1.0 - LAMBDA_INIT),
         ("pa", 2, 1 / D, 1.0), ("f3", 2, 1 / D, 1.0), ("p3", 2, 1 / D, 0.5)]
NIDX = {n: k for k, (n, *_) in enumerate(NORMS)}
HEAD_NORMS = ("hg", "diff")
SUMS = {n: sum(m not in HEAD_NORMS for m, *_ in NORMS[:k + 1]) for k, (n, *_) in enumerate(NORMS)}
SPREAD = ["hg", "peer", "final", "p0", "pc", "p1", "p2", "pa", "p3"]
X_AT = {n: 2 * (k + 1) for k, n in enumerate(["peer", "final", "p0", "pc", "p1", "p2", "pa", "p3"])}
POSTS = [("p0", "conv"), ("pc", "f1"), ("p1", "kv"), ("p2", "attn"), ("pa", "f3"), ("p3", None)]
UNITS = TT * PE_HEADS


SB_TABLES, N_TABLES = 10, 42
SMALL_LOADS = 8


def build(nc, io):
    ctx = ExitStack()
    with ctx:
        def sb(name, shape, dt=F32):
            return ctx.enter_context(nc.sbuf_tensor(name, shape, dt))

        def sem(name):
            return ctx.enter_context(nc.semaphore(name))

        raw = [sb(f"raw{s}", [P, PANEL]) for s in range(SLOTS)]
        hi = [sb(f"hi{s}", [P, PANEL], F32R) for s in range(SLOTS)]
        lo = [sb(f"lo{s}", [P, PANEL], F32R) for s in range(SLOTS)]
        x = sb("x", [P, TT, D])
        xn = sb("xn", [P, TT, D])
        xh = sb("xh", [P, KD, T], F32R)
        xl = sb("xl", [P, KD, T], F32R)
        oh = sb("oh", [P, 3, PAIRS, T], F32R)
        ol = sb("ol", [P, 3, PAIRS, T], F32R)
        ah = sb("ah", [P, 2, T], F32R)
        al = sb("al", [P, 2, T], F32R)
        ident = sb("ident", [P, P])
        cols = sb("cols", [P, KEYS_AT + PE_KEYS])
        rowbuf = sb("rowbuf", [P, 3, P])
        gb = sb("gb", [P, D])
        minus_half = sb("minus_half", [P, 16])
        slopes = sb("slopes", [P, 8])
        ss = sb("ss", [P, len(NORMS), 16])
        rstd = sb("rstd", [P, len(NORMS), 16])
        iota16 = sb("iota16", [P, PE_K])
        ARENA = 16944
        arena = sb("arena", [P, ARENA])
        top = [0]

        def carve(*shape, at=None, dt=None):
            n = int(np.prod(shape))
            a = top[0] if at is None else at
            top[0] = a + n
            assert top[0] <= ARENA, (top[0], ARENA)
            v = arena[:, a:a + n]
            if dt is not None:
                v = v.bitcast(dt)
            if len(shape) == 2:
                v = v.rearrange("p (a b) -> p a b", a=shape[0])
            if len(shape) == 3:
                v = v.rearrange("p (a b c) -> p a b c", a=shape[0], b=shape[1])
            return v

        dist = carve(len(BLOCKS), P)
        strict = carve(P)
        level_mask = carve(LEVELS, P)
        zeros = carve(T)
        dist_c = carve(TT, CPAD)
        valid_c = carve(TT, CPAD)
        wcmp_k, wcmp_v = carve(CMP_LEN // 2, HD), carve(CMP_LEN // 2, HD)
        mixer_base = top[0]
        sb_q, sb_k, sb_v = carve(PAIRS, T), carve(PAIRS, T), carve(TT, SB_W)
        q_st, k_st, v_st = carve(T), carve(T), carve(TT, P)
        sb_u = [carve(BW) for _ in range(2)]
        sb_p = [carve(BW) for _ in range(2)]
        sb_e = [[carve(P + 1), carve(T + 1)] for _ in range(2)]
        sb_a = [carve(BW) for _ in range(2)]
        sb_pt = [carve(3, P) for _ in range(2)]
        top[0] = mixer_base
        n_q = carve(PAIRS, T)
        n_cmp = carve(2, T)
        n_ksel, n_kwin, n_vsel, n_vwin = carve(T), carve(T), carve(TT, P), carve(TT, P)
        n_gate = carve(TT, N_GATES)
        gate_rows = carve(T)
        cmp_blk = [carve(2, CMP_LEN // 2, N_CMP) for _ in range(2)]
        vc_rows = carve(N_CMP)
        kc, vc = carve(CPAD), carve(2, HD)
        nq_st = carve(T)
        n_sc = [carve(BW) for _ in range(4)]
        n_pt = [carve(3, P) for _ in range(4)]
        n_scc = carve(2, TT, CPAD)
        n_ptc = carve(2, TT, P)
        n_mx, n_sum, n_coef = carve(4, TT), carve(4, TT), carve(4, TT)
        c_mx, c_sum = carve(2, TT), carve(2, TT)
        top[0] = mixer_base - CMP_LEN * HD
        hg_q, hg_f = carve(HG_HEADS, T), carve(HG_HEADS, T)
        hg_i, hg_g = carve(TT, HG_W), carve(TT, HG_W)
        hg_k, hg_s, hg_o = carve(HG_HEADS, T), carve(HG_HEADS, T), carve(TT, HG_W)
        q_lev, k_lev = carve(LEVELS, T), carve(LEVELS, T)
        q_x, k_x, a_x = carve(P), carve(P), carve(P)
        hg_t = carve(2, T)
        hg_dump = carve(TT, P)
        a_m = [xn[:, t, :].rearrange("p (l t) -> p l t", l=LEVELS) for t in range(TT)]
        top[0] = mixer_base
        gm = [carve(4, T) for _ in range(2)]
        m_t = carve(KD, T)
        m_tmp = [carve(4, T) for _ in range(2)]
        top[0] = 0
        spare = [raw[(FIRST["ffn0"] + j) % SLOTS] for j in (1, 2)]
        diag = spare[1][:, 0:DIAGS * P].rearrange("p (k t) -> p k t", k=DIAGS)
        v_ring = [spare[1][:, D:2 * D], spare[0][:, 0:D], spare[0][:, D:2 * D]]
        v_ring += [carve(D) for _ in range(RING - len(v_ring))]
        u_ring = [carve(D) for _ in range(RING)]
        pe_sc = carve(2, PE_HEADS, PE_KEYS)
        pe_s = carve(2, PE_KEYS)
        pe_cand = carve(PE_K, PE_K)
        pe_tv, pe_ti, pe_tif = carve(2, PE_K), carve(2, PE_K, dt=U32), carve(2, PE_K)
        pe_best, pe_nb, pe_pos = carve(PE_K), carve(1), carve(PE_K, dt=U32)
        pe_hl, pe_hlf, pe_e = carve(2, PE_K, dt=U32), carve(2, PE_K), carve(2, PE_K)
        pe_idx = carve(UNITS * PE_K, dt=U32)
        pe_exp, pe_sum = carve(UNITS * PE_K), carve(UNITS)
        pe_act = carve(PE_K)
        pe_h, pe_gelu = carve(PE_K), carve(PE_K)
        pe_rec, pe_gate = carve(1), carve(PE_K)
        pe_carrier, pool_carrier = carve(1), carve(1)
        pe_hot = [pe_s.rearrange("p a k -> p (a k)").rearrange("p (k i) -> p k i", k=PE_K), pe_cand]
        pe_q = arena[:, 0:PE_HEADS * T].rearrange("p (h t) -> p h t", h=PE_HEADS)
        idx_now = sb("idx_now", [P, 2, PE_K], U32)
        top[0] = 0
        ff_s, ff_a = carve(2, T), carve(2, T)
        causal = carve(len(BLOCKS), P)
        cv_b, cv_c, cv_z = carve(2, T), carve(2, T), carve(2, T)
        cv_u = carve(2, T + CONV_W - 1)
        df_k, df_v, df_q = carve(DIFF_HEADS, T), carve(TT, D), carve(DIFF_HEADS, T)
        df_qs, df_ks = carve(2, T), carve(2, T)
        df_sc = [carve(BW) for _ in range(4)]
        df_pt = [carve(3, P) for _ in range(2)]
        df_o = carve(TT, D)
        df_mx, df_sum, df_r = carve(4, TT), carve(4, TT), carve(4, TT)
        sq_dump = carve(D)
        lam_in, lam_dot, lam_exp, lam = carve(4, HD), carve(2), carve(2), carve(1)
        fh, fl = oh[:, 0, 0:2, :], ol[:, 0, 0:2, :]
        yh = oh[:, :, :, :].rearrange("p b k t -> p (b k) t")[:, 0:KD, :]
        yl = ol[:, :, :, :].rearrange("p b k t -> p (b k) t")[:, 0:KD, :]

        PS = ctx.enter_context(nc.psum_tensor("ps", [P, 4, 512], F32))
        ACC = ctx.enter_context(nc.psum_tensor("acc", [P, 4, 512], F32))

        def bank(b):
            return PS[:, b, :] if b < 4 else ACC[:, b - 4, :]

        x_loaded = sem("x_loaded")
        cols_loaded = sem("cols_loaded")
        wcmp_loaded = sem("wcmp_loaded")
        raw_ready = [sem(f"raw_ready{s}") for s in range(SLOTS)]
        spread_loaded = sem("spread_loaded")
        hi_done, lo_done = sem("hi_done"), sem("lo_done")
        panel_used = sem("panel_used")
        evacuated = sem("evacuated")
        tables = sem("tables")
        cols_turned, cols_ready = sem("cols_turned"), sem("cols_ready")
        sumsq = [sem(f"sumsq{t}") for t in range(TT)]
        rstd_ready = [sem(f"rstd_ready{t}") for t in range(TT)]
        rows_ready = [sem(f"rows_ready{t}") for t in range(TT)]
        hg_sq, df_sq = sem("hg_sq"), sem("df_sq")
        rstd_step = sem("rstd_step")
        branch_half = sem("branch_half")
        turned, turned_hi, turned_lo = sem("turned"), sem("turned_hi"), sem("turned_lo")
        x_updated = sem("x_updated")
        dve_step = sem("dve_step")
        gain_used = sem("gain_used")
        pe_chain2 = sem("pe_chain2")
        out_stored = sem("out_stored")
        sb_staged, sb_scored, sb_sig, sb_attn = sem("sb_staged"), sem("sb_scored"), sem("sb_sig"), sem("sb_attn")
        sb_scan, sb_turned, sb_pt_ready, sb_out = sem("sb_scan"), sem("sb_turned"), sem("sb_pt_ready"), sem("sb_out")
        o_hi, o_lo = sem("o_hi"), sem("o_lo")
        gate_turned, gate_ready = sem("gate_turned"), sem("gate_ready")
        n_blk, n_kc, n_kc_ready, vc_copied = sem("n_blk"), sem("n_kc"), sem("n_kc_ready"), sem("vc_copied")
        n_staged, n_scored, n_max = sem("n_staged"), sem("n_scored"), sem("n_max")
        n_scaled, n_coef_ready = [sem(f"n_scaled{a}") for a in range(2)], sem("n_coef_ready")
        n_exp, n_turned, n_pt_ready, n_out = sem("n_exp"), sem("n_turned"), sem("n_pt_ready"), sem("n_out")
        n_chain = sem("n_chain")
        c_scored, c_shift, c_exp, c_scaled = sem("c_scored"), sem("c_shift"), sem("c_exp"), sem("c_scaled")
        h_silu, h_lev, h_chain = sem("h_silu"), sem("h_lev"), sem("h_chain")
        h_scored, h_masked, h_cross, h_out, h_o_ready = sem("h_scored"), sem("h_masked"), sem("h_cross"), sem("h_out"), sem("h_o_ready")
        h_zero = sem("h_zero")
        m_zero, m_added, m_mul = sem("m_zero"), sem("m_added"), sem("m_mul")
        m_hi, m_lo = sem("m_hi"), sem("m_lo")

        pe_scored, pe_sc_ready = sem("pe_scored"), sem("pe_sc_ready")
        pe_chain, idx_ready, idx_copied = sem("pe_chain"), sem("idx_ready"), sem("idx_copied")
        u_landed = [sem(f"u_landed{k}") for k in range(RING)]
        v_landed = [sem(f"v_landed{k}") for k in range(RING)]
        u_used, v_used, diag_ready = sem("u_used"), sem("v_used"), sem("diag_ready")
        best_ready, exp_done, gelu_done, act_ready = sem("best_ready"), sem("exp_done"), sem("gelu_done"), sem("act_ready")
        ff_hi, ff_lo = sem("ff_hi"), sem("ff_lo")
        cv_pad, cv_chain, cv_y, cv_hi, cv_lo = sem("cv_pad"), sem("cv_chain"), sem("cv_y"), sem("cv_hi"), sem("cv_lo")
        lam_loaded, lam_dots, lam_exped = sem("lam_loaded"), sem("lam_dots"), sem("lam_exped")
        df_staged, df_scored, df_chain, df_max = sem("df_staged"), sem("df_scored"), sem("df_chain"), sem("df_max")
        df_exp, df_mixed, df_turned, df_pt_ready = sem("df_exp"), sem("df_mixed"), sem("df_turned"), sem("df_pt_ready")
        df_out, df_o_ready = sem("df_out"), sem("df_o_ready")

        def wait(eng, s, value):
            if not isinstance(value, int) or value > 0:
                eng.wait_ge(s, value)

        def along(table, p, m=0, i=0):
            return table[p] + i * (table[p + m] - table[p]) if m else table[p]

        def peeled(eng, n, body):
            body(0)
            with eng.Fori(1, n) as i:
                body(i)

        def skewed(eng, n, body):
            body(0, True)
            with eng.Fori(1, n - 1) as i:
                body(i, True)
            body(n - 1, False)

        def w_in_cols(c, n):
            return io["w_in"][0, :, c:c + n].rearrange("(k p) n -> p k n", p=P)

        def rows_1024(w, c, n=PC):
            return w[:, c:c + n].rearrange("(k p) n -> p k n", p=P)

        block = ctx.enter_context(nc.Block())

        @block.sync
        def _(sp):
            sp.dma_start(x[:, :, :], io["x"][0].rearrange("(t p) d -> p t d", p=P)).then_inc(x_loaded, 16)

            def load(p, src, m=0, i=0):
                wait(sp, lo_done, p + m * i - (SLOTS - 1))
                k = src.shape[1]
                sp.dma_start(raw[p % SLOTS][:, 0:k * src.shape[2]].rearrange("p (k n) -> p k n", k=k), src)\
                    .then_inc(raw_ready[p % SLOTS], 16)

            p = 0
            for c in (C_SBQ, C_SBK, C_SBV):
                for j in range(2):
                    load(p, w_in_cols(c + j * PC, PC))
                    p += 1
            for j in range(2):
                wait(sp, lo_done, p - (SLOTS - 1))
                dst = raw[p % SLOTS][:, :].rearrange("p (k q d) -> p k q d", k=KD, q=4)
                for q in range(4):
                    h = 2 * j + q // 2 + 4 * (q % 2)
                    sp.dma_start(dst[:, :, q, :], w_in_cols(C_NQ + h * HD, HD)).then_inc(raw_ready[p % SLOTS], 16)
                p += 1
            for c in (C_CMP, C_SEL, C_WIN):
                load(p, w_in_cols(c, PC))
                p += 1
            load(p, w_in_cols(C_NG, N_GATES))
            p += 1
            for c in (C_HQ, C_HF, C_HI, C_HG):
                for j in range(2):
                    load(p, w_in_cols(c + j * PC, PC))
                    p += 1
            for b, name in enumerate(("w_branch_sb", "w_branch_nsa", "w_branch_hgrn")):
                for half in range(2):
                    for j in range(2):
                        load(p, w_in_cols(C_MERGE + b * D + half * 512 + j * PC, PC))
                        p += 1
                    wait(sp, lo_done, p - (SLOTS - 1))
                    dst = raw[p % SLOTS][:, :].rearrange("p (i n) -> p i n", i=PAIRS)
                    w = io[name][0, :, half * 512:(half + 1) * 512]
                    for a in range(2):
                        src = (w.rearrange("(a i d) n -> a d i n", a=2, d=HD) if b == 1 else
                               w.rearrange("(i a d) n -> a d i n", a=2, d=HD))[a]
                        sp.dma_start(dst[a * HD:(a + 1) * HD], src).then_inc(raw_ready[p % SLOTS], 16)
                    p += 1
            for name in ("w_out", "peer_w_q"):
                for j in range(4):
                    load(p, rows_1024(io[name][0], j * PC))
                    p += 1

            def load_ffn(f):
                l, k = f // 2, f % 2
                gate, up, down = (io[f"w_ffn_{n}_2"][l, k] for n in ("gate", "up", "down"))
                p0 = FIRST[f"ffn{f}"]

                def down_rows(i):
                    return down[bass.ds(i * PC, PC), :].rearrange("(f p) n -> p f n", p=P)

                def column(w, i):
                    return w[:, bass.ds(i * PC, PC)].rearrange("(k p) n -> p k n", p=P)

                load(p0, column(gate, 0))
                if f == 0:
                    sp.wait_ge(v_used, UNITS * PE_K)
                load(p0 + 1, column(up, 0))
                with sp.Fori(1, FF_STEPS) as i:
                    load(p0 + 2, column(gate, i), 3, i - 1)
                    load(p0 + 3, column(up, i), 3, i - 1)
                    load(p0 + 4, down_rows(i - 1), 3, i - 1)
                load(p0 + 3 * FF_STEPS - 1, down_rows(FF_STEPS - 1))

            load_ffn(0)
            p0 = FIRST["conv_in"]
            for j in range(4):
                for w in range(3):
                    load(p0 + 3 * j + w, rows_1024(io["w_conv_in_2"][0], w * D + j * PC))
            for j in range(4):
                load(FIRST["conv_out"] + j, rows_1024(io["w_conv_out_2"][0], j * PC))
            load_ffn(1)
            for j in range(8):
                load(FIRST["kv"] + j, rows_1024(io["w_kv_2"], j * PC))
            load_ffn(2)
            for j in range(4):
                load(FIRST["q"] + j, rows_1024(io["w_q_2"][0], j * PC))
            for j in range(4):
                load(FIRST["o"] + j, rows_1024(io["w_o_2"][0], j * PC))
            load_ffn(3)
            for t in range(TT):
                sp.wait_ge(x_updated, X_AT["p3"] - TT + t + 1)
                sp.dma_start(io["out"][0, t * P:(t + 1) * P, :], x[:, t, :]).then_inc(out_stored, 16)
            sp.wait_ge(out_stored, 16 * TT)

        @block.gpsimd
        def _(pool):
            steps = [0]

            def table(ins):
                steps[0] += 1
                ins.then_inc(tables, 1)
                pool.wait_ge(tables, steps[0])

            def select(view, pattern, base, mult, op, fill):
                table(nc.gpsimd.affine_select(out=view, in_=view, pattern=pattern, base=base,
                                              channel_multiplier=mult, compare_op=op, fill=fill))

            g = nc.gpsimd
            table(g.memset(ident[:, :], 0.0))
            select(ident[:, :], [[-1, P]], 0, 1, ALU.not_equal, 1.0)
            table(g.memset(minus_half[:, :], -0.5))
            rstd_steps = [0]

            def norm_tile(name, t):
                k = NIDX[name]
                _, w, scale, factor = NORMS[k]
                c = slice(t * w // TT, (t + 1) * w // TT)
                m, rs = ss[:, k, c], rstd[:, k, c]
                pool.wait_ge(*{"hg": (hg_sq, TT * HG_HEADS), "diff": (df_sq, TT * DIFF_HEADS)}.get(name, (sumsq[t], SUMS[name])))
                g.tensor_scalar(m, m, scale / factor ** 2, EPS / factor ** 2, ALU.mult, ALU.add).then_inc(rstd_step, 1)
                rstd_steps[0] += 1
                pool.wait_ge(rstd_step, rstd_steps[0])
                g.tensor_tensor(rs, m, minus_half[:, c], ALU.pow).then_inc(rstd_ready[t], 1)

            def norm(name):
                for t in range(TT):
                    norm_tile(name, t)

            norm("mix")
            table(g.memset(strict, 0.0))
            select(strict, [[-1, P]], 0, 1, ALU.is_gt, NEG)
            table(g.memset(zeros, 0.0))
            for a in range(2):
                for t in range(TT):
                    table(g.memset(sb_e[a][t][:, 0:1], 1.0))
            sb_tables_done = steps[0]
            for n, (t, sk) in enumerate(BLOCKS):
                base = (t - sk) * P
                table(g.iota(dist[:, n, :], [[-1, P]], base=base, channel_multiplier=1, allow_small_or_imprecise_dtypes=True))
                if not base:
                    select(dist[:, n, :], [[-1, P]], 0, 1, ALU.is_ge, FAR)
            pat = [[P, TT], [-CMP_STRIDE, CPAD]]
            table(g.iota(dist_c, pat, base=1 - CMP_LEN, channel_multiplier=1, allow_small_or_imprecise_dtypes=True))
            select(dist_c, pat, 1 - CMP_LEN, 1, ALU.is_ge, FAR)
            table(g.memset(valid_c, 1.0))
            select(valid_c, pat, 1 - CMP_LEN, 1, ALU.is_ge, 0.0)
            for h in range(8):
                table(g.memset(slopes[:, h:h + 1], -2.0 ** -(h + 1)))
            table(g.memset(level_mask, 1.0))
            select(level_mask[:, 0, :], [[-1, P]], 0, 1, ALU.is_equal, 0.0)
            for l in range(1, LEVELS - 1):
                w = 2 ** l
                v = level_mask[:, l, :].rearrange("p (b w) -> p b w", w=w)
                select(v, [[-w, P // w], [0, w]], 0, 1, ALU.is_ge, 0.0)
                select(v, [[w, P // w], [0, w]], w - 1, -1, ALU.is_ge, 0.0)
            table(g.iota(iota16[:, :], [[1, PE_K]], base=0, channel_multiplier=0, allow_small_or_imprecise_dtypes=True))
            assert steps[0] == N_TABLES and sb_tables_done == SB_TABLES, (steps[0], sb_tables_done)

            pool.wait_ge(evacuated, EVAC[FIRST["nsa_q"]])

            def stage(i):
                wait(pool, sb_scored, 2 * i)
                g.tensor_copy(q_st, sb_q[:, bass.ds(i, 1), :].rearrange("p a t -> p (a t)")).then_inc(sb_staged, 1)
                g.tensor_copy(k_st, sb_k[:, bass.ds(i, 1), :].rearrange("p a t -> p (a t)")).then_inc(sb_staged, 1)
                wait(pool, sb_out, 2 * i)
                g.tensor_copy(v_st, sb_v[:, :, bass.ds(i * P, P)]).then_inc(sb_staged, 1)

            peeled(pool, PAIRS, stage)
            pool.wait_ge(sb_out, 2 * PAIRS)
            g.memset(vc, 0.0).then_inc(n_kc_ready, 1)
            g.memset(kc, 0.0).then_inc(n_kc_ready, 1)
            pool.wait_ge(evacuated, EVAC[FIRST["hg"]])

            def stage_nsa(i):
                wait(pool, c_scored, 2 * i)
                g.tensor_copy(nq_st, n_q[:, bass.ds(i, 1), :].rearrange("p a t -> p (a t)")).then_inc(n_staged, 1)

            peeled(pool, PAIRS, stage_nsa)
            pool.wait_ge(n_out, 2 * PAIRS)
            pool.wait_ge(o_lo, 2 * PAIRS)
            g.memset(q_lev, 0.0).then_inc(h_zero, 1)
            g.memset(k_lev, 0.0).then_inc(h_zero, 1)
            g.memset(hg_s, 1.0).then_inc(h_zero, 1)
            g.dma_start(gb[:, 0:HG_W], io["hgrn_norm"].partition_broadcast(P).rearrange("p a n -> p (a n)")).then_inc(spread_loaded, 16)
            norm("hg")
            pool.wait_ge(turned, XEND["hg"])
            g.memset(m_t, 0.0).then_inc(m_zero, 1)

            spread = {"hg": io["hgrn_norm"], "peer": io["norm_ffn"], "final": io["norm_final"].unsqueeze(0),
                      "p0": io["g_norm_2"][0, 1:2], "pc": io["g_norm_2"][0, 3:4], "p1": io["g_norm_2"][0, 5:6],
                      "p2": io["g_norm_2"][1, 1:2], "pa": io["g_norm_2"][1, 3:4],
                      "p3": io["g_norm_2"][1, 5:6]}

            gain_free = {"peer": (h_silu, 5), "final": (gain_used, TT), "p0": (x_updated, X_AT["final"])}
            for k, (name, _) in enumerate(POSTS[1:]):
                gain_free[name] = (gain_used, TT * (k + 2))

            def load_gain(name):
                pool.wait_ge(*gain_free[name])
                src = spread[name]
                g.dma_start(gb[:, 0:src.shape[1]], src.partition_broadcast(P).rearrange("p a n -> p (a n)")).then_inc(spread_loaded, 16)

            load_gain("peer")
            norm("peer")
            tables_, rings, landed, used = ([io[w].rearrange("a e d -> (a e) d") for w in ("peer_u", "peer_v")], (u_ring, v_ring),
                                            (u_landed, v_landed), (u_used, v_used))

            def gather(w, n, r, count):
                wait(pool, used[w], PE_K * n + GROUP * (r + 1) - RING)
                own = slice(r * GROUP, (r + 1) * GROUP)
                g.tensor_copy(idx_now[:, w, own], pe_idx[:, bass.ds(n * PE_K + r * GROUP, GROUP)]).then_inc(idx_copied, 1)
                pool.wait_ge(idx_copied, 2 * count + 1)
                g.tensor_tensor(pool_carrier, minus_half[:, 0:1], minus_half[:, 0:1], ALU.mult).then_inc(idx_copied, 1)
                for k in range(r * GROUP, (r + 1) * GROUP):
                    slot = k % RING
                    g.indirect_dma_start(out=rings[w][slot], out_offset=None, in_=tables_[w],
                                         in_offset=bass.IndirectOffsetOnAxis(ap=idx_now[:, w, k:k + 1], axis=0))\
                        .then_inc(landed[w][slot], 16)

            groups = PE_K // GROUP

            def gather_unit(n):
                pool.wait_ge(idx_ready, n + 1)
                for r in range(groups):
                    gather(0, n, r, 2 * groups * n - groups + 2 * r)
                    gather(1, n - 1, r, 2 * groups * n - groups + 2 * r + 1)

            pool.wait_ge(idx_ready, 1)
            for r in range(groups):
                gather(0, 0, r, r)
            pool.wait_ge(pe_scored, PE_HEADS // 2 + 1)
            gather_unit(1)
            with pool.Fori(2, UNITS) as n:
                gather_unit(n)
            for r in range(groups):
                gather(1, UNITS - 1, r, 2 * groups * UNITS - groups + r)
            load_gain("final")
            for t in range(TT):
                norm_tile("final", t)
                norm_tile("f0", t)

            def post(name):
                load_gain(name)
                norm(name)

            g.memset(cv_u, 0.0).then_inc(cv_pad, 1)
            table(g.memset(causal, 0.0))
            for n, (t, sk) in enumerate(BLOCKS):
                if t == sk:
                    select(causal[:, n, :], [[-1, P]], 0, 1, ALU.is_ge, NEG)
            for k, nm in enumerate(("lambda_q1_2", "lambda_k1_2", "lambda_q2_2", "lambda_k2_2")):
                g.dma_start(lam_in[:, k, :], io[nm].partition_broadcast(P).rearrange("p a n -> p (a n)")).then_inc(lam_loaded, 16)
            post("p0")
            norm("conv")
            post("pc")
            norm("f1")
            post("p1")
            norm("kv")
            post("p2")
            norm("attn")
            pool.wait_ge(evacuated, EVAC[FIRST["o"]])

            def stage_diff(i):
                for b in range(2):
                    h = 2 * i + b
                    wait(pool, df_scored, 2 * h - 2)
                    for dst, src in ((df_qs, df_q), (df_ks, df_k)):
                        g.tensor_copy(dst[:, b, :], src[:, bass.ds(h, 1), :].rearrange("p a t -> p (a t)")).then_inc(df_staged, 1)

            stage_diff(0)
            with pool.Fori(1, DIFF_HEADS // 2) as i:
                stage_diff(i)
            norm("diff")
            post("pa")
            norm("f3")
            post("p3")

        @block.scalar
        def _(act):
            def split(p, m=0, i=0):
                s = p % SLOTS
                act.wait_ge(raw_ready[s], along(LANDED, p, m, i))
                wait(act, panel_used, p + m * i - (SLOTS - 1))
                nc.scalar.activation(hi[s][:, 0:WORDS[p]], raw[s][:, 0:WORDS[p]], ACT.Copy).then_inc(hi_done, 1)

            def evac(p, out, func=ACT.Copy, scale=1.0, in_=None, m=0, i=0):
                act.wait_ge(panel_used, p + m * i + 1)
                nc.scalar.activation(out, bank(BANK[p]) if in_ is None else in_, func, scale=scale).then_inc(evacuated, 1)

            small = [(rowbuf[0:CMP_AT, 0, :], io["g_norm_2"].rearrange("l j (c p) -> (l j c) p", p=P))]
            small += [(rowbuf[GAIN[n] - P:GAIN[n] - P + KD, 1, :], src.rearrange("(c p) -> c p", p=P))
                      for n, src in (("mix", io["norm_mix"][0]), ("peer", io["norm_ffn"][0]), ("kv", io["g_kv_2"]))]
            small.append((rowbuf[GAIN["diff"] - P:KEYS_AT - P, 1, :], io["g_subln_2"]))
            small.append((rowbuf[TAPS - P:GAIN["diff"] - P, 1, :], io["w_conv_2"][0].rearrange("j (c p) -> (j c) p", p=P)))
            small.append((rowbuf[CMP_AT:P, 0, :].rearrange("l (a d) -> l a d", a=2),
                          io["nsa_cmp_pe"][0].unsqueeze(1).to_broadcast([CMP_LEN, 2, HD])))
            small.append((rowbuf[:, 2, :].rearrange("k (a d) -> k a d", a=2), io["peer_sub_keys"][0].rearrange("a k d -> k a d")))
            assert len(small) == SMALL_LOADS
            for dst, src in small:
                act.dma_start(dst, src).then_inc(cols_loaded, 16)

            def norm_rows(name):
                k = NIDX[name]
                wait(act, turned, XBASE[name])
                nc.scalar.activation(xn[:, 0, :], x[:, 0, :], ACT.Square, accum_out=ss[:, k, 0:1]).then_inc(sumsq[0], 1)
                act.wait_ge(rstd_ready[1], k + 1)
                nc.scalar.activation(xn[:, 1, :], x[:, 1, :], ACT.Copy, scale=rstd[:, k, 1:2]).then_inc(rows_ready[1], 1)

            def turn(name, out, gain):
                for b in range((SEND[name] - SBASE[name]) // 2):
                    if name in XBASE:
                        act.wait_ge(turned, XBASE[name] + b + 1)
                    src = ACC[:, b, :].rearrange("p (k t) -> p k t", k=2)
                    if gain is None:
                        nc.scalar.activation(out[:, 2 * b:2 * b + 2, :], src, ACT.Copy).then_inc(turned_hi, 2)
                        continue
                    for j in range(2):
                        c = GAIN[gain] + (2 * b + j if gain != "diff" else 0)
                        nc.scalar.activation(out[:, 2 * b + j, :], src[:, j, :], ACT.Copy, scale=cols[:, c:c + 1])\
                            .then_inc(turned_hi, 1)

            act.wait_ge(x_loaded, 16)
            norm_rows("mix")
            split(0)
            split(1)
            act.wait_ge(cols_turned, 1)
            nc.scalar.activation(cols[:, :], bank(3)[:, 0:KEYS_AT + PE_KEYS], ACT.Copy).then_inc(cols_ready, 1)
            act.wait_ge(cols_ready, 1)
            turn("mix", xh, "mix")
            for w, name in ((wcmp_k, "nsa_w_cmp_k"), (wcmp_v, "nsa_w_cmp_v")):
                act.dma_start(w, io[name][0].rearrange("(l p) j -> p l j", p=P)).then_inc(wcmp_loaded, 16)

            for j in range(2):
                split(j + 2)
                evac(j, sb_q[:, 2 * j:2 * j + 2, :].rearrange("p a t -> p (a t)"), scale=HD ** -0.5)
            for j in range(2):
                split(j + 4)
                evac(2 + j, sb_k[:, 2 * j:2 * j + 2, :].rearrange("p a t -> p (a t)"))
            for j in range(2):
                split(j + 6)
                evac(4 + j, sb_v[:, :, j * PC:(j + 1) * PC], in_=bank(BANK[4 + j]).rearrange("p (t n) -> p t n", t=TT))

            def sb_pair(i):
                for a in range(2):
                    act.wait_ge(sb_scored, 2 * i + a + 1)
                    wait(act, sb_attn, 2 * i + a - 1)
                    z = bank(4 + a)[:, 0:BW]
                    nc.scalar.activation(sb_u[a], z, ACT.Sigmoid, scale=-1.0).then_inc(sb_sig, 1)
                    nc.scalar.activation(sb_p[a], z, ACT.Sigmoid).then_inc(sb_sig, 1)
                for a in range(2):
                    act.wait_ge(sb_turned, 2 * i + a + 1)
                    wait(act, sb_out, 2 * i + a - 1)
                    nc.scalar.activation(sb_pt[a].rearrange("p a b -> p (a b)"), bank(6 + a)[:, 0:3 * P], ACT.Copy).then_inc(sb_pt_ready, 1)
                act.wait_ge(sb_out, 2 * i + 2)
                nc.scalar.activation(oh[:, 0, bass.ds(i, 1), :], bank(3)[:, 0:T].rearrange("p (a t) -> p a t", a=1), ACT.Copy).then_inc(o_hi, 1)

            peeled(act, PAIRS, sb_pair)

            act.wait_ge(o_lo, PAIRS)
            q0 = FIRST["nsa_q"]
            for j in range(2):
                split(q0 + j + 2)
                evac(q0 + j, n_q[:, 2 * j:2 * j + 2, :].rearrange("p a t -> p (a t)"), scale=HD ** -0.5)
            c0 = FIRST["nsa_kv"]
            split(c0 + 2)
            evac(c0, n_cmp.rearrange("p a t -> p (a t)"))
            for j, (k_, v_) in enumerate(((n_ksel, n_vsel), (n_kwin, n_vwin))):
                split(c0 + 3 + j)
                act.wait_ge(panel_used, c0 + 2 + j)
                b = bank(BANK[c0 + 1 + j])
                nc.scalar.activation(k_, b[:, 0:T], ACT.Copy)
                nc.scalar.activation(v_, b[:, T:2 * T].rearrange("p (t n) -> p t n", t=TT), ACT.Copy).then_inc(evacuated, 1)
            g0 = FIRST["nsa_gate"]
            split(g0 + 2)
            evac(g0, gate_rows[0:N_GATES], func=ACT.Sigmoid, in_=bank(BANK[g0])[0:N_GATES, 0:T])
            act.wait_ge(gate_turned, 1)
            nc.scalar.activation(n_gate, bank(BANK[g0])[:, T:T + TT * N_GATES].rearrange("p (t n) -> p t n", t=TT), ACT.Copy).then_inc(gate_ready, 1)
            act.wait_ge(n_kc, 1)
            act.wait_ge(n_kc_ready, 2)
            nc.scalar.activation(vc_rows, bank(3)[:, 0:N_CMP], ACT.Copy).then_inc(vc_copied, 1)
            nc.scalar.activation(kc[:, 0:N_CMP], bank(2)[:, 0:N_CMP], ACT.Copy)
            act.wait_ge(n_kc, 2)
            nc.scalar.activation(vc[0:N_CMP, :, :], bank(4)[0:N_CMP, 0:P].rearrange("p (g d) -> p g d", g=2), ACT.Copy).then_inc(n_kc_ready, 1)

            def nsa_exp(h, a):
                for br in range(2):
                    u = 2 * br + a
                    act.wait_ge(n_max, 2 * h + br + 1)
                    for t in range(TT):
                        nc.scalar.activation(n_sc[u][:, KEYS[t]], n_sc[u][:, KEYS[t]], ACT.Exp, bias=n_mx[:, u, t:t + 1],
                                             accum_out=n_sum[:, u, t:t + 1]).then_inc(n_exp, 1)
                act.wait_ge(c_shift, h + 1)
                nc.scalar.activation(n_scc[:, a], n_scc[:, a], ACT.Exp).then_inc(c_exp, 1)

            def nsa_turned(h, a):
                wait(act, n_out, h - 1)
                for br in range(2):
                    act.wait_ge(n_turned, 3 * h + br + 1)
                    nc.scalar.activation(n_pt[2 * br + a].rearrange("p a b -> p (a b)"), bank(br)[:, 0:3 * P], ACT.Copy).then_inc(n_pt_ready, 1)
                act.wait_ge(n_turned, 3 * h + 3)
                nc.scalar.activation(n_ptc[0:CPAD, a].rearrange("p t s -> p (t s)"), bank(3)[0:CPAD, 0:TT * P], ACT.Copy).then_inc(n_pt_ready, 1)

            def nsa_out(i):
                act.wait_ge(n_out, 2 * i + 2)
                nc.scalar.activation(oh[:, 1, bass.ds(i, 1), :], bank(2)[:, 0:T].rearrange("p (a t) -> p a t", a=1), ACT.Copy).then_inc(o_hi, 1)

            def nsa_pair(i, more):
                if not isinstance(i, int) or i > 0:
                    nsa_out(i - 1)
                act.wait_ge(n_coef_ready, i + 1)
                for br in range(2):
                    for t in range(TT):
                        nc.scalar.activation(n_sc[2 * br][:, KEYS[t]], n_sc[2 * br][:, KEYS[t]], ACT.Copy, scale=n_coef[:, 2 * br, t:t + 1])\
                            .then_inc(n_scaled[0], 1)
                for a in range(2):
                    nsa_turned(2 * i + a, a)
                if more:
                    for a in range(2):
                        nsa_exp(2 * i + 2 + a, a)

            for a in range(2):
                nsa_exp(a, a)
            skewed(act, PAIRS, nsa_pair)
            nsa_out(PAIRS - 1)

            act.wait_ge(o_lo, 2 * PAIRS)
            h0 = FIRST["hg"]
            flat = lambda v, j: v[:, 2 * j:2 * j + 2, :].rearrange("p a t -> p (a t)")
            for j in range(2):
                split(h0 + j + 2)
                act.wait_ge(panel_used, h0 + j + 1)
                if j:
                    act.wait_ge(h_silu, 1)
                nc.scalar.activation(flat(hg_q, j), bank(BANK[h0 + j]), ACT.Sigmoid)
                nc.scalar.activation(hg_t.rearrange("p a t -> p (a t)"), bank(BANK[h0 + j]), ACT.Copy).then_inc(evacuated, 1)
            for j in range(2):
                split(h0 + j + 4)
                evac(h0 + 2 + j, flat(hg_f, j), func=ACT.Sigmoid)
            for j in range(2):
                split(h0 + j + 6)
                b = bank(BANK[h0 + 4 + j]).rearrange("p (t n) -> p t n", t=TT)
                evac(h0 + 4 + j, hg_i[:, :, j * PC:(j + 1) * PC], in_=b)
            for j in range(2):
                split(h0 + j + 8)
                act.wait_ge(panel_used, h0 + 6 + j + 1)
                act.wait_ge(h_silu, (2, 4)[j])
                b = bank(BANK[h0 + 6 + j]).rearrange("p (t n) -> p t n", t=TT)
                nc.scalar.activation(hg_g[:, :, j * PC:(j + 1) * PC], b, ACT.Sigmoid)
                nc.scalar.activation(hg_t, b, ACT.Copy).then_inc(evacuated, 1)

            def hg_head(i):
                act.wait_ge(h_scored, i + 1)
                wait(act, h_out, i)
                nc.scalar.activation(a_x, bank(3)[:, 0:P], ACT.Copy).then_inc(h_cross, 1)
                act.wait_ge(h_out, i + 1)
                for t in range(TT):
                    wait(act, hg_sq, TT * i - 1 + t)
                    nc.scalar.activation(hg_dump[:, t, :], bank(2)[:, t * P:(t + 1) * P], ACT.Square,
                                         accum_out=ss[:, NIDX["hg"], bass.ds(i + t * HG_HEADS, 1)]).then_inc(hg_sq, 1)
                nc.scalar.activation(hg_o[:, :, bass.ds(i * P, P)], bank(2)[:, 0:2 * P].rearrange("p (t v) -> p t v", t=TT), ACT.Copy).then_inc(h_o_ready, 1)

            peeled(act, HG_HEADS, hg_head)
            turn("hg", oh[:, 2, :, :], None)

            def merge(b):
                for half in range(2):
                    p = FIRST["merge"] + 3 * half
                    for j in range(2):
                        split(p + j + 2, 6, b)
                        wait(act, m_mul, 2 * b + half - 1)
                        evac(p + j, gm[half][:, 2 * j:2 * j + 2, :].rearrange("p a t -> p (a t)"), func=ACT.Sigmoid, m=6, i=b)
                    split(p + 4, 6, b)

            peeled(act, 3, merge)

            act.wait_ge(panel_used, FIRST["w_out"])
            for half in range(2):
                act.wait_ge(m_added, 5 + half)
                nc.scalar.activation(xh[:, 4 * half:4 * half + 4, :], m_t[:, 4 * half:4 * half + 4, :], ACT.Copy).then_inc(m_hi, 1)
            for j in range(4):
                split(FIRST["w_out"] + j + 2)

            act.wait_ge(evacuated, EVAC[FIRST["peer_q"]])
            norm_rows("peer")
            turn("peer", xh, "peer")

            def best_exp(n):
                act.wait_ge(best_ready, n + 1)
                nc.scalar.activation(pe_exp[:, bass.ds(n * PE_K, PE_K)], pe_best, ACT.Exp, bias=pe_nb,
                                     accum_out=pe_sum[:, bass.ds(n, 1)]).then_inc(exp_done, 1)

            p0 = FIRST["peer_q"]
            for j in range(4):
                if j < 3:
                    split(p0 + j + 2)
                evac(p0 + j, pe_q[:, 2 * j:2 * j + 2, :].rearrange("p h t -> p (h t)"))
                if j == 2:
                    best_exp(0)
                act.wait_ge(pe_scored, j + 1)
                own = slice(j % 2 * 2 * P, (j % 2 + 1) * 2 * P)
                for a in range(2):
                    nc.scalar.activation(pe_sc[:, a, 2 * j:2 * j + 2, :].rearrange("p h k -> p (h k)"), ACC[:, 2 * a + j // 2, own],
                                         ACT.Copy).then_inc(pe_sc_ready, 1)

            def weights(n):
                act.wait_ge(u_used, PE_K * (n + 1))
                wait(act, act_ready, n)
                nc.scalar.activation(pe_gelu, pe_h, ACT.Gelu).then_inc(gelu_done, 1)
                act.wait_ge(act_ready, n + 1)
                for k in range(PE_K):
                    wait(act, v_used, PE_K * n + k + 1 - DIAGS)
                    nc.scalar.activation(diag[:, k % DIAGS, :], ident[:, :], ACT.Copy, scale=pe_act[:, k:k + 1]).then_inc(diag_ready, 1)

            best_exp(1)
            weights(0)
            with act.Fori(1, UNITS - 1) as n:
                best_exp(n + 1)
                weights(n)
            weights(UNITS - 1)

            def ffn(f):
                p0 = FIRST[f"ffn{f}"]
                last = p0 + 3 * FF_STEPS - 1

                def silu(p, m=0, r=0):
                    act.wait_ge(panel_used, p + m * r + 1)
                    act.wait_ge(evacuated, along(EVAC, p, m, r))
                    nc.scalar.activation(ff_s.rearrange("p f t -> p (f t)"), bank(BANK[p]), ACT.Silu).then_inc(evacuated, 1)

                def upper(p, down_done, m=0, r=0, out=ah[:, :, :]):
                    act.wait_ge(evacuated, along(EVAC, p, m, r) + 2)
                    act.wait_ge(panel_used, down_done)
                    nc.scalar.activation(out, ff_a, ACT.Copy).then_inc(ff_hi, 1)

                split(p0 + 2)
                split(p0 + 3)
                silu(p0)
                upper(p0, p0)

                with act.Fori(1, FF_STEPS - 1) as i:
                    split(p0 + 4, 3, i - 1)
                    split(p0 + 5, 3, i - 1)
                    silu(p0 + 2, 3, i - 1)
                    split(p0 + 6, 3, i - 1)
                    upper(p0 + 2, p0 + 5 + 3 * (i - 1), 3, i - 1)
                i = FF_STEPS - 1
                split(p0 + 4, 3, i - 1)
                split(p0 + 5, 3, i - 1)
                silu(p0 + 2, 3, i - 1)
                upper(p0 + 2, p0, 3, i - 1, fh)
                for p in range(last + 1, min(last + 3, NP)):
                    split(p)

            def post(name, panels):
                k, after = NIDX[name], dict(POSTS)[name]
                for t in range(TT):
                    act.wait_ge(*((branch_half, [n for n, _ in POSTS].index(name) + 1) if t == 0 else (panel_used, panels)))
                    act.wait_ge(sumsq[1 - t], SUMS[name] - 1 + t)
                    nc.scalar.activation(sq_dump, ACC[:, 2 * t:2 * t + 2, :].rearrange("p b n -> p (b n)"), ACT.Square,
                                         accum_out=ss[:, k, t:t + 1]).then_inc(sumsq[t], 1)
                if after is None:
                    return
                k = NIDX[after]
                act.wait_ge(x_updated, X_AT[name] - 1)
                act.wait_ge(sumsq[1], SUMS[after] - 1)
                nc.scalar.activation(sq_dump, x[:, 0, :], ACT.Square, accum_out=ss[:, k, 0:1]).then_inc(sumsq[0], 1)
                act.wait_ge(rstd_ready[0], k + 1)
                nc.scalar.activation(xn[:, 0, :], x[:, 0, :], ACT.Copy, scale=rstd[:, k, 0:1]).then_inc(rows_ready[0], 1)
                turn(after, xh, after)

            split(FIRST["ffn0"] + 1)
            turn("f0", xh, "f0")
            ffn(0)
            post("p0", FIRST["conv_in"])
            p0 = FIRST["conv_in"]

            def conv(j):
                for w, out in enumerate((cv_b, cv_c, None)):
                    split(p0 + w + 2, 3, j)
                    if out is not None:
                        wait(act, cv_y, j)
                        evac(p0 + w, out.rearrange("p f t -> p (f t)"), m=3, i=j)
                act.wait_ge(cv_y, j + 1)
                nc.scalar.activation(yh[:, bass.ds(2 * j, 2), :], cv_z, ACT.Copy).then_inc(cv_hi, 1)

            peeled(act, 4, conv)
            for j in range(4):
                split(FIRST["conv_out"] + j + 2)
            post("pc", FIRST["ffn1"])
            ffn(1)
            post("p1", FIRST["kv"])
            for j in range(8):
                p = FIRST["kv"] + j
                split(p + 2)
                if j < 4:
                    evac(p, df_k[:, 2 * j:2 * j + 2, :].rearrange("p h t -> p (h t)"))
                else:
                    c = (j - 4) * PC
                    evac(p, df_v[:, :, c:c + PC], in_=bank(BANK[p]).rearrange("p (t n) -> p t n", t=TT))
            act.wait_ge(panel_used, FIRST["ffn2"])
            turn("f2", xh, "f2")
            ffn(2)
            post("p2", FIRST["q"])
            for j in range(4):
                p = FIRST["q"] + j
                split(p + 2)
                evac(p, df_q[:, 2 * j:2 * j + 2, :].rearrange("p h t -> p (h t)"), scale=HD ** -0.5)
            act.wait_ge(lam_dots, 2)
            nc.scalar.activation(lam_exp, lam_dot, ACT.Exp).then_inc(lam_exped, 1)

            def diff_exp(h, b):
                for c in range(2):
                    u = 2 * b + c
                    act.wait_ge(df_max, 2 * h + c + 1)
                    for t in range(TT):
                        nc.scalar.activation(df_sc[u][:, KEYS[t]], df_sc[u][:, KEYS[t]], ACT.Exp, bias=df_mx[:, u, t:t + 1],
                                             accum_out=df_sum[:, u, t:t + 1]).then_inc(df_exp, 1)

            def diff_turned(h, b):
                act.wait_ge(df_turned, h + 1)
                wait(act, df_out, h - 1)
                nc.scalar.activation(df_pt[b].rearrange("p n t -> p (n t)"), bank(b)[:, 0:3 * P], ACT.Copy).then_inc(df_pt_ready, 1)

            def diff_out(h, b):
                act.wait_ge(df_out, h + 1)
                for t in range(TT):
                    wait(act, df_sq, TT * (h - 2) + t + 1)
                    nc.scalar.activation(sq_dump[:, (TT * b + t) * P:(TT * b + t + 1) * P], bank(2 + b)[:, t * P:(t + 1) * P], ACT.Square,
                                         accum_out=ss[:, NIDX["diff"], bass.ds(h + t * DIFF_HEADS, 1)]).then_inc(df_sq, 1)
                nc.scalar.activation(df_o[:, :, bass.ds(h * P, P)], bank(2 + b)[:, 0:TT * P].rearrange("p (t e) -> p t e", t=TT),
                                     ACT.Copy).then_inc(df_o_ready, 1)

            def diff_pair(i, more):
                for b in range(2):
                    diff_turned(2 * i + b, b)
                if more:
                    for b in range(2):
                        diff_exp(2 * i + 2 + b, b)
                for b in range(2):
                    diff_out(2 * i + b, b)

            for b in range(2):
                diff_exp(b, b)
            skewed(act, DIFF_HEADS // 2, diff_pair)
            turn("diff", xh, "diff")
            for j in range(4):
                split(FIRST["o"] + j + 2)
            post("pa", FIRST["ffn3"])
            ffn(3)
            post("p3", NP)

        @block.vector
        def _(dve):
            v = nc.vector
            chain = [0]

            def link(ins):
                chain[0] += 1
                ins.then_inc(dve_step, 1)
                dve.wait_ge(dve_step, chain[0])

            def split(p, m=0, i=0):
                s = p % SLOTS
                dve.wait_ge(hi_done, p + m * i + 1)
                v.tensor_tensor(lo[s][:, 0:WORDS[p]], raw[s][:, 0:WORDS[p]], hi[s][:, 0:WORDS[p]].bitcast(F32), ALU.subtract).then_inc(lo_done, 1)

            def square(rows, dump, out):
                return v.scalar_tensor_tensor(out=dump, in0=rows, scalar=1.0, in1=rows, op0=ALU.mult, op1=ALU.mult, accum_out=out)

            def norm_rows(name):
                k = NIDX[name]
                wait(dve, turned, XBASE[name])
                square(x[:, 1, :], xn[:, 1, :], ss[:, k, 1:2]).then_inc(sumsq[1], 1)
                dve.wait_ge(rstd_ready[0], k + 1)
                v.tensor_scalar(xn[:, 0, :], x[:, 0, :], rstd[:, k, 0:1], None, ALU.mult).then_inc(rows_ready[0], 1)

            def turn(name, out_hi, out_lo, gain):
                for b in range((SEND[name] - SBASE[name]) // 2):
                    dve.wait_ge(turned_hi, SBASE[name] + 2 * b + 2)
                    src = ACC[:, b, :].rearrange("p (k t) -> p k t", k=2)
                    for j in range(2):
                        c = GAIN[gain] + (2 * b + j if gain != "diff" else 0) if gain else 0
                        s = cols[:, c:c + 1] if gain else 1.0
                        v.scalar_tensor_tensor(out=out_lo[:, 2 * b + j, :], in0=src[:, j, :], scalar=s,
                                               in1=out_hi[:, 2 * b + j, :].bitcast(F32), op0=ALU.mult, op1=ALU.subtract).then_inc(turned_lo, 1)

            dve.wait_ge(x_loaded, 16)
            norm_rows("mix")
            split(0)
            split(1)
            dve.wait_ge(cols_ready, 1)
            turn("mix", xh, xl, "mix")
            for j in range(6):
                split(j + 2)

            dve.wait_ge(tables, SB_TABLES)

            def sb_pair(i):
                for a in range(2):
                    dve.wait_ge(sb_sig, 4 * i + 2 * a + 1)
                    for t in range(TT):
                        n = (t + 1) * P
                        v.tensor_tensor_scan(out=sb_e[a][t][:, 1:n + 1], data0=sb_u[a][:, KEYS[t]][:, ::-1], data1=zeros[:, 0:n], initial=1.0,
                                             op0=ALU.mult, op1=ALU.add).then_inc(sb_scan, 1)
                    dve.wait_ge(sb_scan, 4 * i + 2 * a + 2)
                    dve.wait_ge(sb_sig, 4 * i + 2 * a + 2)
                    wait(dve, sb_turned, 2 * i + a - 1)
                    for t in range(TT):
                        last = v.tensor_tensor(sb_a[a][:, KEYS[t]], sb_p[a][:, KEYS[t]], sb_e[a][t][:, (t + 1) * P - 1::-1], ALU.mult)
                    last.then_inc(sb_attn, 1)
                dve.wait_ge(o_hi, i + 1)
                v.tensor_tensor(ol[:, 0, bass.ds(i, 1), :], bank(3)[:, 0:T].rearrange("p (a t) -> p a t", a=1),
                                oh[:, 0, bass.ds(i, 1), :].bitcast(F32), ALU.subtract).then_inc(o_lo, 1)

            peeled(dve, PAIRS, sb_pair)

            for j in range(3):
                split(FIRST["nsa_kv"] + j)
            dve.wait_ge(evacuated, EVAC[FIRST["nsa_kv"] + 1])
            half = CMP_STRIDE // 2
            for g in range(2):
                own = slice(g * HD, (g + 1) * HD)
                for w in range(2):
                    src = n_cmp[own, w, :].rearrange("p (n l q) -> p q l n", l=half, q=2)
                    emb = cols[own, CMP_AT:CMP_AT + CMP_LEN].rearrange("p (l q) -> p q l", q=2)
                    for q in range(2):
                        for j in range(2):
                            l = slice(j * half, (j + 1) * half)
                            v.tensor_tensor(cmp_blk[g][q * HD:(q + 1) * HD, w, l, :], src[:, q, :, j:j + N_CMP],
                                            emb[:, q, l].unsqueeze(2).to_broadcast([HD, half, N_CMP]), ALU.add).then_inc(n_blk, 1)
            for j in range(3):
                split(FIRST["nsa_kv"] + 3 + j)
            dve.wait_ge(tables, N_TABLES)
            dve.wait_ge(gate_ready, 1)

            SCORE_LINKS, SCALE_LINKS = 6, 4

            def nsa_links(before):
                done = [before]

                def then(ins):
                    done[0] = done[0] + 1
                    ins.then_inc(n_chain, 1)
                    dve.wait_ge(n_chain, done[0])
                return then

            def nsa_scores(h, i, a, before):
                then = nsa_links(before)
                wait(dve, n_turned, 3 * h - 3)
                slope = slopes[:, bass.ds(i + 4 * a, 1)]
                for br in range(2):
                    u = 2 * br + a
                    dve.wait_ge(n_scored, 2 * h + br + 1)
                    then(v.scalar_tensor_tensor(out=n_sc[u], in0=dist.rearrange("p n s -> p (n s)"),
                                                scalar=slope, in1=bank(4 + 2 * a + br)[:, 0:BW], op0=ALU.mult, op1=ALU.add))
                    v.tensor_reduce(n_mx[:, u, 0:1], n_sc[u][:, KEYS[0]], AX.X, ALU.max)
                    then(v.tensor_reduce(n_mx[:, u, 1:2], n_sc[u][:, KEYS[1]], AX.X, ALU.max))
                    v.tensor_scalar(n_mx[:, u, :], n_mx[:, u, :], -1.0, None, ALU.mult).then_inc(n_max, 1)
                dve.wait_ge(c_scored, h + 1)
                then(v.scalar_tensor_tensor(out=n_scc[:, a].rearrange("p t c -> p (t c)"), in0=dist_c.rearrange("p t c -> p (t c)"), scalar=slope,
                                            in1=bank(3)[:, T:T + TT * CPAD], op0=ALU.mult, op1=ALU.add))
                then(v.tensor_reduce(c_mx[:, a, :], n_scc[:, a], AX.X, ALU.max))
                v.tensor_tensor(n_scc[:, a], n_scc[:, a], c_mx[:, a, :].unsqueeze(2).to_broadcast([P, TT, CPAD]), ALU.subtract).then_inc(c_shift, 1)

            def nsa_scale(i, before):
                then = nsa_links(before)
                gates = n_gate.rearrange("p t (a r) -> p r a t", a=2)
                dve.wait_ge(c_exp, 2 * i + 2)
                then(v.tensor_reduce(c_sum, n_scc, AX.X, ALU.add))
                then(v.reciprocal(c_sum, c_sum))
                v.tensor_tensor(c_sum, c_sum, gates[:, bass.ds(3 * i, 1)].rearrange("p r a t -> p (r a) t"), ALU.mult)
                then(v.tensor_tensor(n_scc, n_scc, valid_c.unsqueeze(1).to_broadcast([P, 2, TT, CPAD]), ALU.mult))
                v.tensor_tensor(n_scc, n_scc, c_sum.unsqueeze(3).to_broadcast([P, 2, TT, CPAD]), ALU.mult).then_inc(c_scaled, 1)
                dve.wait_ge(n_exp, 8 * i + 8)
                then(v.reciprocal(n_coef, n_sum))
                coef = n_coef.rearrange("p (b a) t -> p b a t", b=2)
                v.tensor_tensor(coef, coef, gates[:, bass.ds(3 * i + 1, 2)], ALU.mult).then_inc(n_coef_ready, 1)
                dve.wait_ge(n_coef_ready, i + 1)
                for br in range(2):
                    u = 2 * br + 1
                    for t in range(TT):
                        v.tensor_scalar(n_sc[u][:, KEYS[t]], n_sc[u][:, KEYS[t]], n_coef[:, u, t:t + 1], None, ALU.mult).then_inc(n_scaled[1], 1)

            def nsa_out(i):
                dve.wait_ge(o_hi, PAIRS + i + 1)
                v.tensor_tensor(ol[:, 1, bass.ds(i, 1), :], bank(2)[:, 0:T].rearrange("p (a t) -> p a t", a=1),
                                oh[:, 1, bass.ds(i, 1), :].bitcast(F32), ALU.subtract).then_inc(o_lo, 1)

            def nsa_pair(i, more):
                c = 2 * SCORE_LINKS + (2 * SCORE_LINKS + SCALE_LINKS) * i
                nsa_scale(i, c)
                if not isinstance(i, int) or i > 0:
                    nsa_out(i - 1)
                c = c + SCALE_LINKS
                if more:
                    for a in range(2):
                        nsa_scores(2 * i + 2 + a, i + 1, a, c + a * SCORE_LINKS)

            for a in range(2):
                nsa_scores(a, 0, a, a * SCORE_LINKS)
            skewed(dve, PAIRS, nsa_pair)
            nsa_out(PAIRS - 1)

            h0 = FIRST["hg"]
            flat = lambda w, j: w[:, 2 * j:2 * j + 2, :].rearrange("p a t -> p (a t)")
            for j in range(2):
                split(h0 + j + 2)
                dve.wait_ge(evacuated, EVAC[h0 + j + 1])
                v.tensor_tensor(flat(hg_q, j), flat(hg_q, j), hg_t.rearrange("p a t -> p (a t)"), ALU.mult).then_inc(h_silu, 1)
            for j in range(4):
                split(h0 + j + 4)
            dve.wait_ge(evacuated, EVAC[h0 + 4])
            v.tensor_scalar(hg_k, hg_f, -1.0, 1.0, ALU.mult, ALU.add).then_inc(h_silu, 1)
            dve.wait_ge(spread_loaded, 16)
            for j in range(2):
                split(h0 + j + 8)
                dve.wait_ge(evacuated, EVAC[h0 + 7 + j])
                gv = hg_g[:, :, j * PC:(j + 1) * PC]
                link(v.tensor_tensor(gv, gv, hg_t, ALU.mult))
                v.tensor_tensor(gv, gv, gb[:, j * PC:(j + 1) * PC].unsqueeze(1).to_broadcast([P, TT, PC]), ALU.mult).then_inc(h_silu, 1)
            dve.wait_ge(h_zero, 3)
            dve.wait_ge(h_silu, 5)

            def hg_head(i):
                c = 14 * i
                done = [0]

                def then(ins, n=1):
                    ins.then_inc(h_chain, 1)
                    done[0] += 1

                def sync():
                    dve.wait_ge(h_chain, c + done[0])

                one = lambda w: w[:, bass.ds(i, 1), :].rearrange("p a t -> p (a t)")
                q, f, k, s = one(hg_q), one(hg_f), one(hg_k), one(hg_s)
                wait(dve, h_scored, i)
                v.tensor_copy(q_lev[:, 0, :], q).then_inc(h_lev, 1)
                v.tensor_copy(k_lev[:, 0, :], k).then_inc(h_lev, 1)
                for l in range(1, LEVELS + 1):
                    h = 2 ** (l - 1)
                    half = lambda w, r: w.rearrange("p (b r h) -> p b r h", r=2, h=h)[:, :, r, :]
                    if l < LEVELS:
                        qo, ko = half(q_lev[:, l, :], 1), half(k_lev[:, l, :], 0)
                    else:
                        qo, ko = q_x.unsqueeze(1), k_x.unsqueeze(1)
                    v.tensor_tensor(ko, half(k, 0), half(s, 0), ALU.mult).then_inc(h_lev, 1)
                    if l > 1:
                        sync()
                    v.tensor_tensor(qo, half(q, 1), half(f, 1), ALU.mult).then_inc(h_lev, 1)
                    if l == LEVELS:
                        break
                    n = T // (2 * h)
                    left = half(f, 0)[:, :, h - 1:h].to_broadcast([P, n, h])
                    right = half(f, 1)[:, :, h - 1:h].to_broadcast([P, n, h])
                    dve.wait_ge(h_lev, 18 * i + 2 * l + 1)
                    then(v.tensor_tensor(half(s, 0), half(s, 0), right, ALU.mult))
                    dve.wait_ge(h_lev, 18 * i + 2 * l + 2)
                    sync()
                    then(v.tensor_tensor(half(f, 1), half(f, 1), left, ALU.mult))
                for t in range(TT):
                    dve.wait_ge(h_scored, i + 1)
                    wait(dve, h_out, i)
                    v.tensor_tensor(a_m[t], ACC[:, 2 * t:2 * t + 2, :].rearrange("p b (l t) -> p (b l) t", t=P), level_mask, ALU.mult).then_inc(h_masked, 1)

            peeled(dve, HG_HEADS, hg_head)
            k = NIDX["hg"]
            heads = lambda w: w.rearrange("p t (h d) -> p (t h) d", d=P)
            dve.wait_ge(h_o_ready, HG_HEADS)
            dve.wait_ge(h_out, HG_HEADS)
            for t in range(TT):
                link(v.tensor_tensor(hg_o[:, t, :], hg_o[:, t, :], hg_g[:, t, :], ALU.mult))
            for t in range(TT):
                own = slice(t * HG_HEADS, (t + 1) * HG_HEADS)
                dve.wait_ge(rstd_ready[t], k + 1)
                v.tensor_tensor(heads(hg_o)[:, own], heads(hg_o)[:, own], rstd[:, k, own].unsqueeze(2).to_broadcast([P, HG_HEADS, P]), ALU.mult)\
                    .then_inc(rows_ready[t], 1)
            turn("hg", oh[:, 2, :, :], ol[:, 2, :, :], None)

            dve.wait_ge(m_zero, 1)

            def merge(b):
                for half in range(2):
                    p = FIRST["merge"] + 3 * half
                    split(p + 2, 6, b)
                    split(p + 3, 6, b)
                    split(p + 4, 6, b)
                    u = 2 * b + half
                    dve.wait_ge(panel_used, p + 6 * b + 3)
                    wait(dve, m_added, u - 1)
                    v.tensor_tensor(m_tmp[half].rearrange("p (b f) t -> p b (f t)", b=2), gm[half].rearrange("p (b f) t -> p b (f t)", b=2),
                                    ACC[:, 2 * half:2 * half + 2, :], ALU.mult).then_inc(m_mul, 1)
                    dve.wait_ge(m_mul, u + 1)
                    v.tensor_tensor(m_t[:, 4 * half:4 * half + 4, :], m_t[:, 4 * half:4 * half + 4, :], m_tmp[half], ALU.add).then_inc(m_added, 1)

            peeled(dve, 3, merge)

            for half in range(2):
                f = slice(4 * half, 4 * half + 4)
                dve.wait_ge(m_hi, half + 1)
                v.tensor_tensor(xl[:, f, :], m_t[:, f, :], xh[:, f, :].bitcast(F32), ALU.subtract).then_inc(m_lo, 1)
            for j in range(4):
                p = FIRST["w_out"] + j
                split(p + 2)
                dve.wait_ge(panel_used, p + 1)
                xc = x[:, :, j * PC:(j + 1) * PC]
                v.tensor_tensor(xc, xc, bank(BANK[p]).rearrange("p (t n) -> p t n", t=TT), ALU.add).then_inc(evacuated, 1)

            dve.wait_ge(evacuated, EVAC[FIRST["peer_q"]])
            norm_rows("peer")
            turn("peer", xh, xl, "peer")
            dve.wait_ge(turned, XEND["peer"])
            dve.wait_ge(spread_loaded, 16 * 2)
            for t in range(TT):
                dve.wait_ge(rows_ready[t], XIDX["peer"] + 1)
                v.tensor_tensor(xn[:, t, :], xn[:, t, :], gb[:, :], ALU.mult).then_inc(gain_used, 1)
            dve.wait_ge(gain_used, TT)
            p0 = FIRST["peer_q"]
            split(p0 + 2)

            def best(n, t, h):
                c = 44 * n
                done = [0]

                def then(ins):
                    done[0] += 1
                    ins.then_inc(pe_chain, 1)

                def sync():
                    dve.wait_ge(pe_chain, c + done[0])
                    then(v.tensor_copy(pe_carrier, minus_half[:, 0:1]))

                def top16(src, vals, idx):
                    for a in range(len(src)):
                        then(v.max(vals[a][:, 0:8], src[a]))
                    sync()
                    for a in range(len(src)):
                        then(v.max_index(idx[a][:, 0:8], vals[a][:, 0:8], src[a]))
                    sync()
                    for a in range(len(src)):
                        then(v.match_replace(src[a], vals[a][:, 0:8], src[a], -3e38))
                    sync()
                    for a in range(len(src)):
                        then(v.max(vals[a][:, 8:16], src[a]))
                    sync()
                    for a in range(len(src)):
                        then(v.max_index(idx[a][:, 8:16], vals[a][:, 8:16], src[a]))
                    sync()

                wait(dve, exp_done, n)
                scores = PS[:, :, :].rearrange("p (a g) (h k) -> p a (g h) k", a=2, h=PE_HEADS // 2) if t else pe_sc
                then(v.tensor_copy(pe_s, scores[:, :, bass.ds(h, 1), :].rearrange("p a h k -> p a (h k)")))
                sync()
                top16([pe_s[:, a, :] for a in range(2)], [pe_tv[:, a, :] for a in range(2)], [pe_ti[:, a, :] for a in range(2)])
                then(v.tensor_copy(pe_tif, pe_ti))
                then(v.tensor_tensor(pe_cand, pe_tv[:, 0, :].unsqueeze(2).to_broadcast([P, PE_K, PE_K]),
                                     pe_tv[:, 1, :].unsqueeze(1).to_broadcast([P, PE_K, PE_K]), ALU.add))
                sync()
                top16([pe_cand.rearrange("p i j -> p (i j)")], [pe_best], [pe_pos])
                v.tensor_scalar(pe_nb, pe_best[:, 0:1], -1.0, None, ALU.mult).then_inc(best_ready, 1)
                then(v.tensor_scalar(pe_hl[:, 0, :], pe_pos, 4, None, ALU.logical_shift_right))
                then(v.tensor_scalar(pe_hl[:, 1, :], pe_pos, 15, None, ALU.bitwise_and))
                sync()
                then(v.tensor_copy(pe_hlf, pe_hl))
                sync()
                for a in range(2):
                    then(v.tensor_tensor(pe_hot[a], iota16[:, :].unsqueeze(1).to_broadcast([P, PE_K, PE_K]),
                                         pe_hlf[:, a, :].unsqueeze(2).to_broadcast([P, PE_K, PE_K]), ALU.is_equal))
                sync()
                for a in range(2):
                    then(v.tensor_tensor(pe_hot[a], pe_hot[a], pe_tif[:, a, :].unsqueeze(1).to_broadcast([P, PE_K, PE_K]), ALU.mult))
                sync()
                for a in range(2):
                    then(v.tensor_reduce(pe_e[:, a, :], pe_hot[a], AX.X, ALU.add))
                sync()
                v.scalar_tensor_tensor(out=pe_idx[:, bass.ds(n * PE_K, PE_K)], in0=pe_e[:, 0, :], scalar=float(PE_KEYS), in1=pe_e[:, 1, :],
                                       op0=ALU.mult, op1=ALU.add).then_inc(idx_ready, 1)
                assert done[0] == 44, done

            def dots(n, t):
                wait(dve, gelu_done, n)
                for k in range(PE_K):
                    slot = k % RING
                    dve.wait_ge(u_landed[slot], 16 * (PE_K // RING * n + k // RING + 1))
                    v.scalar_tensor_tensor(out=u_ring[slot], in0=u_ring[slot], scalar=1.0, in1=xn[:, t, :], op0=ALU.mult, op1=ALU.mult,
                                           accum_out=pe_h[:, k:k + 1]).then_inc(u_used, 1)

            def weights(n):
                dve.wait_ge(exp_done, n + 1)
                v.reciprocal(pe_rec, pe_sum[:, bass.ds(n, 1)]).then_inc(pe_chain2, 1)
                dve.wait_ge(pe_chain2, 2 * n + 1)
                v.tensor_scalar(pe_gate, pe_exp[:, bass.ds(n * PE_K, PE_K)], pe_rec, None, ALU.mult).then_inc(pe_chain2, 1)
                dve.wait_ge(pe_chain2, 2 * n + 2)
                wait(dve, diag_ready, PE_K * n)
                dve.wait_ge(gelu_done, n + 1)
                v.tensor_tensor(pe_act, pe_gate, pe_gelu, ALU.mult).then_inc(act_ready, 1)

            dve.wait_ge(pe_sc_ready, 2)
            best(0, 0, 0)
            split(p0 + 3)
            best(1, 0, 1)
            dots(0, 0)
            weights(0)
            split(p0 + 4)
            dve.wait_ge(pe_sc_ready, PE_HEADS)
            with dve.Fori(1, PE_HEADS - 1) as n:
                best(n + 1, 0, n + 1)
                dots(n, 0)
                weights(n)
            dve.wait_ge(pe_scored, PE_HEADS // 2 + 1)
            n = PE_HEADS - 1
            best(n + 1, 1, 0)
            dots(n, 0)
            weights(n)
            with dve.Fori(PE_HEADS, UNITS - 1) as n:
                best(n + 1, 1, n + 1 - PE_HEADS)
                dots(n, 1)
                weights(n)
            dots(UNITS - 1, 1)
            weights(UNITS - 1)
            dve.wait_ge(spread_loaded, 16 * 3)
            for t in range(TT):
                dve.wait_ge(v_used, PE_K * PE_HEADS * (t + 1))
                v.tensor_tensor(x[:, t, :], x[:, t, :], ACC[:, 2 * t:2 * t + 2, :].rearrange("p b n -> p (b n)"), ALU.add).then_inc(x_updated, 1)
                dve.wait_ge(x_updated, 2 * t + 1)
                k = NIDX["final"]
                square(x[:, t, :], xn[:, t, :], ss[:, k, t:t + 1]).then_inc(sumsq[t], 1)
                dve.wait_ge(rstd_ready[t], k + 1)
                v.scalar_tensor_tensor(out=x[:, t, :], in0=x[:, t, :], scalar=rstd[:, k, t:t + 1], in1=gb[:, :],
                                       op0=ALU.mult, op1=ALU.mult).then_inc(x_updated, 1)
                dve.wait_ge(x_updated, 2 * t + 2)
                k = NIDX["f0"]
                square(x[:, t, :], xn[:, t, :], ss[:, k, t:t + 1]).then_inc(sumsq[t], 1)
                dve.wait_ge(rstd_ready[t], k + 1)
                v.tensor_scalar(xn[:, t, :], x[:, t, :], rstd[:, k, t:t + 1], None, ALU.mult).then_inc(rows_ready[t], 1)
            turn("f0", xh, xl, "f0")
            split(FIRST["ffn0"] + 1)

            def ffn(f):
                p0 = FIRST[f"ffn{f}"]
                last = p0 + 3 * FF_STEPS - 1

                def product(p, i, m=0, r=0):
                    dve.wait_ge(evacuated, along(EVAC, p, m, r))
                    dve.wait_ge(panel_used, p + m * r + 1)
                    wait(dve, ff_lo, FF_STEPS * f + i)
                    v.tensor_tensor(ff_a.rearrange("p f t -> p (f t)"), ff_s.rearrange("p f t -> p (f t)"), bank(BANK[p]), ALU.mult)\
                        .then_inc(evacuated, 1)

                def rest(i, up=ah[:, :, :], out=al[:, :, :]):
                    dve.wait_ge(ff_hi, FF_STEPS * f + i + 1)
                    v.tensor_tensor(out, ff_a, up.bitcast(F32), ALU.subtract).then_inc(ff_lo, 1)

                split(p0 + 2)
                split(p0 + 3)
                product(p0 + 1, 0)
                rest(0)

                with dve.Fori(1, FF_STEPS - 1) as i:
                    split(p0 + 4, 3, i - 1)
                    split(p0 + 5, 3, i - 1)
                    product(p0 + 3, i, 3, i - 1)
                    split(p0 + 6, 3, i - 1)
                    rest(i)
                i = FF_STEPS - 1
                split(p0 + 4, 3, i - 1)
                split(p0 + 5, 3, i - 1)
                product(p0 + 3, i, 3, i - 1)
                rest(i, fh, fl)
                for p in range(last + 1, min(last + 3, NP)):
                    split(p)

            def post(name):
                k, after = NIDX[name], dict(POSTS)[name]
                u = TT * (1 + [n for n, _ in POSTS].index(name))
                dve.wait_ge(spread_loaded, 16 * (SPREAD.index(name) + 1))
                dve.wait_ge(turned, XBASE[after] if after else XEND["f3"])
                for t in range(TT):
                    dve.wait_ge(sumsq[t], SUMS[name])
                    v.tensor_tensor(xn[:, t, :], ACC[:, 2 * t:2 * t + 2, :].rearrange("p b n -> p (b n)"), gb[:, :], ALU.mult).then_inc(gain_used, 1)
                    dve.wait_ge(gain_used, u + t + 1)
                    dve.wait_ge(rstd_ready[t], k + 1)
                    v.scalar_tensor_tensor(out=x[:, t, :], in0=xn[:, t, :], scalar=rstd[:, k, t:t + 1], in1=x[:, t, :],
                                           op0=ALU.mult, op1=ALU.add).then_inc(x_updated, 1)
                if after is None:
                    return
                k = NIDX[after]
                dve.wait_ge(x_updated, X_AT[name])
                square(x[:, 1, :], xn[:, 1, :], ss[:, k, 1:2]).then_inc(sumsq[1], 1)
                dve.wait_ge(rstd_ready[1], k + 1)
                v.tensor_scalar(xn[:, 1, :], x[:, 1, :], rstd[:, k, 1:2], None, ALU.mult).then_inc(rows_ready[1], 1)
                turn(after, xh, xl, after)

            ffn(0)
            post("p0")
            p0 = FIRST["conv_in"]
            dve.wait_ge(cv_pad, 1)

            def conv(j):
                c = 5 * j
                done = [0]

                def then(ins, n=1):
                    done[0] += n
                    ins.then_inc(cv_chain, n)
                    dve.wait_ge(cv_chain, c + done[0])

                for w in range(3):
                    split(p0 + w + 2, 3, j)
                dve.wait_ge(evacuated, along(EVAC, p0 + 2, 3, j))
                dve.wait_ge(panel_used, p0 + 3 * j + 3)
                v.tensor_tensor(cv_u[:, :, CONV_W - 1:], cv_c, bank(BANK[p0 + 2]).rearrange("p (f t) -> p f t", f=2), ALU.mult).then_inc(evacuated, 1)
                dve.wait_ge(evacuated, along(EVAC, p0 + 3, 3, j))
                wait(dve, cv_lo, j)
                tap = lambda w, f: cols[:, bass.ds(2 * j + (TAPS + w * KD + f), 1)]
                v.tensor_scalar(cv_z[:, 0, :], cv_u[:, 0, 2:2 + T], tap(2, 0), None, ALU.mult)
                then(v.tensor_scalar(cv_z[:, 1, :], cv_u[:, 1, 2:2 + T], tap(2, 1), None, ALU.mult))
                for w in (1, 0):
                    for f in range(2):
                        then(v.scalar_tensor_tensor(out=cv_z[:, f, :], in0=cv_u[:, f, w:w + T], scalar=tap(w, f), in1=cv_z[:, f, :],
                                                    op0=ALU.mult, op1=ALU.add))
                v.tensor_tensor(cv_z, cv_z, cv_b, ALU.mult).then_inc(cv_y, 1)
                dve.wait_ge(cv_hi, j + 1)
                v.tensor_tensor(yl[:, bass.ds(2 * j, 2), :], cv_z, yh[:, bass.ds(2 * j, 2), :].bitcast(F32), ALU.subtract).then_inc(cv_lo, 1)
                assert done[0] == 5

            peeled(dve, 4, conv)
            for j in range(4):
                split(FIRST["conv_out"] + j + 2)
            post("pc")
            ffn(1)
            post("p1")
            for j in range(8):
                split(FIRST["kv"] + j + 2)
            turn("f2", xh, xl, "f2")
            ffn(2)
            post("p2")
            for j in range(4):
                split(FIRST["q"] + j + 2)
            dve.wait_ge(lam_loaded, 64)
            for a in range(2):
                v.scalar_tensor_tensor(out=lam_in[:, 2 * a, :], in0=lam_in[:, 2 * a, :], scalar=1.0, in1=lam_in[:, 2 * a + 1, :], op0=ALU.mult,
                                       op1=ALU.mult, accum_out=lam_dot[:, a:a + 1]).then_inc(lam_dots, 1)
            dve.wait_ge(lam_exped, 1)
            link(v.tensor_tensor(lam, lam_exp[:, 1:2], lam_exp[:, 0:1], ALU.subtract))
            link(v.tensor_scalar(lam, lam, -LAMBDA_INIT, None, ALU.add))

            DIFF_SCORE_LINKS, DIFF_MIX_LINKS = 4, 3

            def diff_links(before):
                done = [before]

                def then(ins):
                    done[0] = done[0] + 1
                    ins.then_inc(df_chain, 1)
                    dve.wait_ge(df_chain, done[0])
                return then

            def diff_scores(h, b, before):
                then = diff_links(before)
                wait(dve, df_turned, h - 1)
                for c in range(2):
                    u = 2 * b + c
                    dve.wait_ge(df_scored, 2 * h + c + 1)
                    then(v.tensor_tensor(df_sc[u], bank(4 + u)[:, 0:BW], causal.rearrange("p n s -> p (n s)"), ALU.add))
                    v.tensor_reduce(df_mx[:, u, 0:1], df_sc[u][:, KEYS[0]], AX.X, ALU.max)
                    then(v.tensor_reduce(df_mx[:, u, 1:2], df_sc[u][:, KEYS[1]], AX.X, ALU.max))
                    v.tensor_scalar(df_mx[:, u, :], df_mx[:, u, :], -1.0, None, ALU.mult).then_inc(df_max, 1)

            def diff_mix(h, b, before):
                then = diff_links(before)
                p, q = 2 * b, 2 * b + 1
                dve.wait_ge(df_exp, 4 * h + 4)
                then(v.reciprocal(df_r[:, p:q + 1, :], df_sum[:, p:q + 1, :]))
                then(v.tensor_scalar(df_r[:, q, :], df_r[:, q, :], lam, None, ALU.mult))
                v.tensor_scalar(df_sc[p][:, KEYS[0]], df_sc[p][:, KEYS[0]], df_r[:, p, 0:1], None, ALU.mult)
                then(v.tensor_scalar(df_sc[p][:, KEYS[1]], df_sc[p][:, KEYS[1]], df_r[:, p, 1:2], None, ALU.mult))
                for t in range(TT):
                    v.scalar_tensor_tensor(out=df_sc[p][:, KEYS[t]], in0=df_sc[q][:, KEYS[t]], scalar=df_r[:, q, t:t + 1], in1=df_sc[p][:, KEYS[t]],
                                           op0=ALU.mult, op1=ALU.add).then_inc(df_mixed, 1)

            def diff_pair(i, more):
                c = 2 * DIFF_SCORE_LINKS + 2 * (DIFF_SCORE_LINKS + DIFF_MIX_LINKS) * i
                for b in range(2):
                    diff_mix(2 * i + b, b, c + b * DIFF_MIX_LINKS)
                c = c + 2 * DIFF_MIX_LINKS
                if more:
                    for b in range(2):
                        diff_scores(2 * i + 2 + b, b, c + b * DIFF_SCORE_LINKS)

            dve.wait_ge(tables, N_TABLES + 3)
            for b in range(2):
                diff_scores(b, b, b * DIFF_SCORE_LINKS)
            skewed(dve, DIFF_HEADS // 2, diff_pair)
            k = NIDX["diff"]
            heads = lambda w: w.rearrange("p t (h e) -> p (t h) e", e=P)
            dve.wait_ge(df_o_ready, DIFF_HEADS)
            for t in range(TT):
                own = slice(t * DIFF_HEADS, (t + 1) * DIFF_HEADS)
                o = heads(df_o)[:, own]
                dve.wait_ge(rstd_ready[t], k + 1)
                v.tensor_tensor(o, o, rstd[:, k, own].unsqueeze(2).to_broadcast([P, DIFF_HEADS, P]), ALU.mult).then_inc(rows_ready[t], 1)
            turn("diff", xh, xl, "diff")
            for j in range(4):
                split(FIRST["o"] + j + 2)
            post("pa")
            ffn(3)
            post("p3")

        @block.tensor
        def _(pe):
            def mm(out, l, r, first, last):
                return nc.tensor.matmul(out, l, r, start=first, stop=last)

            def begin(p, m=0, i=0):
                pe.wait_ge(lo_done, p + m * i + 1)
                if BANK[p] is not None:
                    wait(pe, evacuated, along(EVAC, p, m, i) - 1)

            def exact3(out, lh, ll, rh, rl, first, last):
                mm(out, lh, rh, first, False)
                mm(out, lh, rl, False, False)
                return mm(out, ll, rh, False, last)

            def views(p, kt):
                s = p % SLOTS
                return [w[s][:, :WORDS[p]].rearrange("p (k n) -> p k n", k=kt) for w in (hi, lo)]

            def feature_tile(p, f, out, kt=KD, rh=xh, rl=xl, stream=None):
                wh, wl = views(p, kt)
                c = slice(f * P, (f + 1) * P)
                for k in range(kt):
                    if stream:
                        pe.wait_ge(turned_lo, SBASE[stream] + k + 1)
                    last = exact3(out, wh[:, k, c], wl[:, k, c], rh[:, k, :], rl[:, k, :], k == 0, k == kt - 1)
                return last

            def token_tile(p, t, out, c=slice(0, PC), lh=xh, ll=xl, ks=range(KD)):
                wh, wl = views(p, KD)
                r = slice(t * P, (t + 1) * P)
                for k in ks:
                    last = exact3(out, lh[:, k, r], ll[:, k, r], wh[:, k, c], wl[:, k, c], k == 0, k == KD - 1)
                return last

            def panel_a(p, m=0, i=0, stream=None):
                begin(p, m, i)
                for f in range(2):
                    last = feature_tile(p, f, bank(BANK[p])[:, f * T:(f + 1) * T], stream=None if f else stream)
                last.then_inc(panel_used, 1)

            def panel_b(p, m=0, i=0, n=PC):
                begin(p, m, i)
                for t in range(TT):
                    last = token_tile(p, t, bank(BANK[p])[:, t * n:(t + 1) * n], slice(0, n))
                last.then_inc(panel_used, 1)

            def turn(name, rows):
                if SBASE[name]:
                    pe.wait_ge(turned_lo, SBASE[name])
                for t in range(TT):
                    pe.wait_ge(rows_ready[t], XIDX[name] + 1)
                    for b in range(XEND[name] - XBASE[name]):
                        for j in range(2):
                            c = (2 * b + j) * P
                            last = nc.tensor.transpose(ACC[:, b, j * T + t * P:j * T + (t + 1) * P], rows[:, t, c:c + P], ident[:, :])
                        if t == TT - 1:
                            last.then_inc(turned, 1)

            pe.wait_ge(tables, 2)
            turn("mix", xn)
            pe.wait_ge(cols_loaded, 16 * SMALL_LOADS)
            nc.tensor.transpose(bank(3)[:, 0:P], rowbuf[:, 0, :], ident[:, :])
            nc.tensor.transpose(bank(3)[:, P:KEYS_AT], rowbuf[0:KEYS_AT - P, 1, :], ident[0:KEYS_AT - P, 0:KEYS_AT - P])
            nc.tensor.transpose(bank(3)[:, KEYS_AT:KEYS_AT + PE_KEYS], rowbuf[:, 2, :], ident[:, :]).then_inc(cols_turned, 1)
            for p in range(4):
                panel_a(p, stream=None if p else "mix")
            for p in range(4, 6):
                panel_b(p)

            pe.wait_ge(tables, SB_TABLES)

            def sb_pair(i):
                pe.wait_ge(sb_staged, 3 * i + 2)
                for a in range(2):
                    r = slice(a * HD, (a + 1) * HD)
                    wait(pe, sb_sig, 4 * i + 2 * a - 2)
                    for n, (t, sk) in enumerate(BLOCKS):
                        out = bank(4 + a)[:, n * P:(n + 1) * P]
                        last = mm(out, q_st[r, t * P:(t + 1) * P], k_st[r, sk * P:(sk + 1) * P], True, t != sk)
                        if t == sk:
                            last = mm(out, ident[:, :], strict, False, True)
                    last.then_inc(sb_scored, 1)
                for a in range(2):
                    pe.wait_ge(sb_attn, 2 * i + a + 1)
                    wait(pe, sb_pt_ready, 2 * i + a - 1)
                    for n in range(len(BLOCKS)):
                        last = nc.tensor.transpose(bank(6 + a)[:, n * P:(n + 1) * P], sb_a[a][:, n * P:(n + 1) * P], ident[:, :])
                    last.then_inc(sb_turned, 1)
                pe.wait_ge(sb_staged, 3 * i + 3)
                wait(pe, o_lo, i)
                for a in range(2):
                    r = slice(a * HD, (a + 1) * HD)
                    pe.wait_ge(sb_pt_ready, 2 * i + a + 1)
                    mm(bank(3)[r, 0:P], v_st[:, 0, r], sb_pt[a][:, 0, :], True, True)
                    mm(bank(3)[r, P:T], v_st[:, 0, r], sb_pt[a][:, 1, :], True, False)
                    mm(bank(3)[r, P:T], v_st[:, 1, r], sb_pt[a][:, 2, :], False, True).then_inc(sb_out, 1)

            peeled(pe, PAIRS, sb_pair)

            q0, c0, g0 = FIRST["nsa_q"], FIRST["nsa_kv"], FIRST["nsa_gate"]
            for j in range(2):
                panel_a(q0 + j)
            panel_a(c0)
            for j in range(2):
                p = c0 + 1 + j
                begin(p)
                b = bank(BANK[p])
                feature_tile(p, 0, b[:, 0:T])
                for t in range(TT):
                    last = token_tile(p, t, b[:, T + t * P:T + (t + 1) * P], slice(P, 2 * P))
                last.then_inc(panel_used, 1)
            begin(g0)
            wh, wl = views(g0, KD)
            for k in range(KD):
                last = exact3(bank(BANK[g0])[0:N_GATES, 0:T], wh[:, k, :], wl[:, k, :], xh[:, k, :], xl[:, k, :], k == 0, k == KD - 1)
            last.then_inc(panel_used, 1)
            pe.wait_ge(n_blk, 16)
            pe.wait_ge(wcmp_loaded, 32)
            pe.wait_ge(o_lo, PAIRS)
            for g in range(2):
                if g:
                    pe.wait_ge(evacuated, EVAC[FIRST["hg"]])
                    for t in range(TT):
                        last = nc.tensor.transpose(bank(BANK[g0])[:, T + t * N_GATES:T + (t + 1) * N_GATES],
                                                   gate_rows[0:N_GATES, t * P:(t + 1) * P], ident[0:N_GATES, 0:N_GATES])
                    last.then_inc(gate_turned, 1)
                r = slice(g * HD, (g + 1) * HD)
                for w, weights in enumerate((wcmp_k, wcmp_v)):
                    for l in range(CMP_LEN // 2):
                        last = mm(bank(2 + w)[r, 0:N_CMP], weights[:, l, :], cmp_blk[g][:, w, l, :], l == 0, l == CMP_LEN // 2 - 1)
            last.then_inc(n_kc, 1)
            pe.wait_ge(vc_copied, 1)
            nc.tensor.transpose(bank(4)[0:N_CMP, 0:P], vc_rows, ident[:, :]).then_inc(n_kc, 1)
            pe.wait_ge(n_kc_ready, 3)
            pe.wait_ge(gate_ready, 1)

            def nsa_scores(h, i, a):
                pe.wait_ge(n_staged, i + 1)
                r = slice(a * HD, (a + 1) * HD)
                for br, key in enumerate((n_ksel, n_kwin)):
                    wait(pe, n_max, 2 * h - 3 + br)
                    for t in range(TT):
                        last = mm(bank(4 + 2 * a + br)[:, KEYS[t]], nq_st[r, t * P:(t + 1) * P], key[r, 0:(t + 1) * P], True, True)
                    last.then_inc(n_scored, 1)

            def nsa_cmp_scores(h, i, a):
                r = slice(a * HD, (a + 1) * HD)
                wait(pe, c_shift, h)
                wait(pe, n_pt_ready, 6 * i)
                for t in range(TT):
                    c = T + t * CPAD
                    last = mm(bank(3)[:, c:c + CPAD], nq_st[r, t * P:(t + 1) * P], kc[r, 0:CPAD], True, True)
                last.then_inc(c_scored, 1)

            def nsa_turn(h, i, a):
                wait(pe, n_pt_ready, 3 * h)
                for br in range(2):
                    pe.wait_ge(n_scaled[a], 4 * i + 2 * br + 2)
                    for n in range(len(BLOCKS)):
                        last = nc.tensor.transpose(bank(br)[:, n * P:(n + 1) * P], n_sc[2 * br + a][:, n * P:(n + 1) * P], ident[:, :])
                    last.then_inc(n_turned, 1)
                pe.wait_ge(c_scaled, i + 1)
                for t in range(TT):
                    last = nc.tensor.transpose(bank(3)[0:CPAD, t * P:(t + 1) * P], n_scc[:, a, t, :], ident[:, :])
                last.then_inc(n_turned, 1)

            def nsa_sum(h, i, a):
                pe.wait_ge(n_pt_ready, 3 * h + 3)
                if a == 0:
                    wait(pe, o_lo, PAIRS + i)
                r = slice(a * HD, (a + 1) * HD)
                for t in range(TT):
                    out = bank(2)[r, t * P:(t + 1) * P]
                    mm(out, vc[0:CPAD, a, :], n_ptc[0:CPAD, a, t, :], True, False)
                    for br, val in enumerate((n_vsel, n_vwin)):
                        pt = n_pt[2 * br + a]
                        for s in range(t + 1):
                            last = mm(out, val[:, s, r], pt[:, t + s, :], False, br == 1 and s == t)
                last.then_inc(n_out, 1)

            def nsa_pair(i, more):
                if more:
                    for a in range(2):
                        nsa_scores(2 * i + 2 + a, i + 1, a)
                for a in range(2):
                    nsa_turn(2 * i + a, i, a)
                if more:
                    nsa_cmp_scores(2 * i + 2, i + 1, 0)
                for a in range(2):
                    nsa_sum(2 * i + a, i, a)
                if more:
                    nsa_cmp_scores(2 * i + 3, i + 1, 1)

            for a in range(2):
                nsa_scores(a, 0, a)
                nsa_cmp_scores(a, 0, a)
            skewed(pe, PAIRS, nsa_pair)

            h0 = FIRST["hg"]
            for j in range(4):
                panel_a(h0 + j)
            for j in range(4, 8):
                panel_b(h0 + j)

            def hg_head(i):
                if isinstance(i, int):
                    pe.wait_ge(evacuated, EVAC[FIRST["merge"]])
                    pe.wait_ge(o_lo, 2 * PAIRS)
                for l in range(LEVELS):
                    pe.wait_ge(h_lev, 18 * i + 2 * l + 2)
                    for t in range(TT):
                        c = slice(t * P, (t + 1) * P)
                        mm(ACC[:, 2 * t + l // 4, (l % 4) * P:(l % 4 + 1) * P], k_lev[:, l, c], q_lev[:, l, c], True, True)
                pe.wait_ge(h_lev, 18 * i + 18)
                wait(pe, h_cross, i)
                mm(bank(3)[:, 0:P], k_x, q_x, True, True).then_inc(h_scored, 1)
                wait(pe, h_o_ready, i)
                for t in range(TT):
                    pe.wait_ge(h_masked, 2 * i + t + 1)
                    out = bank(2)[:, t * P:(t + 1) * P]
                    for l in range(LEVELS):
                        last = mm(out, a_m[t][:, l, :], hg_i[:, t, bass.ds(i * P, P)], l == 0, l == LEVELS - 1 and t == 0)
                pe.wait_ge(h_cross, i + 1)
                mm(out, a_x, hg_i[:, 0, bass.ds(i * P, P)], False, True).then_inc(h_out, 1)

            panel_a(FIRST["merge"])
            peeled(pe, HG_HEADS, hg_head)
            panel_a(FIRST["merge"] + 1)
            turn("hg", hg_o)

            pe.wait_ge(turned_lo, SEND["hg"])

            def merge(b):
                for half in range(2):
                    p = FIRST["merge"] + 3 * half
                    if half or not isinstance(b, int):
                        for j in range(2):
                            panel_a(p + j, 6, b)
                    begin(p + 2, 6, b)
                    wait(pe, m_mul, 2 * b + half - 1)
                    rh = oh[:, bass.ds(b, 1)].rearrange("p a k t -> p (a k) t")
                    rl = ol[:, bass.ds(b, 1)].rearrange("p a k t -> p (a k) t")
                    for f in range(4):
                        last = feature_tile(p + 2, f, ACC[:, 2 * half + f // 2, (f % 2) * T:(f % 2 + 1) * T], PAIRS, rh, rl)
                    last.then_inc(panel_used, 1)

            peeled(pe, 3, merge)

            pe.wait_ge(m_lo, 2)
            for j in range(4):
                panel_b(FIRST["w_out"] + j)

            turn("peer", xn)
            def peer_scores(out, t, heads):
                for h in heads:
                    for a in range(2):
                        r = slice(a * HD, (a + 1) * HD)
                        last = mm(out[:, 2 * a + h // 4, (h % 4) * P:(h % 4 + 1) * P], pe_q[r, h, t * P:(t + 1) * P], cols[r, KEYS_AT:KEYS_AT + PE_KEYS], True, True)
                last.then_inc(pe_scored, 1)

            def first_scores(j):
                pe.wait_ge(evacuated, EVAC[FIRST["peer_q"]] + j + 1)
                wait(pe, pe_sc_ready, 2 * j)
                peer_scores(ACC, 0, (2 * j, 2 * j + 1))

            for j in range(4):
                panel_a(FIRST["peer_q"] + j, stream=None if j else "peer")
                if j == 0:
                    first_scores(0)
                if j > 1:
                    first_scores(j - 1)
            first_scores(3)
            peer_scores(PS, 1, range(PE_HEADS))
            pe.wait_ge(pe_sc_ready, PE_HEADS)
            for t in range(TT):
                def expert_sums(n, first=False, final=False):
                    for k in range(PE_K):
                        slot = k % RING
                        pe.wait_ge(diag_ready, PE_K * n + k + 1)
                        pe.wait_ge(v_landed[slot], 16 * (PE_K // RING * n + k // RING + 1))
                        for half in range(2):
                            last = mm(ACC[:, 2 * t + half, :], diag[:, k % DIAGS, :], v_ring[slot][:, half * 512:(half + 1) * 512],
                                      first and k == 0, final and k == PE_K - 1)
                        last.then_inc(v_used, 1)

                n0 = t * PE_HEADS
                expert_sums(n0, first=True)
                with pe.Fori(n0 + 1, n0 + PE_HEADS - 1) as n:
                    expert_sums(n)
                expert_sums(n0 + PE_HEADS - 1, final=True)

            def ffn(f):
                p0 = FIRST[f"ffn{f}"]

                def down(p, i, m=0, r=0, first=False, final=False):
                    begin(p, m, r)
                    pe.wait_ge(ff_lo, FF_STEPS * f + i + 1)
                    wh, wl = views(p, 2)
                    uh, ul = (fh, fl) if final else (ah, al)
                    for t in range(TT):
                        for half in range(2):
                            for k in range(2):
                                c, w = slice(t * P, (t + 1) * P), slice(half * 512, (half + 1) * 512)
                                last = exact3(ACC[:, 2 * t + half, :], uh[:, k, c], ul[:, k, c], wh[:, k, w], wl[:, k, w],
                                              first and k == 0, final and k == 1)
                        if final and t == 0:
                            last.then_inc(branch_half, 1)
                    last.then_inc(panel_used, 1)

                panel_a(p0, stream=f"f{f}")
                panel_a(p0 + 1)
                panel_a(p0 + 2)
                panel_a(p0 + 3)
                down(p0 + 4, 0, first=True)
                with pe.Fori(2, FF_STEPS) as i:
                    panel_a(p0 + 2, 3, i - 1)
                    panel_a(p0 + 3, 3, i - 1)
                    down(p0 + 4, i - 1, 3, i - 1)
                down(p0 + 3 * FF_STEPS - 1, FF_STEPS - 1, final=True)

            def project(name, lh, ll, late=None):
                for j in range(4):
                    p = FIRST[name] + j
                    begin(p)
                    own = slice((j % 2) * PC, (j % 2 + 1) * PC)
                    early = 0
                    if j == 0 and late is not None:
                        early = KD - 2
                        for t in range(TT):
                            token_tile(p, t, ACC[:, 2 * t + j // 2, own], lh=lh, ll=ll, ks=range(early))
                        pe.wait_ge(*late)
                    for t in range(TT):
                        last = token_tile(p, t, ACC[:, 2 * t + j // 2, own], lh=lh, ll=ll, ks=range(early, KD))
                        if j == 3 and t == 0:
                            last.then_inc(branch_half, 1)
                    last.then_inc(panel_used, 1)

            def turn_after(post):
                k = [n for n, _ in POSTS].index(post)
                pe.wait_ge(gain_used, TT * (k + 2))
                turn(POSTS[k][1], xn)

            for t in range(TT):
                pe.wait_ge(rows_ready[t], XIDX["f0"] + 1)
            turn("f0", xn)
            ffn(0)
            turn_after("p0")

            def conv(j):
                for w in range(3):
                    panel_a(FIRST["conv_in"] + w, 3, j, stream="conv" if w == 0 and isinstance(j, int) else None)

            peeled(pe, 4, conv)
            pe.wait_ge(cv_lo, 3)
            project("conv_out", yh, yl, late=(cv_lo, 4))
            turn_after("pc")
            ffn(1)
            turn_after("p1")
            for j in range(4):
                panel_a(FIRST["kv"] + j, stream=None if j else "kv")
            for j in range(4, 8):
                panel_b(FIRST["kv"] + j)
            ffn(2)
            turn_after("p2")
            for j in range(4):
                panel_a(FIRST["q"] + j, stream=None if j else "attn")

            def diff_scores(h, b):
                pe.wait_ge(df_staged, 2 * h + 2)
                for c in range(2):
                    u, r = 2 * b + c, slice(c * HD, (c + 1) * HD)
                    wait(pe, df_max, 2 * h - 3 + c)
                    for t in range(TT):
                        last = mm(bank(4 + u)[:, KEYS[t]], df_qs[r, b, t * P:(t + 1) * P], df_ks[r, b, 0:(t + 1) * P], True, True)
                    last.then_inc(df_scored, 1)

            def diff_turn(h, b):
                pe.wait_ge(df_mixed, 2 * h + 2)
                wait(pe, df_pt_ready, h - 1)
                for n in range(len(BLOCKS)):
                    last = nc.tensor.transpose(bank(b)[:, n * P:(n + 1) * P], df_sc[2 * b][:, n * P:(n + 1) * P], ident[:, :])
                last.then_inc(df_turned, 1)

            def diff_values(h, b):
                pe.wait_ge(df_pt_ready, h + 1)
                wait(pe, df_o_ready, h - 1)
                out = bank(2 + b)
                val = lambda s: df_v[:, s, bass.ds(h * P, P)]
                mm(out[:, 0:P], df_pt[b][:, 0, :], val(0), True, True)
                mm(out[:, P:2 * P], df_pt[b][:, 1, :], val(0), True, False)
                mm(out[:, P:2 * P], df_pt[b][:, 2, :], val(1), False, True).then_inc(df_out, 1)

            def diff_pair(i, more):
                if more:
                    for b in range(2):
                        diff_scores(2 * i + 2 + b, b)
                for b in range(2):
                    diff_turn(2 * i + b, b)
                for b in range(2):
                    diff_values(2 * i + b, b)

            for b in range(2):
                diff_scores(b, b)
            skewed(pe, DIFF_HEADS // 2, diff_pair)
            turn("diff", df_o)
            pe.wait_ge(turned_lo, SEND["diff"])
            project("o", xh, xl)
            turn_after("pa")
            ffn(3)


def kernel(**inputs):
    import concourse.bacc as bacc
    from concourse.bass_utils import run_bass_kernel_spmd

    nc = bacc.Bacc("TRN2", target_bir_lowering=False, num_devices=1)
    arrays, io = {}, {}
    for name, a in inputs.items():
        a = np.ascontiguousarray(a)
        arrays[f"in_{name}"] = a
        io[name] = nc.dram_tensor(f"in_{name}", a.shape, mybir.dt.from_np(a.dtype), kind="ExternalInput").ap()
    io["out"] = nc.dram_tensor("out_0", (1, T, D), F32, kind="ExternalOutput").ap()
    build(nc, io)
    r = run_bass_kernel_spmd(nc, [arrays], core_ids=[0])
    return r.results[0]["out_0"]
```
